# Optimizing a Trainium2 kernel written in Bass

```python
import jax
import jax.numpy as jnp
from jax import lax
import numpy as np

D_MODEL = 1024
BATCH = 1
SEQ = 128
DEPTH = 2
DEC_BATCH = 1
DEC_SEQ = 1024
PAST_LEN = 128

GRID_W = 64
MIX_W = D_MODEL
MLSTM_W = D_MODEL // 4
MLSTM_HEADS = 4
MLSTM_DH = MLSTM_W // MLSTM_HEADS
N_GATES = 4 * MLSTM_HEADS
CHUNK = 64
CONV_CH = D_MODEL // 4
CONV_WIDTH = 31
CONV_PAD = CONV_WIDTH // 2
MLA_W = D_MODEL // 2
MLA_HEADS = 8
MLA_V = MLA_W // MLA_HEADS
MLA_NOPE = 64
MLA_ROPE = 32
MLA_QK = MLA_NOPE + MLA_ROPE
Q_RANK = 256
KV_RANK = 128
Q_BLOCK = 128
ROPE_BASE = 10000.0
D_FF = (8 * D_MODEL + 3 * 256 - 1) // (3 * 256) * 256
EPS = 1e-6
IN_SIZES = (MLSTM_W, MLSTM_W, MLSTM_W, MLSTM_W, N_GATES, 2 * CONV_CH, Q_RANK, KV_RANK, MLA_ROPE)
IN_COLS = 4 * MLSTM_W + N_GATES + 2 * CONV_CH + Q_RANK + KV_RANK + MLA_ROPE

kernel_name = 'hybrid_mlstm_conv_mla_dit_step'

def rmsnorm(x, g):
    x32 = x.astype(jnp.float32)
    y = x32 * lax.rsqrt(jnp.mean(x32 * x32, axis=-1, keepdims=True) + EPS)
    return (y * g.astype(jnp.float32)).astype(x.dtype)

def layernorm(x, g, b):
    x32 = x.astype(jnp.float32)
    mu = jnp.mean(x32, axis=-1, keepdims=True)
    xc = x32 - mu
    y = xc * lax.rsqrt(jnp.mean(xc * xc, axis=-1, keepdims=True) + EPS)
    return (y * g.astype(jnp.float32) + b.astype(jnp.float32)).astype(x.dtype)

def split_in(z):
    out, start = [], 0
    for size in IN_SIZES:
        out.append(z[..., start:start + size])
        start += size
    return out

def mlstm_scan(q, k, v, log_i, log_f, C0, n0, m0):
    B, T, H, DH = q.shape
    NC = T // CHUNK
    f32 = jnp.float32

    def chunks(a):
        a = a.astype(f32).reshape((B, NC, CHUNK) + a.shape[2:])
        return jnp.moveaxis(jnp.moveaxis(a, 1, 0), 3, 2)

    tril = jnp.tril(jnp.ones((CHUNK, CHUNK), dtype=bool))

    def step(carry, inp):
        C, n, m = carry
        qc, kc, vc, ic, fc = inp
        b = jnp.cumsum(fc, axis=-1)
        d = jnp.where(tril, b[..., :, None] - b[..., None, :] + ic[..., None, :], -jnp.inf)
        inter = b + m[..., None]
        m_row = jnp.maximum(inter, jnp.max(d, axis=-1))
        w_inter = jnp.exp(inter - m_row)
        s = jnp.einsum('bhld,bhsd->bhls', qc, kc) * jnp.exp(d - m_row[..., None])
        num = w_inter[..., None] * jnp.einsum('bhld,bhde->bhle', qc, C) + jnp.einsum('bhls,bhse->bhle', s, vc)
        den = w_inter * jnp.einsum('bhld,bhd->bhl', qc, n) + jnp.sum(s, axis=-1)
        h = num / jnp.maximum(jnp.abs(den), jnp.exp(-m_row))[..., None]
        b_end = b[..., -1]
        g = b_end[..., None] - b + ic
        m_new = jnp.maximum(b_end + m, jnp.max(g, axis=-1))
        decay = jnp.exp(b_end + m - m_new)
        kw = kc * jnp.exp(g - m_new[..., None])[..., None]
        C_new = decay[..., None, None] * C + jnp.einsum('bhld,bhle->bhde', kw, vc)
        n_new = decay[..., None] * n + jnp.sum(kw, axis=2)
        return (C_new, n_new, m_new), h

    init = (C0.astype(f32), n0.astype(f32), m0.astype(f32))
    final, h = lax.scan(step, init, (chunks(q), chunks(k), chunks(v), chunks(log_i), chunks(log_f)))
    h = jnp.moveaxis(jnp.moveaxis(h, 2, 3), 0, 1).reshape(B, T, H, DH)
    return h, final

def mlstm_mixer(q_raw, k_raw, v_raw, o_raw, gate_raw, b_gate, norm_g, init_fwd, init_bwd):
    B, T, _ = q_raw.shape
    shp = (B, T, MLSTM_HEADS, MLSTM_DH)
    q = q_raw.reshape(shp) * (MLSTM_DH ** -0.5)
    k = k_raw.reshape(shp)
    v = v_raw.reshape(shp)
    g = (gate_raw + b_gate).astype(jnp.float32).reshape(B, T, 4, MLSTM_HEADS)
    li_f, lf_f = g[:, :, 0], jax.nn.log_sigmoid(g[:, :, 1])
    li_b, lf_b = g[:, :, 2], jax.nn.log_sigmoid(g[:, :, 3])
    h_f, st_f = mlstm_scan(q, k, v, li_f, lf_f, *init_fwd)
    rev = lambda a: jnp.flip(a, axis=1)
    h_b, st_b = mlstm_scan(rev(q), rev(k), rev(v), rev(li_b), rev(lf_b), *init_bwd)
    h = (h_f + rev(h_b)).astype(q_raw.dtype)
    h = rmsnorm(h, norm_g.reshape(MLSTM_HEADS, MLSTM_DH)).reshape(B, T, MLSTM_W)
    return h * jax.nn.sigmoid(o_raw), st_f, st_b

def conv_module(a, dw_w, dw_b, ln_g, ln_b, pw_w):
    u = a[..., :CONV_CH] * jax.nn.sigmoid(a[..., CONV_CH:])
    y = lax.conv_general_dilated(u, dw_w[:, None, :], window_strides=(1,), padding=[(CONV_PAD, CONV_PAD)],
                                 dimension_numbers=('NWC', 'WIO', 'NWC'), feature_group_count=CONV_CH) + dw_b
    return jax.nn.silu(layernorm(y, ln_g, ln_b)) @ pw_w

def axial_rope(a):
    T = a.shape[1]
    ROWS = T // GRID_W
    rows = jnp.repeat(jnp.arange(ROWS), GRID_W)
    cols = jnp.tile(jnp.arange(GRID_W), ROWS)
    half = MLA_ROPE // 2
    quarter = half // 2
    freqs = ROPE_BASE ** (-jnp.arange(quarter, dtype=jnp.float32) / quarter)

    def rot(x, pos):
        ang = pos.astype(jnp.float32)[:, None] * freqs[None, :]
        cos = jnp.cos(ang)[None, :, None, :].astype(x.dtype)
        sin = jnp.sin(ang)[None, :, None, :].astype(x.dtype)
        x1, x2 = x[..., :quarter], x[..., quarter:]
        return jnp.concatenate([x1 * cos - x2 * sin, x1 * sin + x2 * cos], axis=-1)

    return jnp.concatenate([rot(a[..., :half], rows), rot(a[..., half:], cols)], axis=-1)

def with_rope(a):
    return jnp.concatenate([a[..., :MLA_NOPE], axial_rope(a[..., MLA_NOPE:])], axis=-1)

def mla_queries(cq_raw, cq_g, w_uq, qn_g):
    B, T, _ = cq_raw.shape
    q = (rmsnorm(cq_raw, cq_g) @ w_uq).reshape(B, T, MLA_HEADS, MLA_QK)
    return rmsnorm(q, qn_g)

def mla_keys_values(ckv, krope, w_ukv, kn_g):
    B, T, _ = ckv.shape
    kv = (ckv @ w_ukv).reshape(B, T, MLA_HEADS, MLA_NOPE + MLA_V)
    k_nope, v = kv[..., :MLA_NOPE], kv[..., MLA_NOPE:]
    k_r = jnp.broadcast_to(krope[:, :, None, :], (B, T, MLA_HEADS, MLA_ROPE))
    k = rmsnorm(jnp.concatenate([k_nope, k_r], axis=-1), kn_g)
    return k, v

def attend(q, k, v):
    s = jnp.einsum('bqhd,bkhd->bhqk', q, k).astype(jnp.float32) * (MLA_QK ** -0.5)
    p = jax.nn.softmax(s, axis=-1).astype(v.dtype)
    return jnp.einsum('bhqk,bkhd->bqhd', p, v)

def blocked_attend(q, k, v):
    B, T, H, DQ = q.shape
    qb = jnp.moveaxis(q.reshape(B, T // Q_BLOCK, Q_BLOCK, H, DQ), 1, 0)
    out = lax.map(lambda qq: attend(qq, k, v), qb)
    return jnp.moveaxis(out, 0, 1).reshape(B, T, H, MLA_V)

def trunk_layer(x, cond, p, ctx):
    sh1, sc1, g1, sh2, sc2, g2 = jnp.split(jax.nn.silu(cond) @ p['w_ada'] + p['b_ada'], 6, axis=-1)
    h = rmsnorm(x, p['norm1_g']) * (1 + sc1) + sh1
    q_m, k_m, v_m, o_m, gate_m, conv_in, cq_raw, ckv_raw, krope = split_in(h @ p['w_in'])
    B, T, _ = x.shape
    if ctx is None:
        zero_state = (jnp.zeros((B, MLSTM_HEADS, MLSTM_DH, MLSTM_DH), jnp.float32),
                      jnp.zeros((B, MLSTM_HEADS, MLSTM_DH), jnp.float32),
                      jnp.zeros((B, MLSTM_HEADS), jnp.float32))
        init_f = zero_state
        init_b = zero_state
    else:
        init_f, init_b = ctx[2], ctx[3]
    y_m, st_f, st_b = mlstm_mixer(q_m, k_m, v_m, o_m, gate_m, p['b_gates'], p['mlstm_norm_g'], init_f, init_b)
    y_c = conv_module(conv_in, p['conv_dw_w'], p['conv_dw_b'], p['conv_ln_g'], p['conv_ln_b'], p['conv_pw_w'])
    q = mla_queries(cq_raw, p['mla_cq_g'], p['mla_w_uq'], p['mla_qn_g'])
    ckv = rmsnorm(ckv_raw, p['mla_ckv_g'])
    k, v = mla_keys_values(ckv, krope, p['mla_w_ukv'], p['mla_kn_g'])
    if ctx is None:
        y_a = attend(q, k, v)
    else:
        k_ctx, v_ctx = mla_keys_values(ctx[0], ctx[1], p['mla_w_ukv'], p['mla_kn_g'])
        y_a = blocked_attend(with_rope(q), jnp.concatenate([with_rope(k), k_ctx], axis=1),
                             jnp.concatenate([v, v_ctx], axis=1))
    mix = jnp.concatenate([y_m, y_c, y_a.reshape(B, T, MLA_W)], axis=-1) @ p['w_out']
    x = x + g1 * mix
    h2 = rmsnorm(x, p['norm2_g']) * (1 + sc2) + sh2
    gu = h2 @ p['ffn_w_gu']
    x = x + g2 * ((jax.nn.silu(gu[..., :D_FF]) * gu[..., D_FF:]) @ p['ffn_w_down'])
    return x, (ckv, krope, st_f, st_b)

def setup_inputs(seed: int = 0) -> dict:
    key = jax.random.key(seed)
    ks = jax.random.split(key, 32)
    f32 = jnp.float32
    nrm = lambda k, shape, scale: jax.random.normal(k, shape, f32) * scale
    gain = lambda k, shape: 1.0 + 0.02 * jax.random.normal(k, shape, f32)
    forget_base = jnp.linspace(3.0, 6.0, MLSTM_HEADS)
    zeros_h = jnp.zeros((MLSTM_HEADS,), f32)
    gate_base = jnp.stack([zeros_h, forget_base, zeros_h, forget_base]).reshape(N_GATES)
    return {
        'x_prompt': nrm(ks[0], (BATCH, SEQ, D_MODEL), 1.0),
        'x_sample': nrm(ks[1], (DEC_BATCH, DEC_SEQ, D_MODEL), 1.0),
        'cache_ckv': nrm(ks[2], (DEC_BATCH, DEPTH, PAST_LEN, KV_RANK), 1.0),
        'cache_krope': nrm(ks[3], (DEC_BATCH, DEPTH, PAST_LEN, MLA_ROPE), 1.0),
        'state_C': nrm(ks[4], (DEC_BATCH, DEPTH, 2, MLSTM_HEADS, MLSTM_DH, MLSTM_DH), 0.5),
        'state_n': nrm(ks[5], (DEC_BATCH, DEPTH, 2, MLSTM_HEADS, MLSTM_DH), 0.5),
        'state_m': nrm(ks[6], (DEC_BATCH, DEPTH, 2, MLSTM_HEADS), 1.0),
        'c': nrm(ks[7], (DEC_BATCH, D_MODEL), 1.0),
        'c_ctx': nrm(ks[8], (D_MODEL,), 1.0),
        'w_ada': nrm(ks[9], (DEPTH, D_MODEL, 6 * D_MODEL), D_MODEL ** -0.5),
        'b_ada': nrm(ks[10], (DEPTH, 6 * D_MODEL), 0.01),
        'norm1_g': gain(ks[11], (DEPTH, D_MODEL)),
        'w_in': nrm(ks[12], (DEPTH, D_MODEL, IN_COLS), D_MODEL ** -0.5),
        'b_gates': gate_base[None, :] + nrm(ks[13], (DEPTH, N_GATES), 0.1),
        'mlstm_norm_g': gain(ks[14], (DEPTH, MLSTM_W)),
        'conv_dw_w': nrm(ks[15], (DEPTH, CONV_WIDTH, CONV_CH), CONV_WIDTH ** -0.5),
        'conv_dw_b': nrm(ks[16], (DEPTH, CONV_CH), 0.01),
        'conv_ln_g': gain(ks[17], (DEPTH, CONV_CH)),
        'conv_ln_b': nrm(ks[18], (DEPTH, CONV_CH), 0.01),
        'conv_pw_w': nrm(ks[19], (DEPTH, CONV_CH, CONV_CH), CONV_CH ** -0.5),
        'mla_cq_g': gain(ks[20], (DEPTH, Q_RANK)),
        'mla_w_uq': nrm(ks[21], (DEPTH, Q_RANK, MLA_HEADS * MLA_QK), Q_RANK ** -0.5),
        'mla_ckv_g': gain(ks[22], (DEPTH, KV_RANK)),
        'mla_w_ukv': nrm(ks[23], (DEPTH, KV_RANK, MLA_HEADS * (MLA_NOPE + MLA_V)), KV_RANK ** -0.5),
        'mla_qn_g': gain(ks[24], (DEPTH, MLA_QK)),
        'mla_kn_g': gain(ks[25], (DEPTH, MLA_QK)),
        'w_out': nrm(ks[26], (DEPTH, MIX_W, D_MODEL), MIX_W ** -0.5),
        'norm2_g': gain(ks[27], (DEPTH, D_MODEL)),
        'ffn_w_gu': nrm(ks[28], (DEPTH, D_MODEL, 2 * D_FF), D_MODEL ** -0.5),
        'ffn_w_down': nrm(ks[29], (DEPTH, D_FF, D_MODEL), D_FF ** -0.5),
    }

def reference(x_prompt, x_sample, cache_ckv, cache_krope, state_C, state_n, state_m, c, c_ctx,
              w_ada, b_ada, norm1_g, w_in, b_gates, mlstm_norm_g, conv_dw_w, conv_dw_b, conv_ln_g,
              conv_ln_b, conv_pw_w, mla_cq_g, mla_w_uq, mla_ckv_g, mla_w_ukv, mla_qn_g, mla_kn_g,
              w_out, norm2_g, ffn_w_gu, ffn_w_down):
    def params(l):
        return {'w_ada': w_ada[l], 'b_ada': b_ada[l], 'norm1_g': norm1_g[l], 'w_in': w_in[l],
                'b_gates': b_gates[l], 'mlstm_norm_g': mlstm_norm_g[l], 'conv_dw_w': conv_dw_w[l],
                'conv_dw_b': conv_dw_b[l], 'conv_ln_g': conv_ln_g[l], 'conv_ln_b': conv_ln_b[l],
                'conv_pw_w': conv_pw_w[l], 'mla_cq_g': mla_cq_g[l], 'mla_w_uq': mla_w_uq[l],
                'mla_ckv_g': mla_ckv_g[l], 'mla_w_ukv': mla_w_ukv[l], 'mla_qn_g': mla_qn_g[l],
                'mla_kn_g': mla_kn_g[l], 'w_out': w_out[l], 'norm2_g': norm2_g[l],
                'ffn_w_gu': ffn_w_gu[l], 'ffn_w_down': ffn_w_down[l]}

    y_prompt = x_prompt
    cond_ctx = c_ctx[None, None, :]
    ckv_l, kr_l, C_l, n_l, m_l = [], [], [], [], []
    for l in range(DEPTH):
        y_prompt, (ckv, kr, st_f, st_b) = trunk_layer(y_prompt, cond_ctx, params(l), None)
        ckv_l.append(ckv)
        kr_l.append(kr)
        C_l.append(jnp.stack([st_f[0], st_b[0]], axis=1))
        n_l.append(jnp.stack([st_f[1], st_b[1]], axis=1))
        m_l.append(jnp.stack([st_f[2], st_b[2]], axis=1))
    new_cache_ckv = jnp.stack(ckv_l, axis=1)
    new_cache_krope = jnp.stack(kr_l, axis=1)
    new_state_C = jnp.stack(C_l, axis=1)
    new_state_n = jnp.stack(n_l, axis=1)
    new_state_m = jnp.stack(m_l, axis=1)

    y_sample = x_sample
    cond_lat = c[:, None, :]
    for l in range(DEPTH):
        ctx = (cache_ckv[:, l], cache_krope[:, l],
               (state_C[:, l, 0], state_n[:, l, 0], state_m[:, l, 0]),
               (state_C[:, l, 1], state_n[:, l, 1], state_m[:, l, 1]))
        y_sample, _ = trunk_layer(y_sample, cond_lat, params(l), ctx)

    return (y_prompt, y_sample, new_cache_ckv, new_cache_krope, new_state_C, new_state_n, new_state_m)


_drawn_inputs = setup_inputs


def setup_inputs(seed=0):
    import zlib

    import numpy as np

    out = dict(_drawn_inputs(seed))
    spreads = {}
    factors = {'cache_ckv': 5.244,
     'cache_krope': 8.0,
     'state_C': 5.902,
     'state_n': 8.0,
     'state_m': 8.0,
     'mlstm_norm_g': 8.0,
     'conv_dw_b': 8.0,
     'conv_ln_g': 8.0,
     'conv_ln_b': 22.93,
     'mla_cq_g': 8.0,
     'mla_ckv_g': 3.058,
     'mla_qn_g': 8.0,
     'mla_kn_g': 8.0,
     'norm2_g': 2.896}
    for name, (base, spread) in spreads.items():
        noise = np.random.default_rng([zlib.crc32(name.encode()), seed]).standard_normal(out[name].shape)
        drawn = base * np.exp(spread * noise) if base else spread * noise
        out[name] = jnp.asarray(drawn.astype(out[name].dtype))
    for name, factor in factors.items():
        out[name] = (out[name] * factor).astype(out[name].dtype)
    return out
```

```python
from contextlib import ExitStack

import concourse.bass as bass
import numpy as np
from concourse import mybir

F32 = mybir.dt.float32
F32R = mybir.dt.float32r
ACT = mybir.ActivationFunctionType
ALU = mybir.AluOpType
AX = mybir.AxisListType

P = 128
D_MODEL = 1024
SEQ = 128
DEC_SEQ = 1024
PAST = 128
DEPTH = 2
GRID_W = 64
HEADS_M = 4
DH = 64
CONV_CH = 256
CONV_WIDTH = 31
CONV_PAD = CONV_WIDTH // 2
HEADS_A = 8
NOPE = 64
ROPE = 32
QK = NOPE + ROPE
V_DIM = 64
Q_RANK = 256
KV_RANK = 128
ROPE_BASE = 10000.0
D_FF = 2816
EPS = 1e-6
NEG = -1e30

TOK = SEQ + DEC_SEQ
TILES = TOK // P
KC = D_MODEL // P
BLK = 384
NB = TOK // BLK
FC = D_FF // P
KEYS = TOK + PAST
KTILES = KEYS // P
SEG = P + 2 * CONV_PAD
U_LEN = SEG + DEC_SEQ + 2 * CONV_PAD
Y_LEN = U_LEN - 2 * CONV_PAD
SCALE_A = float(QK) ** -0.5
SCALE_M = float(DH) ** -0.5

V_BADA, V_N1, V_N2, V_MNG, V_DWB, V_LNG, V_LNB, V_CQG, V_CKVG, V_DW = 0, 48, 56, 64, 66, 68, 70, 72, 74, 75
V_M0 = V_DW + 2 * CONV_WIDTH
V_BG = V_M0 + 1
V_QN = V_BG + 1
V_KN = V_QN + QK
NVEC = V_KN + QK
C_ID, C_ONE, C_ROPE = 0, P, 2 * P
NCONST = C_ROPE + 8 * 32
M_MASK, M_SEL, M_PAIR, M_RESET = 0, 2 * P, 2 * P + 8 * P, 2 * P + 12 * P
NMC = M_RESET + TOK
Z_Q, Z_K, Z_V, Z_O, Z_CQ, Z_CKV, Z_MISC = 0, 2, 4, 6, 8, 10, 11
NZ = 12
STRIDE = 4096


class Chain:

    def __init__(self, eng, sem, layer):
        self.eng, self.sem, self.base, self.n = eng, sem, layer * STRIDE, 0

    def inc(self, ins):
        self.n += 1
        ins.then_inc(self.sem, 1)

    def settle(self, back=0):
        self.eng.wait_ge(self.sem, self.base + (self.n - back))

    def link(self, ins):
        self.inc(ins)
        self.settle()

    def enter(self, i, size):
        self.outer, self.size = (self.base, self.n), size
        self.base, self.n = self.base + self.n + i * size, 0

    def leave(self, count):
        self.settle()
        if self.size > self.n:
            self.eng.sem_inc(self.sem, self.size - self.n)
        self.base, self.n = self.outer[0], self.outer[1] + count * self.size

    def end_layer(self):
        self.settle()
        assert self.n <= STRIDE, self.n
        if STRIDE > self.n:
            self.eng.sem_inc(self.sem, STRIDE - self.n)


class Signal:

    def __init__(self, sem, per_layer, first=0):
        self.sem, self.per, self.first = sem, per_layer, first

    def at(self, layer, k):
        return layer * self.per + (k + self.first)


def build(nc, xin, cvec, vec, const, mconst, wada, win, wout, wgu, wdn, pww, whd, ctx_ckv, ctx_kr,
          c0, yout, o_ckv, o_kr, o_c, o_m, spill):
    ctx = ExitStack()
    with ctx:
        def sb(name, shape, dt=F32, where=ctx):
            return where.enter_context(nc.sbuf_tensor(name, shape, dt))

        cst = sb("cst", [P, NCONST])
        ident, ones = cst[:, C_ID:C_ID + P], cst[:, C_ONE:C_ONE + P]
        vecs = sb("vecs", [P, NVEC])
        cond = sb("cond", [P, KC, 2])
        mod = sb("mod", [P, 48, 2])
        gain = sb("gain", [P, 2, KC, 2])
        small = sb("small", [P, 64])
        diag = sb("diag", [P, TILES, P])

        hx = ExitStack()
        sb("hnum_at", [P, 4, TOK], F32, hx)
        hnum = sb("hnum", [P, TILES, 8, DH], F32, hx)
        hx.close()
        a_hi = sb("a_hi", [P, KC, TOK], F32R)
        a_lo = sb("a_lo", [P, KC, TOK], F32R)
        z = sb("z", [P, 8, TOK])
        x = z
        rest = ExitStack()
        z2 = sb("z2", [P, 4, TOK], F32, rest)

        def zc(c):
            return z[:, c, :] if c < 8 else z2[:, c - 8, :]

        s0 = ExitStack()
        wada_sb = sb("wada_sb", [P, 2, 4, KC, P], F32, s0)
        s0.close()
        s1 = ExitStack()
        nsq = sb("nsq", [P, 2, TOK], F32, s1)
        nt = sb("nt", [P, 2, TOK], F32, s1)
        s1.close()
        s2 = ExitStack()
        w_raw = sb("w_raw", [P, 2, KC * P], F32, s2)
        w_hi = sb("w_hi", [P, 2, KC * P], F32R, s2)
        w_lo = sb("w_lo", [P, 2, KC * P], F32R, s2)
        u = sb("u", [P, 2, U_LEN], F32, s2)
        sigb = sb("sigb", [P, TOK], F32, s2)
        yc = sb("yc", [P, 2, U_LEN], F32, s2)
        csq = sb("csq", [P, 2, TOK], F32, s2)
        s2.close()
        s2b = ExitStack()
        pw = sb("pw", [P, 2, 2, P], F32, s2b)
        s2b.close()
        s4 = ExitStack()
        mc = sb("mc", [P, M_RESET], F32, s4)
        reset = sb("reset", [DH, TOK], F32, s4)
        ra = sb("ra", [P, TOK], F32, s4)
        rb = sb("rb", [P, TOK], F32, s4)
        rr = sb("rr", [DH, TOK], F32, s4)
        lf = sb("lf", [DH, TOK], F32, s4)
        kt = sb("kt", [P, TILES, 2 * P], F32, s4)
        vaug = sb("vaug", [P, TILES, HEADS_M, DH + 1], F32, s4)
        em = sb("em", [P, 2, HEADS_M, P], F32, s4)
        sp_ = sb("sp_", [P, 2, HEADS_M, P], F32, s4)
        kw = sb("kw", [P, 2, HEADS_M, DH], F32, s4)
        ni = sb("ni", [P, 2, HEADS_M, DH + 1], F32, s4)
        cols = sb("cols", [P, 4, TILES, 8], F32, s4)
        den = sb("den", [P, 3, TILES, 8], F32, s4)
        mrow = sb("mrow", [DH, 4, TILES], F32, s4)
        dcol = sb("dcol", [P, 4, TILES], F32, s4)
        cst_st = sb("cst_st", [P, 2, 2, 2, DH + 1], F32, s4)
        s4.close()
        s4b = ExitStack()
        sb("s4b_at", [P, M_RESET], F32, s4b)
        hsq = sb("hsq", [P, TILES * HEADS_M, DH], F32, s4b)
        yt = sb("yt", [P, TOK], F32, s4b)
        s4b.close()
        s5 = ExitStack()
        krt = sb("krt", [P, KTILES, ROPE], F32, s5)
        ctxk = sb("ctxk", [P, PAST], F32, s5)
        hw = sb("hw", [P, 2, 320], F32, s5)
        qt_ = sb("qt_", [P, TILES, QK], F32, s5)
        kt_ = sb("kt_", [P, KTILES, QK], F32, s5)
        sq_ = sb("sq_", [P, TILES + KTILES, QK], F32, s5)
        rp = sb("rp", [P, 4, 8, 16], F32, s5)
        qh = sb("qh", [P, TOK], F32R, s5)
        ql = sb("ql", [P, TOK], F32R, s5)
        kh = sb("kh", [P, KEYS], F32R, s5)
        kl = sb("kl", [P, KEYS], F32R, s5)
        va = sb("va", [P, KTILES, P], F32, s5)
        nmx = sb("nmx", [P, TILES], F32, s5)
        pt = sb("pt", [P, 3, 512], F32, s5)
        rec = sb("rec", [P, 512], F32, s5)
        ya = sb("ya", [P, 512], F32, s5)
        s5.close()
        rest.close()
        s8 = ExitStack()
        g_hi = sb("g_hi", [P, 2, TOK], F32R, s8)
        g_lo = sb("g_lo", [P, 2, TOK], F32R, s8)
        f_raw = sb("f_raw", [P, 2, KC * P], F32, s8)
        gu_hi = sb("gu_hi", [P, 2, 2, KC, P], F32R, s8)
        gu_lo = sb("gu_lo", [P, 2, 2, KC, P], F32R, s8)
        d_hi = sb("d_hi", [P, 2, D_MODEL], F32R, s8)
        d_lo = sb("d_lo", [P, 2, D_MODEL], F32R, s8)
        sg = sb("sg", [P, 2, BLK], F32, s8)
        at = sb("at", [P, 2, BLK], F32, s8)
        s8.close()

        ps = ctx.enter_context(nc.psum_tensor("ps", [P, 8, 512], F32))
        flat = ps[:, :, :].rearrange("p b n -> p (b n)")

        def banks(b, n=NB):
            return ps[:, b:b + n, 0:BLK]

        def blocks(ap):
            return ap.rearrange("p (b n) -> p b n", n=BLK)

        def spread(ap, n):
            return ap.unsqueeze(len(ap.shape)).to_broadcast([*ap.shape, n])

        def sig(name, per, first=0):
            return Signal(ctx.enter_context(nc.semaphore(name)), per, first)

        NG = FC // 2
        const_in = sig("const_in", 0)
        cond_ok = sig("cond_ok", 0)
        x_in = sig("x_in", 16)
        vec_in = sig("vec_in", 16)
        ada_in = [sig(f"ada_in{i}", 6 * 16) for i in range(2)]
        ada_used = sig("ada_used", 12)
        mod_ok = sig("mod_ok", 1)
        sq_ok = sig("sq_ok", 2 * KC)
        sq_used = sig("sq_used", 2 * KC)
        rs_var = sig("rs_var", 5)
        rs_root = sig("rs_root", 5)
        rs_diag = sig("rs_diag", 2)
        rs_row = sig("rs_row", 2)
        nh_ok = sig("nh_ok", 2 * KC)
        ahi_ok = sig("ahi_ok", 2 * KC)
        alo_ok = sig("alo_ok", 2 * KC)
        spilled = sig("spilled", 32)
        w_in_ = [sig(f"w_in{i}", 12 * 16) for i in range(2)]
        w_hi_ok = sig("w_hi_ok", 24)
        w_lo_ok = sig("w_lo_ok", 24)
        w_used = sig("w_used", 24)
        z_free_a = sig("z_free_a", 14)
        z_free_d = sig("z_free_d", 10)
        sigb_ok = sig("sigb_ok", 2)
        u_zero = sig("u_zero", 1)
        c_sq = sig("c_sq", 3)
        c_sum = sig("c_sum", 2)
        c_diag = sig("c_diag", 2)
        c_row = sig("c_row", 2)
        cq_ok = sig("cq_ok", 1)
        ckv_out = sig("ckv_out", 48)
        pw_in = sig("pw_in", 16)
        cv_y = sig("cv_y", 1)
        cv_sum = sig("cv_sum", 2)
        cv_xc = sig("cv_xc", 1)
        cv_sq = sig("cv_sq", 1)
        cv_diag = sig("cv_diag", 1)
        cv_row = sig("cv_row", 1)
        cv_n = sig("cv_n", 1)
        cv_act = sig("cv_act", 1)
        cv_pw = sig("cv_pw", 1)
        cv_hi = sig("cv_hi", 2)
        cv_done = sig("cv_done", 1)
        ml_in = sig("ml_in", 48)
        ml_gate = sig("ml_gate", 1)
        ml_ln = sig("ml_ln", 1)
        ml_rows = sig("ml_rows", 1)
        ml_dexp = sig("ml_dexp", 1)
        ml_tr = sig("ml_tr", 3)
        ml_cols = sig("ml_cols", 1)
        ml_dcol = sig("ml_dcol", 1)
        ml_kvt = sig("ml_kvt", TILES)
        ml_kv_a = sig("ml_kv_a", TILES)
        ml_kv_v = sig("ml_kv_v", TILES)
        ml_zero = sig("ml_zero", 1)
        ml_bc = sig("ml_bc", 2 * TILES)
        ml_qk = sig("ml_qk", TILES)
        ml_em = sig("ml_em", 2 * TILES)
        ml_exp = sig("ml_exp", 2 * TILES)
        ml_s = sig("ml_s", 2 * TILES)
        ml_kw = sig("ml_kw", 2 * TILES)
        ml_pv = sig("ml_pv", 2 * TILES)
        ml_out = sig("ml_out", 2 * TILES)
        ml_hsum = sig("ml_hsum", 1)
        ml_hsq = sig("ml_hsq", 1)
        ml_var = sig("ml_var", 1)
        ml_root = sig("ml_root", 1)
        ml_h = sig("ml_h", 1)
        ml_og = sig("ml_og", 2)
        ml_ht = sig("ml_ht", 1)
        ml_y = sig("ml_y", 2)
        ml_yhi = sig("ml_yhi", 2)
        ml_done = sig("ml_done", 1)
        st_out = sig("st_out", 48)
        x_back = sig("x_back", 16)
        at_in = sig("at_in", 32)
        at_k1 = sig("at_k1", 1)
        at_krt = sig("at_krt", 1)
        kr_t = sig("kr_t", 1)
        H = HEADS_A
        hw_in = [sig(f"hw_in{i}", 4 * 16) for i in range(2)]
        at_proj = sig("at_proj", H, first=1)
        at_tok = sig("at_tok", H)
        at_ktok = sig("at_ktok", H)
        at_sq = sig("at_sq", H)
        at_var = sig("at_var", H)
        at_root = sig("at_root", H)
        at_rope = sig("at_rope", H)
        at_trp = sig("at_trp", H)
        at_hi = sig("at_hi", H)
        at_lo = sig("at_lo", H)
        at_s = sig("at_s", TILES * H)
        at_mx = sig("at_mx", TILES * H)
        at_mrow = sig("at_mrow", H)
        at_mhi = sig("at_mhi", H)
        at_mlo = sig("at_mlo", H)
        STEPS = 19
        at_st = sig("at_st", STEPS * H)
        at_exp = sig("at_exp", STEPS * H)
        at_pv = sig("at_pv", STEPS * H)
        at_y = sig("at_y", 3 * H, first=1)
        at_yhi = sig("at_yhi", 3 * H)
        at_done = sig("at_done", 3 * H, first=1)
        f_in = [sig(f"f_in{i}", 3 * NG * 16) for i in range(2)]
        f_hi_ok = sig("f_hi_ok", 6 * NG)
        f_lo_ok = sig("f_lo_ok", 6 * NG)
        f_gu = sig("f_gu", 6 * NG)
        f_silu = sig("f_silu", 6 * NG)
        f_act = sig("f_act", 6 * NG, first=1)
        f_dn = sig("f_dn", 24 * NG, first=1)
        f_res = sig("f_res", 24 * NG, first=1)
        y_out = sig("y_out", 0)
        pe_own = ctx.enter_context(nc.semaphore("pe_own"))
        act_own = ctx.enter_context(nc.semaphore("act_own"))
        dve_own = ctx.enter_context(nc.semaphore("dve_own"))

        A = nc.scalar.activation
        V = nc.vector
        MM = nc.tensor.matmul

        block = ctx.enter_context(nc.Block())

        @block.sync
        def _(sp):
            sp.dma_start(cst[:, :], const).then_inc(const_in.sem, 16)
            sp.dma_start(cond[:, :, :], cvec).then_inc(const_in.sem, 16)
            sp.dma_start(x[:, :, :], xin).then_inc(const_in.sem, 16)
            with sp.Fori(0, DEPTH) as l:
                sp.wait_ge(f_res.sem, f_res.at(l, 0))
                sp.dma_start(vecs[:, :], vec[bass.ds(l, 1)].rearrange("a p n -> (a p) n")).then_inc(vec_in.sem, 16)
                for p in range(12):
                    if p >= 2:
                        sp.wait_ge(ada_used.sem, ada_used.at(l, p - 1))
                    sp.dma_start(wada_sb[:, p % 2], wada[bass.ds(l, 1), p].rearrange("a p j k n -> (a p) j k n")) \
                        .then_inc(ada_in[p % 2].sem, 16)
                sp.wait_ge(const_in.sem, 48)
                sp.dma_start(spill, x[:, :, :]).then_inc(spilled.sem, 32)
                sp.wait_ge(alo_ok.sem, alo_ok.at(l, KC))
                sp.wait_ge(spilled.sem, spilled.at(l, 32))
                for n in range(16):
                    if n >= 2:
                        sp.wait_ge(w_hi_ok.sem, w_hi_ok.at(l, n - 1))
                        sp.wait_ge(w_lo_ok.sem, w_lo_ok.at(l, n - 1))
                    sp.dma_start(w_raw[:, n % 2], win[bass.ds(l, 1), n].rearrange("a p n -> (a p) n")) \
                        .then_inc(w_in_[n % 2].sem, 16)
                sp.wait_ge(w_used.sem, w_used.at(l, 16))
                sp.dma_start(pw[:, :, :, :], pww[bass.ds(l, 1)].rearrange("a p k o n -> (a p) k o n")).then_inc(pw_in.sem, 16)
                sp.wait_ge(cq_ok.sem, cq_ok.at(l, 1))
                sp.dma_start(o_ckv[bass.ds(l, 1)].rearrange("a p n -> (a p) n"), zc(Z_CKV)[:, 0:SEQ]).then_inc(ckv_out.sem, 16)
                for g in range(2):
                    sp.dma_start(o_kr[bass.ds(l, 1), g].rearrange("a p n -> (a p) n"),
                                 zc(Z_MISC)[4 + 32 * g:20 + 32 * g, 0:SEQ]).then_inc(ckv_out.sem, 16)
                sp.wait_ge(cv_done.sem, cv_done.at(l, 1))
                sp.dma_start(mc[:, :], mconst[:, 0:M_RESET]).then_inc(ml_in.sem, 16)
                sp.dma_start(reset[:, :], mconst[0:DH, M_RESET:NMC]).then_inc(ml_in.sem, 16)
                sp.dma_start(cst_st[:, 1], c0[bass.ds(l, 1)].rearrange("a p d j n -> (a p) d j n")).then_inc(ml_in.sem, 16)
                sp.wait_ge(ml_out.sem, ml_out.at(l, 2))
                sp.dma_start(o_c[bass.ds(l, 1)].rearrange("a p d j n -> (a p) d j n"), cst_st[:, 0]).then_inc(st_out.sem, 16)
                sp.dma_start(o_m[bass.ds(l, 1), 0].rearrange("a p n -> (a p) n"), rb[DH:DH + 4, SEQ - 1:SEQ]).then_inc(st_out.sem, 16)
                sp.dma_start(o_m[bass.ds(l, 1), 1].rearrange("a p n -> (a p) n"), rb[DH + 32:DH + 36, 0:1]).then_inc(st_out.sem, 16)
                sp.wait_ge(ml_done.sem, ml_done.at(l, 1))
                sp.wait_ge(st_out.sem, st_out.at(l, 48))
                sp.dma_start(x[:, :, :], spill).then_inc(x_back.sem, 16)
                sp.dma_start(ctxk[:, :], ctx_ckv[bass.ds(l, 1)].rearrange("a p n -> (a p) n")).then_inc(at_in.sem, 16)
                sp.dma_start(krt[:, TILES, :], ctx_kr[bass.ds(l, 1)].rearrange("a p n -> (a p) n")).then_inc(at_in.sem, 16)
                with sp.Fori(0, H // 2) as i:
                    for e in range(2):
                        sp.wait_ge(at_proj.sem, at_proj.at(l, i * 2))
                        sp.dma_start(hw[:, e], whd[bass.ds(l, 1), bass.ds(i * 2 + e, 1)]
                                     .rearrange("a b p n -> (a b p) n")).then_inc(hw_in[e].sem, 16)
                sp.wait_ge(at_done.sem, at_done.at(l, 3 * H))
                sp.wait_ge(at_exp.sem, at_exp.at(l, STEPS * H))
                for n in range(16, 24):
                    if n >= 18:
                        sp.wait_ge(w_hi_ok.sem, w_hi_ok.at(l, n - 1))
                        sp.wait_ge(w_lo_ok.sem, w_lo_ok.at(l, n - 1))
                    sp.dma_start(w_raw[:, n % 2], wout[bass.ds(l, 1), n - 16].rearrange("a p n -> (a p) n")) \
                        .then_inc(w_in_[n % 2].sem, 16)
                sp.wait_ge(alo_ok.sem, alo_ok.at(l, 2 * KC))

                def ff(slot, before, src):
                    if before is not None:
                        sp.wait_ge(f_hi_ok.sem, before)
                        sp.wait_ge(f_lo_ok.sem, before)
                    sp.dma_start(f_raw[:, slot], src).then_inc(f_in[slot].sem, 16)

                def gu_src(f, part):
                    return wgu[bass.ds(l, 1), f, :, part].rearrange("a p n -> (a p) n")

                for n in range(4):
                    ff(n % 2, f_hi_ok.at(l, n - 1) if n >= 2 else None, gu_src(n // 2, n % 2))
                with sp.Fori(0, NG - 1) as g:
                    base = f_hi_ok.at(l, g * 6)
                    for n in range(2):
                        ff(n, base + 4 + n - 1, wdn[bass.ds(l, 1), bass.ds(g * 2 + n, 1)].rearrange("a b p n -> (a b p) n"))
                    for n in range(4):
                        ff(n % 2, base + 6 + n - 1,
                           wgu[bass.ds(l, 1), bass.ds(g * 2 + (2 + n // 2), 1), :, n % 2].rearrange("a b p n -> (a b p) n"))
                for n in range(2):
                    ff(n, f_hi_ok.at(l, 6 * (NG - 1) + 4 + n - 1), wdn[bass.ds(l, 1), 2 * (NG - 1) + n].rearrange("a p n -> (a p) n"))
            sp.wait_ge(f_res.sem, f_res.at(DEPTH, 0))
            sp.dma_start(yout, x[:, :, :]).then_inc(y_out.sem, 16)
            sp.wait_ge(y_out.sem, 16)
            sp.wait_ge(ckv_out.sem, ckv_out.at(DEPTH, 0))
            sp.wait_ge(st_out.sem, st_out.at(DEPTH, 0))
            sp.wait_ge(spilled.sem, spilled.at(DEPTH, 0))

        @block.tensor
        def _(pe):
            for s in (f_dn, at_proj):
                pe.sem_inc(s.sem, 1)
            pe.wait_ge(const_in.sem, 48)
            pe.wait_ge(cond_ok.sem, 1)
            with pe.Fori(0, DEPTH) as l:
                pe.wait_ge(f_res.sem, f_res.at(l, 0))
                for p in range(12):
                    pe.wait_ge(ada_in[p % 2].sem, ada_in[0].at(l, 16 * (p // 2 + 1)))
                    for j in range(4):
                        for k in range(KC):
                            mm = MM(ps[:, 7, (4 * p + j) * 2:(4 * p + j) * 2 + 2], wada_sb[:, p % 2, j, k, :], cond[:, k, :],
                                    start=(k == 0), stop=(k == KC - 1))
                    mm.then_inc(ada_used.sem, 1)

                def norm(which):
                    for c in range(KC):
                        pe.wait_ge(sq_ok.sem, sq_ok.at(l, which * KC + c + 1))
                        for t in range(TILES):
                            mm = MM(ps[:, 6, t:t + 1], nsq[:, c % 2, t * P:(t + 1) * P], ones[:, 0:1],
                                    start=(c == 0 and t == 0), stop=(c == KC - 1), skip_group_check=True)
                        mm.then_inc(sq_used.sem, 1)
                    pe.wait_ge(rs_diag.sem, rs_diag.at(l, which + 1))
                    for t in range(TILES):
                        mm = MM(flat[:, t * P:(t + 1) * P], ones, diag[:, t, :], start=True, stop=True)
                    mm.then_inc(rs_row.sem, 1)

                def chunk3(n, wait_rhs):
                    pe.wait_ge(w_lo_ok.sem, w_lo_ok.at(l, n + 1))
                    if n in (3, 5):
                        pe.wait_ge(z_free_d.sem, z_free_d.at(l, n // 2))
                    elif n >= 18:
                        pe.wait_ge(z_free_d.sem, z_free_d.at(l, n - 15))
                    elif n >= 2:
                        pe.wait_ge(z_free_a.sem, z_free_a.at(l, n // 2 if n < 6 else n - 3))
                    for k in range(KC):
                        if wait_rhs:
                            pe.wait_ge(alo_ok.sem, alo_ok.at(l, k + 1))
                        whi, wlo = w_hi[:, n % 2, k * P:(k + 1) * P], w_lo[:, n % 2, k * P:(k + 1) * P]
                        for w, a, first, last in ((whi, a_hi, True, False), (whi, a_lo, False, False), (wlo, a_hi, False, True)):
                            for b in range(NB):
                                mm = MM(ps[:, 3 * (n % 2) + b, 0:BLK], w, a[:, k, b * BLK:(b + 1) * BLK],
                                        start=(k == 0 and first), stop=(k == KC - 1 and last))
                    mm.then_inc(w_used.sem, 1)

                norm(0)
                pe.wait_ge(alo_ok.sem, alo_ok.at(l, KC))
                for n in range(16):
                    chunk3(n, False)

                pe.wait_ge(z_free_a.sem, z_free_a.at(l, 14))
                for i, cs in enumerate(((0, 1), (2,))):
                    for c in cs:
                        pe.wait_ge(c_sq.sem, c_sq.at(l, c + 1))
                        for t in range(TILES):
                            sq = csq[:, c % 2, t * P:(t + 1) * P]
                            mm = MM(ps[:, 6, 16 * i + t:16 * i + t + 1], sq, ones[:, 0:1],
                                    start=(c == cs[0] and t == 0), stop=(c == cs[-1]), skip_group_check=True)
                    mm.then_inc(c_sum.sem, 1)
                    pe.wait_ge(c_diag.sem, c_diag.at(l, i + 1))
                    for t in range(TILES):
                        mm = MM(flat[:, t * P:(t + 1) * P], ones, diag[:, t, :], start=True, stop=True)
                    mm.then_inc(c_row.sem, 1)

                pe.wait_ge(cv_y.sem, cv_y.at(l, 1))
                for b in range(NB):
                    for c in range(2):
                        mm = MM(ps[:, 3 + b, 0:BLK], ones, csq[:, c, b * BLK:(b + 1) * BLK], start=(c == 0), stop=(c == 1))
                mm.then_inc(cv_sum.sem, 1)
                pe.wait_ge(cv_sq.sem, cv_sq.at(l, 1))
                for c in range(2):
                    for t in range(TILES):
                        mm = MM(ps[:, 6, 32 + t:33 + t], csq[:, c, t * P:(t + 1) * P], ones[:, 0:1],
                                start=(c == 0 and t == 0), stop=(c == 1), skip_group_check=True)
                mm.then_inc(cv_sum.sem, 1)
                pe.wait_ge(cv_diag.sem, cv_diag.at(l, 1))
                for t in range(TILES):
                    mm = MM(flat[:, t * P:(t + 1) * P], ones, diag[:, t, :], start=True, stop=True)
                mm.then_inc(cv_row.sem, 1)
                pe.wait_ge(cv_act.sem, cv_act.at(l, 1))
                pe.wait_ge(pw_in.sem, pw_in.at(l, 16))
                for o in range(2):
                    for b in range(NB):
                        for c in range(2):
                            mm = MM(ps[:, 3 * o + b, 0:BLK], pw[:, c, o, :], csq[:, c, b * BLK:(b + 1) * BLK],
                                    start=(c == 0), stop=(c == 1))
                mm.then_inc(cv_pw.sem, 1)

                pe.wait_ge(ml_dexp.sem, ml_dexp.at(l, 1))
                pe.wait_ge(cv_done.sem, cv_done.at(l, 1))
                for dj in range(4):
                    mm = MM(ps[:, 7, dj * TILES:(dj + 1) * TILES], mc[0:DH, M_PAIR + dj * P:M_PAIR + (dj + 1) * P],
                            mrow[:, 3, :], start=True, stop=True)
                mm.then_inc(ml_tr.sem, 1)
                for t in range(TILES):
                    mm = nc.tensor.transpose(flat[:, t * P:(t + 1) * P], ra[:, t * P:(t + 1) * P], ident)
                mm.then_inc(ml_tr.sem, 1)
                for t in range(TILES):
                    mm = nc.tensor.transpose(flat[:, 1536 + t * P:1536 + (t + 1) * P], rb[:, t * P:(t + 1) * P], ident)
                mm.then_inc(ml_tr.sem, 1)
                pe.wait_ge(ml_cols.sem, ml_cols.at(l, 1))
                pe.wait_ge(ml_dcol.sem, ml_dcol.at(l, 1))
                for t in range(TILES):
                    if t >= 2:
                        pe.wait_ge(ml_kv_a.sem, ml_kv_a.at(l, t - 1))
                        pe.wait_ge(ml_kv_v.sem, ml_kv_v.at(l, t - 1))
                    for c in range(4):
                        mm = nc.tensor.transpose(ps[:, t % 2 + 2 * (c // 2), (c % 2) * P:(c % 2 + 1) * P], zc(Z_K + c)[:, t * P:(t + 1) * P], ident)
                    mm.then_inc(ml_kvt.sem, 1)
                pe.wait_ge(ml_kv_v.sem, ml_kv_v.at(l, TILES))
                pe.wait_ge(ml_kv_a.sem, ml_kv_a.at(l, TILES))
                pe.wait_ge(ml_zero.sem, ml_zero.at(l, 1))
                for i in range(TILES):
                    tiles = (i, (TILES - i) % TILES)
                    if i:
                        pe.wait_ge(ml_s.sem, ml_s.at(l, 2 * i))
                    for d, t in enumerate(tiles):
                        ts = slice(t * P, (t + 1) * P)
                        for h in range(HEADS_M):
                            sel = mc[0:DH, M_SEL + (4 * d + h) * P:M_SEL + (4 * d + h + 1) * P]
                            mm = MM(ps[:, d, h * P:(h + 1) * P], sel, rr[:, ts], start=True, stop=True)
                        mm.then_inc(ml_bc.sem, 1)
                    for d, t in enumerate(tiles):
                        ts = slice(t * P, (t + 1) * P)
                        for h in range(HEADS_M):
                            half, at0 = slice(DH * (h % 2), DH * (h % 2) + DH), 2 * P * d + P * (h // 2)
                            mm = MM(ps[:, 2 + h % 2, at0:at0 + P], zc(Z_K + h // 2)[half, ts], zc(Z_Q + h // 2)[half, ts],
                                    start=True, stop=True)
                    mm.then_inc(ml_qk.sem, 1)
                    if i:
                        pe.wait_ge(ml_out.sem, ml_out.at(l, 2 * i))
                    for d, t in enumerate(tiles):
                        for h in range(HEADS_M):
                            half, at0 = slice(DH * (h % 2), DH * (h % 2) + DH), 130 * d + 65 * (h // 2)
                            MM(ps[:, 4 + h % 2, at0:at0 + 65], zc(Z_Q + h // 2)[half, t * P:(t + 1) * P],
                               cst_st[half, min(i, 1), d, h // 2, :], start=True, stop=True)
                    for d, t in enumerate(tiles):
                        pe.wait_ge(ml_kw.sem, ml_kw.at(l, 2 * i + d + 1))
                        for h in range(HEADS_M):
                            half = slice(DH * (h % 2), DH * (h % 2) + DH)
                            MM(ps[half, 6 + d, 260 + 65 * (h // 2):325 + 65 * (h // 2)], kw[:, d, h, :], vaug[:, t, h, :],
                               start=True, stop=True)
                        pe.wait_ge(ml_s.sem, ml_s.at(l, 2 * i + d + 1))
                        for h in range(HEADS_M):
                            mm = MM(ps[:, 6 + d, h * 65:(h + 1) * 65], sp_[:, d, h, :], vaug[:, t, h, :], start=True, stop=True)
                        mm.then_inc(ml_pv.sem, 1)
                pe.wait_ge(ml_h.sem, ml_h.at(l, 1))
                for c in range(2):
                    for t in range(TILES):
                        mm = nc.tensor.transpose(flat[:, 1536 * c + t * P:1536 * c + (t + 1) * P],
                                                 hnum[:, t, 2 * c:2 * c + 2, :].rearrange("p h d -> p (h d)"), ident)
                mm.then_inc(ml_ht.sem, 1)

                pe.wait_ge(ml_done.sem, ml_done.at(l, 1))
                for t in range(TILES):
                    mm = nc.tensor.transpose(flat[:, t * P:(t + 1) * P], zc(Z_MISC)[:, t * P:(t + 1) * P], ident)
                mm.then_inc(kr_t.sem, 1)
                with pe.Fori(0, H // 2) as i:
                    for e in range(2):
                        h = i * 2 + e

                        def at_(s, n, k):
                            return s.at(l, (i * 2 + e) * n + k)

                        pe.wait_ge(at_in.sem, at_in.at(l, 32))
                        pe.wait_ge(at_krt.sem, at_krt.at(l, 1))
                        pe.wait_ge(at_k1.sem, at_k1.at(l, 1))
                        pe.wait_ge(hw_in[e].sem, hw_in[e].at(l, i * 16 + 16))
                        pe.wait_ge(at_done.sem, at_(at_done, 3, 0))
                        for t in range(TILES):
                            for c in range(2):
                                MM(ps[:, t // 5, (t % 5) * QK:(t % 5 + 1) * QK], zc(Z_CQ + c)[:, t * P:(t + 1) * P],
                                   hw[:, e, c * QK:(c + 1) * QK], start=(c == 0), stop=(c == 1))
                        for t in range(KTILES):
                            lat = zc(Z_CKV)[:, t * P:(t + 1) * P] if t < TILES else ctxk[:, :]
                            mm = MM(flat[:, 1024 + t * P:1024 + (t + 1) * P], lat, hw[:, e, 2 * QK:2 * QK + P], start=True, stop=True)
                        mm.then_inc(at_proj.sem, 1)
                        pe.wait_ge(at_rope.sem, at_(at_rope, 1, 1))
                        for t in range(TILES):
                            nc.tensor.transpose(flat[0:QK, t * P:(t + 1) * P], qt_[:, t, :], ident)
                        for t in range(KTILES):
                            mm = nc.tensor.transpose(flat[0:QK, 1536 + t * P:1536 + (t + 1) * P], kt_[:, t, :], ident)
                        mm.then_inc(at_trp.sem, 1)
                        pe.wait_ge(at_lo.sem, at_(at_lo, 1, 1))
                        pe.wait_ge(at_hi.sem, at_(at_hi, 1, 1))
                        for t in range(TILES):
                            if t >= 2:
                                pe.wait_ge(at_mx.sem, at_(at_mx, TILES, t - 1))
                            q = qh[0:QK, t * P:(t + 1) * P]
                            if t == 0:
                                mm = MM(ps[:, 0, 0:SEQ], q, kh[0:QK, 0:SEQ], start=True, stop=True)
                            else:
                                for b in range(NB):
                                    mm = MM(ps[:, 3 * (t % 2) + b, 0:BLK], q, kh[0:QK, SEQ + b * BLK:SEQ + (b + 1) * BLK],
                                            start=True, stop=True)
                            mm.then_inc(at_s.sem, 1)
                        pe.wait_ge(at_mx.sem, at_(at_mx, TILES, TILES))
                        for t in range(TILES):
                            mm = MM(flat[QK:QK + 1, t * P:(t + 1) * P], nmx[:, t:t + 1], ident, start=True, stop=True)
                        mm.then_inc(at_mrow.sem, 1)
                        pe.wait_ge(at_mlo.sem, at_(at_mlo, 1, 1))
                        pe.wait_ge(at_mhi.sem, at_(at_mhi, 1, 1))
                        steps = [(0, 0, SEQ, 0)] + [(1 + qb, SEQ + 512 * qb, 512, kt0) for qb in range(2) for kt0 in range(1, KTILES)]

                        def pv(s):
                            o, _, n, kt0 = steps[s]
                            if o and kt0 == 1:
                                pe.wait_ge(at_y.sem, at_(at_y, 3, max(o - 1, 0)))
                            pe.wait_ge(at_exp.sem, at_(at_exp, STEPS, s + 1))
                            MM(ps[:, 6 + o % 2, 0:n], va[:, kt0, :], pt[:, s % 3, 0:n], start=(kt0 <= 1),
                               stop=(kt0 == 0 or kt0 == KTILES - 1)).then_inc(at_pv.sem, 1)

                        for s, (o, q0, n, kt0) in enumerate(steps):
                            if s >= 3:
                                pe.wait_ge(at_exp.sem, at_(at_exp, STEPS, s - 2))
                            ks, qs = slice(kt0 * P, (kt0 + 1) * P), slice(q0, q0 + n)
                            MM(ps[:, 3 + s % 3, 0:n], kh[0:QK + 1, ks], qh[0:QK + 1, qs], start=True, stop=False)
                            MM(ps[:, 3 + s % 3, 0:n], kh[0:QK + 1, ks], ql[0:QK + 1, qs], start=False, stop=False)
                            MM(ps[:, 3 + s % 3, 0:n], kl[0:QK + 1, ks], qh[0:QK + 1, qs], start=False, stop=True).then_inc(at_st.sem, 1)
                            if s >= 2:
                                pv(s - 2)
                        pv(STEPS - 2)
                        pv(STEPS - 1)

                pe.wait_ge(at_done.sem, at_done.at(l, 3 * H))
                for n in range(16, 24):
                    chunk3(n, False)
                pe.wait_ge(z_free_d.sem, z_free_d.at(l, 10))
                norm(1)
                pe.wait_ge(alo_ok.sem, alo_ok.at(l, 2 * KC))

                def unit(v, g):
                    f, b = v // NB, v % NB
                    pe.wait_ge(f_lo_ok.sem, f_lo_ok.at(l, g * 6 + 2 * (f + 1)))
                    pe.wait_ge(f_hi_ok.sem, f_hi_ok.at(l, g * 6 + 2 * (f + 1)))
                    if v >= 1 or not isinstance(g, int):
                        pe.wait_ge(f_act.sem, f_act.at(l, g * 6 + (v - 1)))
                    for part in range(2):
                        for k in range(KC):
                            whi, wlo = gu_hi[:, f, part, k, :], gu_lo[:, f, part, k, :]
                            for j, (w, a) in enumerate(((whi, a_hi), (whi, a_lo), (wlo, a_hi))):
                                mm = MM(ps[:, 2 * (v % 2) + part, 0:BLK], w, a[:, k, b * BLK:(b + 1) * BLK],
                                        start=(k == 0 and j == 0), stop=(k == KC - 1 and j == 2))
                    mm.then_inc(f_gu.sem, 1)

                def down(g):
                    pe.wait_ge(f_act.sem, f_act.at(l, g * 6 + 6))
                    pe.wait_ge(f_lo_ok.sem, f_lo_ok.at(l, g * 6 + 6))
                    pe.wait_ge(f_hi_ok.sem, f_hi_ok.at(l, g * 6 + 6))
                    for o in range(KC):
                        for b in range(NB):
                            n = o * NB + b
                            pe.wait_ge(f_res.sem, f_res.at(l, g * 24 + max(n - 3, 0)))
                            bs, os_ = slice(b * BLK, (b + 1) * BLK), slice(o * P, (o + 1) * P)
                            for f in range(2):
                                for j, (w, a) in enumerate(((d_hi, g_hi), (d_hi, g_lo), (d_lo, g_hi))):
                                    mm = MM(ps[:, 4 + n % 4, 0:BLK], w[:, f, os_], a[:, f, bs],
                                            start=(f == 0 and j == 0), stop=(f == 1 and j == 2))
                            mm.then_inc(f_dn.sem, 1)

                unit(0, 0)
                with pe.Fori(0, NG - 1) as g:
                    for v in range(1, 6):
                        unit(v, g)
                    unit(0, g + 1)
                    down(g)
                for v in range(1, 6):
                    unit(v, NG - 1)
                down(NG - 1)

        @block.scalar
        def _(act):
            act.wait_ge(const_in.sem, 48)
            A(cond[:, :, :], cond[:, :, :], ACT.Silu).then_inc(cond_ok.sem, 1)
            with act.Fori(0, DEPTH) as l:
                own = Chain(act, act_own, l)

                def root(src, dst, k):
                    act.wait_ge(rs_var.sem, rs_var.at(l, k))
                    A(dst, src, ACT.Sqrt).then_inc(rs_root.sem, 1)

                def norm(which):
                    for c in range(KC):
                        if which:
                            act.wait_ge(z_free_d.sem, z_free_d.at(l, 2 + c + 1))
                        if c >= 2:
                            act.wait_ge(sq_used.sem, sq_used.at(l, which * KC + c - 1))
                        A(nsq[:, c % 2, :], x[:, c, :], ACT.Square).then_inc(sq_ok.sem, 1)
                    root(small[:, 0:TILES], small[:, 9:9 + TILES], (1, 5)[which])
                    for c in range(KC):
                        act.wait_ge(nh_ok.sem, nh_ok.at(l, which * KC + c + 1))
                        A(a_hi[:, c, :], nt[:, c % 2, :], ACT.Copy).then_inc(ahi_ok.sem, 1)

                def w_high(n):
                    act.wait_ge(w_in_[n % 2].sem, w_in_[0].at(l, 16 * (n // 2 + 1)))
                    if n >= 2:
                        act.wait_ge(w_used.sem, w_used.at(l, n - 1))
                    A(w_hi[:, n % 2, :], w_raw[:, n % 2, :], ACT.Copy).then_inc(w_hi_ok.sem, 1)

                act.wait_ge(ada_used.sem, ada_used.at(l, 12))
                norm(0)
                w_high(0)
                w_high(1)
                for n in range(16):
                    src = banks(3 * (n % 2))
                    if n < 4:
                        if n % 2 == 0:
                            act.wait_ge(w_used.sem, w_used.at(l, n + 1))
                            if n:
                                act.wait_ge(z_free_d.sem, z_free_d.at(l, 1))
                            A(blocks(sigb[:, :]), src, ACT.Sigmoid).then_inc(z_free_a.sem, 1)
                    else:
                        act.wait_ge(w_used.sem, w_used.at(l, n + 1))
                        if n == 4:
                            act.wait_ge(spilled.sem, spilled.at(l, 32))
                        A(blocks(zc(n - 4)), src, ACT.Copy, scale=SCALE_M if n - 4 < Z_K else 1.0).then_inc(z_free_a.sem, 1)
                    if n + 2 < 16:
                        w_high(n + 2)

                act.wait_ge(z_free_a.sem, z_free_a.at(l, 14))
                for c in range(3):
                    if c == 2:
                        act.wait_ge(c_sum.sem, c_sum.at(l, 1))
                    A(csq[:, c % 2, :], zc(Z_CQ + c), ACT.Square).then_inc(c_sq.sem, 1)
                    if c:
                        root(small[:, 0:TILES], small[:, 9:9 + TILES], 1 + c)

                act.wait_ge(cv_xc.sem, cv_xc.at(l, 1))
                A(csq[:, :, :], yc[:, :, 0:TOK], ACT.Square).then_inc(cv_sq.sem, 1)
                root(small[:, 0:TILES], small[:, 9:9 + TILES], 4)
                act.wait_ge(cv_n.sem, cv_n.at(l, 1))
                for c in range(2):
                    aa = A(csq[:, c, :], yc[:, c, 0:TOK], ACT.Silu, bias=vecs[:, V_LNB + c:V_LNB + c + 1],
                           scale=vecs[:, V_LNG + c:V_LNG + c + 1])
                aa.then_inc(cv_act.sem, 1)
                act.wait_ge(cv_pw.sem, cv_pw.at(l, 1))
                for o in range(2):
                    A(blocks(a_hi[:, 2 + o, :]), banks(3 * o), ACT.Copy).then_inc(cv_hi.sem, 1)

                act.wait_ge(cv_done.sem, cv_done.at(l, 1))
                misc = zc(Z_MISC)
                bg = vecs[:, V_BG:V_BG + 1]
                A(rb[0:DH, :], misc[0:DH, :], ACT.Identity, bias=bg[0:DH, :])
                own.link(A(ra[0:DH, :], misc[DH:P, :], ACT.Abs, bias=bg[DH:P, :]))
                own.link(A(ra[0:DH, :], ra[0:DH, :], ACT.Exp, scale=-1.0))
                A(lf[:, :], ra[0:DH, :], ACT.Ln, bias=ones[0:DH, 0:1]).then_inc(ml_ln.sem, 1)
                act.wait_ge(ml_rows.sem, ml_rows.at(l, 1))
                A(mrow[:, 3, :], mrow[:, 2, :], ACT.Exp).then_inc(ml_dexp.sem, 1)

                def turned(half, row):
                    return flat[:, 1536 * half:1536 * half + TOK].rearrange("p (t q c) -> p t q c", q=4, c=32)[
                        :, :, 2 * row:2 * row + 2, 0:HEADS_M]

                def by_head(ap):
                    return ap.rearrange("p t (d h) -> p t d h", d=2)

                act.wait_ge(ml_tr.sem, ml_tr.at(l, 3))
                A(by_head(cols[:, 0]), turned(0, 0), ACT.Copy)
                A(by_head(cols[:, 1]), turned(0, 1), ACT.Exp)
                A(by_head(cols[:, 2]), turned(1, 0), ACT.Exp)
                A(by_head(cols[:, 3]), turned(1, 1), ACT.Exp, scale=-1.0).then_inc(ml_cols.sem, 1)
                for t in range(TILES):
                    act.wait_ge(ml_kvt.sem, ml_kvt.at(l, t + 1))
                    A(kt[:, t, :], ps[:, t % 2, 0:2 * P], ACT.Copy).then_inc(ml_kv_a.sem, 1)
                act.wait_ge(ml_cols.sem, ml_cols.at(l, 1))
                for i in range(TILES):
                    for d, t in enumerate((i, (TILES - i) % TILES)):
                        act.wait_ge(ml_em.sem, ml_em.at(l, 2 * i + d + 1))
                        for h in range(HEADS_M):
                            aa = A(em[:, d, h, :], em[:, d, h, :], ACT.Exp, bias=cols[:, 0, t, 4 * d + h:4 * d + h + 1])
                        aa.then_inc(ml_exp.sem, 1)
                for c in range(2):
                    A(zc(Z_O + c), zc(Z_O + c), ACT.Sigmoid).then_inc(ml_og.sem, 1)
                act.wait_ge(ml_hsum.sem, ml_hsum.at(l, 1))
                A(hsq[:, :, :].rearrange("p (t h) d -> p t (h d)", h=4), hnum[:, :, 0:4, :].rearrange("p t h d -> p t (h d)"),
                  ACT.Square).then_inc(ml_hsq.sem, 1)
                act.wait_ge(ml_var.sem, ml_var.at(l, 1))
                A(den[:, 2, :, 0:4], den[:, 1, :, 0:4], ACT.Sqrt).then_inc(ml_root.sem, 1)
                for c in range(2):
                    act.wait_ge(ml_y.sem, ml_y.at(l, c + 1))
                    A(a_hi[:, c, :], yt[:, :], ACT.Copy).then_inc(ml_yhi.sem, 1)

                with act.Fori(0, H // 2) as i:
                    for e in range(2):
                        def at_(s, n, k):
                            return s.at(l, (i * 2 + e) * n + k)

                        act.wait_ge(at_proj.sem, at_(at_proj, 1, 1))
                        A(qt_[:, 0:5, :], ps[:, 0, 0:5 * QK].rearrange("p (t n) -> p t n", n=QK), ACT.Copy)
                        A(qt_[:, 5:9, :], ps[:, 1, 0:4 * QK].rearrange("p (t n) -> p t n", n=QK), ACT.Copy)
                        kv = flat[:, 1024:1024 + KTILES * P].rearrange("p (t n) -> p t n", n=P)
                        A(kt_[:, :, 0:NOPE], kv[:, :, 0:NOPE], ACT.Copy).then_inc(at_tok.sem, 1)
                        act.wait_ge(at_tok.sem, at_(at_tok, 1, 1))
                        act.wait_ge(at_ktok.sem, at_(at_ktok, 1, 1))
                        A(sq_[:, 0:TILES, :], qt_[:, :, :], ACT.Square)
                        A(sq_[:, TILES:, :], kt_[:, :, :], ACT.Square).then_inc(at_sq.sem, 1)
                        act.wait_ge(at_var.sem, at_(at_var, 1, 1))
                        A(small[:, 20:39], small[:, 0:19], ACT.Sqrt).then_inc(at_root.sem, 1)
                        act.wait_ge(at_trp.sem, at_(at_trp, 1, 1))
                        A(qh[0:QK, :], flat[0:QK, 0:TOK], ACT.Copy)
                        A(kh[0:QK, :], flat[0:QK, 1536:1536 + KEYS], ACT.Copy).then_inc(at_hi.sem, 1)
                        act.wait_ge(at_mrow.sem, at_(at_mrow, 1, 1))
                        A(qh[QK:QK + 1, :], flat[QK:QK + 1, 0:TOK], ACT.Copy).then_inc(at_mhi.sem, 1)

                        def yhigh(o):
                            act.wait_ge(at_y.sem, at_(at_y, 3, o + 1))
                            q0, n = ((0, SEQ), (SEQ, 512), (SEQ + 512, 512))[o]
                            half = slice(DH * e, DH * e + DH)
                            A(a_hi[half, bass.ds(i + 4, 1), q0:q0 + n], ya[half, 0:n].unsqueeze(1), ACT.Copy).then_inc(at_yhi.sem, 1)

                        for s in range(STEPS):
                            n = SEQ if s == 0 else 512
                            act.wait_ge(at_st.sem, at_(at_st, STEPS, s + 1))
                            if s >= 3:
                                act.wait_ge(at_pv.sem, at_(at_pv, STEPS, s - 2))
                            A(pt[:, s % 3, 0:n], ps[:, 3 + s % 3, 0:n], ACT.Exp, scale=SCALE_A).then_inc(at_exp.sem, 1)
                            if s in (5, 14):
                                yhigh(s // 10)
                        yhigh(2)

                act.wait_ge(at_done.sem, at_done.at(l, 3 * H))
                for n in range(16, 24):
                    w_high(n)
                act.wait_ge(w_used.sem, w_used.at(l, 24))
                norm(1)

                def f_high(slot, count, dst, used_sem, used):
                    act.wait_ge(f_in[slot].sem, f_in[0].at(l, count))
                    if used_sem is not None:
                        act.wait_ge(used_sem.sem, used)
                    A(dst, f_raw[:, slot], ACT.Copy).then_inc(f_hi_ok.sem, 1)

                def silu(v, g):
                    act.wait_ge(f_gu.sem, f_gu.at(l, g * 6 + (v + 1)))
                    if v >= 1 or not isinstance(g, int):
                        act.wait_ge(f_act.sem, f_act.at(l, g * 6 + (v - 1)))
                    A(sg[:, v % 2, :], ps[:, 2 * (v % 2), 0:BLK], ACT.Silu).then_inc(f_silu.sem, 1)

                act.wait_ge(alo_ok.sem, alo_ok.at(l, 2 * KC))
                for n in range(4):
                    f_high(n % 2, 16 * (n // 2 + 1), gu_hi[:, n // 2, n % 2], None, None)
                silu(0, 0)
                with act.Fori(0, NG - 1) as g:
                    for n in range(2):
                        f_high(n, 32 + g * 48 + 16, d_hi[:, n], f_dn, f_dn.at(l, g * 24))
                    silu(1, g)
                    silu(2, g)
                    for n in range(2):
                        f_high(n, 32 + g * 48 + 32, gu_hi[:, 0, n], f_gu, f_gu.at(l, g * 6 + 3))
                    for v in range(3, 6):
                        silu(v, g)
                    for n in range(2):
                        f_high(n, 32 + g * 48 + 48, gu_hi[:, 1, n], f_gu, f_gu.at(l, g * 6 + 6))
                    silu(0, g + 1)
                for n in range(2):
                    f_high(n, 32 + (NG - 1) * 48 + 16, d_hi[:, n], f_dn, f_dn.at(l, (NG - 1) * 24))
                for v in range(1, 6):
                    silu(v, NG - 1)
                own.end_layer()

        @block.vector
        def _(dve):
            for s in (f_res, at_done, at_y, f_act):
                dve.sem_inc(s.sem, 1)
            dve.wait_ge(const_in.sem, 48)
            with dve.Fori(0, DEPTH) as l:
                own = Chain(dve, dve_own, l)
                link = own.link
                TT, TS, STT = V.tensor_tensor, V.tensor_scalar, V.scalar_tensor_tensor

                dve.wait_ge(vec_in.sem, vec_in.at(l, 16))
                dve.wait_ge(ada_used.sem, ada_used.at(l, 12))
                link(TT(mod[:, :, :], ps[:, 7, 0:96].rearrange("p (j s) -> p j s", s=2), spread(vecs[:, V_BADA:V_BADA + 48], 2), ALU.add))
                for w, vn in ((0, V_N1), (1, V_N2)):
                    scale = mod[:, 8 + 24 * w:16 + 24 * w, :]
                    link(STT(gain[:, w], scale, 1.0, spread(vecs[:, vn:vn + KC], 2), ALU.add, ALU.mult))

                def root(sums, n, width, k):
                    TS(small[:, 0:n], sums, 1.0 / width, EPS, ALU.mult, ALU.add).then_inc(rs_var.sem, 1)
                    dve.wait_ge(rs_root.sem, rs_root.at(l, k))
                    link(V.reciprocal(small[:, 40:40 + n], small[:, 9:9 + n]))

                def diagonals():
                    return TT(diag[:, :, :], ident.unsqueeze(1).to_broadcast([P, TILES, P]), spread(small[:, 40:40 + TILES], P), ALU.mult)

                row = flat[:, 0:TOK]

                def norm(which):
                    dve.wait_ge(sq_used.sem, sq_used.at(l, (which + 1) * KC))
                    root(ps[:, 6, 0:TILES], TILES, D_MODEL, (1, 5)[which])
                    diagonals().then_inc(rs_diag.sem, 1)
                    dve.wait_ge(rs_row.sem, rs_row.at(l, which + 1))

                    def low(c):
                        dve.wait_ge(ahi_ok.sem, ahi_ok.at(l, which * KC + c + 1))
                        TT(a_lo[:, c, :], nt[:, c % 2, :], a_hi[:, c, :].bitcast(F32), ALU.subtract).then_inc(alo_ok.sem, 1)

                    for c in range(KC):
                        if c >= 2:
                            dve.wait_ge(alo_ok.sem, alo_ok.at(l, which * KC + c - 1))
                        link(TT(nt[:, c % 2, :], x[:, c, :], row, ALU.mult))
                        for s, part in ((0, slice(0, SEQ)), (1, slice(SEQ, TOK))):
                            ins = TS(nt[:, c % 2, part], nt[:, c % 2, part], gain[:, which, c, s:s + 1],
                                     mod[:, 24 * which + c, s:s + 1], ALU.mult, ALU.add)
                        ins.then_inc(nh_ok.sem, 1)
                        if c:
                            low(c - 1)
                    low(KC - 1)

                def w_low(n):
                    dve.wait_ge(w_hi_ok.sem, w_hi_ok.at(l, n + 1))
                    TT(w_lo[:, n % 2, :], w_raw[:, n % 2, :], w_hi[:, n % 2, :].bitcast(F32), ALU.subtract).then_inc(w_lo_ok.sem, 1)

                norm(0)
                dve.wait_ge(alo_ok.sem, alo_ok.at(l, KC))
                link(V.memset(u[:, :, :], 0.0))
                w_low(0)
                w_low(1)
                for n in range(16):
                    if n in (1, 3):
                        dve.wait_ge(w_used.sem, w_used.at(l, n + 1))
                        dve.wait_ge(z_free_a.sem, z_free_a.at(l, n // 2 + 1))
                        c, b0 = n // 2, 3
                        TT(u[:, c, CONV_PAD:CONV_PAD + SEQ], ps[:, b0, 0:SEQ], sigb[:, 0:SEQ], ALU.mult)
                        at0 = SEG + CONV_PAD
                        TT(u[:, c, at0:at0 + BLK - SEQ], ps[:, b0, SEQ:BLK], sigb[:, SEQ:BLK], ALU.mult)
                        TT(blocks(u[:, c, at0 + BLK - SEQ:at0 + DEC_SEQ]), banks(b0 + 1, 2), blocks(sigb[:, BLK:TOK]),
                           ALU.mult).then_inc(z_free_d.sem, 1)
                    if n + 2 < 16:
                        w_low(n + 2)

                for i, (cs, width, vg) in enumerate((((0, 1), Q_RANK, V_CQG), ((2,), KV_RANK, V_CKVG))):
                    dve.wait_ge(c_sum.sem, c_sum.at(l, i + 1))
                    root(ps[:, 6, 16 * i:16 * i + TILES], TILES, width, 2 + i)
                    diagonals().then_inc(c_diag.sem, 1)
                    dve.wait_ge(c_row.sem, c_row.at(l, i + 1))
                    for c in cs:
                        ins = STT(zc(Z_CQ + c), zc(Z_CQ + c), vecs[:, vg + c - cs[0]:vg + c - cs[0] + 1], row, ALU.mult, ALU.mult)
                    if i:
                        ins.then_inc(cq_ok.sem, 1)

                dve.wait_ge(z_free_d.sem, z_free_d.at(l, 2))
                for k in range(CONV_WIDTH):
                    for c in range(2):
                        tap = vecs[:, V_DW + c * CONV_WIDTH + k:V_DW + c * CONV_WIDTH + k + 1]
                        if k == 0:
                            own.inc(TS(yc[:, c, 0:Y_LEN], u[:, c, 0:Y_LEN], tap, vecs[:, V_DWB + c:V_DWB + c + 1], ALU.mult, ALU.add))
                        elif k < CONV_WIDTH - 1:
                            own.settle(1)
                            own.inc(STT(yc[:, c, 0:Y_LEN], u[:, c, k:k + Y_LEN], tap, yc[:, c, 0:Y_LEN], ALU.mult, ALU.add))
                        else:
                            own.settle()
                            STT(csq[:, c, 0:SEQ], u[:, c, k:k + SEQ], tap, yc[:, c, 0:SEQ], ALU.mult, ALU.add)
                            ins = STT(csq[:, c, SEQ:TOK], u[:, c, SEG + k:SEG + k + DEC_SEQ], tap, yc[:, c, SEG:SEG + DEC_SEQ],
                                      ALU.mult, ALU.add)
                ins.then_inc(cv_y.sem, 1)
                dve.wait_ge(cv_sum.sem, cv_sum.at(l, 1))
                for c in range(2):
                    ins = STT(blocks(yc[:, c, 0:TOK]), banks(3), -1.0 / CONV_CH, blocks(csq[:, c, :]), ALU.mult, ALU.add)
                ins.then_inc(cv_xc.sem, 1)
                dve.wait_ge(cv_sum.sem, cv_sum.at(l, 2))
                root(ps[:, 6, 32:32 + TILES], TILES, CONV_CH, 4)
                diagonals().then_inc(cv_diag.sem, 1)
                dve.wait_ge(cv_row.sem, cv_row.at(l, 1))
                for c in range(2):
                    ins = TT(yc[:, c, 0:TOK], yc[:, c, 0:TOK], row, ALU.mult)
                ins.then_inc(cv_n.sem, 1)
                for o in range(2):
                    dve.wait_ge(cv_hi.sem, cv_hi.at(l, o + 1))
                    ins = TT(blocks(a_lo[:, 2 + o, :]), banks(3 * o), blocks(a_hi[:, 2 + o, :].bitcast(F32)), ALU.subtract)
                ins.then_inc(cv_done.sem, 1)

                dve.wait_ge(cv_done.sem, cv_done.at(l, 1))
                dve.wait_ge(ml_in.sem, ml_in.at(l, 48))
                dve.wait_ge(ml_ln.sem, ml_ln.at(l, 1))
                V.memset(cst_st[:, 0], 0.0)
                V.memset(vaug[:, :, :, DH:DH + 1], 1.0)
                V.memset(mrow[:, 0:2, :], 0.0)
                V.memset(rr[:, :], 0.0).then_inc(ml_zero.sem, 1)
                link(TS(ra[0:DH, :], zc(Z_MISC)[DH:P, :], vecs[DH:P, V_BG:V_BG + 1], 0.0, ALU.add, ALU.min))
                link(TT(lf[:, :], ra[0:DH, :], lf[:, :], ALU.subtract))
                for r0, back in ((0, False), (32, True)):
                    rows = slice(r0, r0 + HEADS_M)

                    def way(ap):
                        return ap[:, ::-1] if back else ap

                    V.tensor_tensor_scan(way(ra[rows, :]), way(reset[rows, :]), way(lf[rows, :]), 0.0, ALU.mult, ALU.add)
                    V.tensor_tensor_scan(way(rr[rows, 0:SEQ]), way(lf[rows, 0:SEQ]), way(rb[rows, 0:SEQ]), 0.0, ALU.add, ALU.max)
                    ins = V.tensor_tensor_scan(way(rr[rows, SEQ:TOK]), way(lf[rows, SEQ:TOK]), way(rb[rows, SEQ:TOK]),
                                               vecs[rows, V_M0:V_M0 + 1], ALU.add, ALU.max)
                link(ins)

                def tiled(ap):
                    return ap.rearrange("p (t n) -> p t n", n=P)

                fw, bw = slice(0, HEADS_M), slice(32, 32 + HEADS_M)
                V.tensor_copy(rb[DH:P, :], rr[:, :])
                V.tensor_copy(mrow[fw, 0, 1:2], vecs[fw, V_M0:V_M0 + 1])
                V.tensor_copy(mrow[bw, 0, TILES - 1:TILES], vecs[bw, V_M0:V_M0 + 1])
                V.tensor_copy(mrow[fw, 0, 2:TILES], tiled(rr[fw, :])[:, 1:TILES - 1, P - 1])
                link(V.tensor_copy(mrow[bw, 0, 1:TILES - 1], tiled(rr[bw, :])[:, 2:TILES, 0]))
                link(TT(rr[:, :], ra[0:DH, :], rr[:, :], ALU.subtract))
                V.tensor_copy(mrow[fw, 1, :], tiled(rr[fw, :])[:, :, P - 1])
                V.tensor_copy(mrow[bw, 1, :], tiled(rr[bw, :])[:, :, 0])
                link(TT(ra[0:DH, :], rb[0:DH, :], ra[0:DH, :], ALU.subtract))
                TT(mrow[:, 2, :], mrow[:, 0, :], mrow[:, 1, :], ALU.add)
                TT(tiled(ra[DH:P, :]), tiled(ra[0:DH, :]), spread(mrow[:, 1, :], P), ALU.add)
                TT(tiled(rb[0:DH, :]), tiled(rr[:, :]), spread(mrow[:, 0, :], P), ALU.add).then_inc(ml_rows.sem, 1)
                dve.wait_ge(ml_tr.sem, ml_tr.at(l, 2))
                V.tensor_copy(dcol[:, :, :], ps[:, 7, 0:4 * TILES].rearrange("p (j t) -> p j t", t=TILES)).then_inc(ml_dcol.sem, 1)
                for t in range(TILES):
                    dve.wait_ge(ml_kvt.sem, ml_kvt.at(l, t + 1))
                    V.tensor_copy(vaug[:, t, :, 0:DH], ps[:, 2 + t % 2, 0:2 * P].rearrange("p (h d) -> p h d", h=HEADS_M)) \
                        .then_inc(ml_kv_v.sem, 1)
                dve.wait_ge(ml_dcol.sem, ml_dcol.at(l, 1))
                dve.wait_ge(ml_cols.sem, ml_cols.at(l, 1))
                for i in range(TILES):
                    tiles = (i, (TILES - i) % TILES)
                    for d in range(2):
                        dve.wait_ge(ml_bc.sem, ml_bc.at(l, 2 * i + d + 1))
                        TT(em[:, d], ps[:, d, :].rearrange("p (h n) -> p h n", h=HEADS_M),
                           mc[:, M_MASK + d * P:M_MASK + (d + 1) * P].unsqueeze(1).to_broadcast([P, HEADS_M, P]),
                           ALU.add).then_inc(ml_em.sem, 1)
                    for d in range(2):
                        dve.wait_ge(ml_exp.sem, ml_exp.at(l, 2 * i + d + 1))
                        dve.wait_ge(ml_qk.sem, ml_qk.at(l, i + 1))
                        if i:
                            dve.wait_ge(ml_pv.sem, ml_pv.at(l, 2 * (i - 1) + d + 1))
                        TT(sp_[:, d].rearrange("p (j e) n -> p j e n", e=2),
                           ps[:, 2:4, 2 * P * d:2 * P * (d + 1)].rearrange("p e (j n) -> p j e n", j=2),
                           em[:, d].rearrange("p (j e) n -> p j e n", e=2), ALU.mult).then_inc(ml_s.sem, 1)
                    for d, t in enumerate(tiles):
                        dve.wait_ge(ml_pv.sem, ml_pv.at(l, 2 * i + d + 1))
                        ds = slice(4 * d, 4 * d + 4)
                        link(TT(ni[:, d].rearrange("p (j e) n -> p j e n", e=2),
                                ps[:, 4:6, 130 * d:130 * (d + 1)].rearrange("p e (j n) -> p j e n", j=2),
                                spread(cols[:, 2, t, ds].rearrange("p (j e) -> p j e", e=2), DH + 1), ALU.mult))
                        out = ps[:, 6 + d, 0:260].rearrange("p (h n) -> p h n", n=DH + 1)
                        TT(hnum[:, t, ds, :], out[:, :, 0:DH], ni[:, d, :, 0:DH], ALU.add)
                        TT(den[:, 0, t, ds], out[:, :, DH], ni[:, d, :, DH], ALU.add)
                        st = cst_st[:, min(i, 1), d]
                        for j in range(2):
                            ins = STT(st[:, j, :], st[:, j, :], dcol[:, 2 * d + j, t:t + 1], ps[:, 6 + d, 260 + 65 * j:325 + 65 * j],
                                      ALU.mult, ALU.add)
                        ins.then_inc(ml_out.sem, 1)
                dve.wait_ge(ml_out.sem, ml_out.at(l, 2 * TILES))
                dve.wait_ge(st_out.sem, st_out.at(l, 48))
                link(STT(den[:, 1], den[:, 0], -1.0, den[:, 0], ALU.mult, ALU.max))
                link(TT(den[:, 1], den[:, 1], cols[:, 3], ALU.max))
                link(V.reciprocal(den[:, 2], den[:, 1]))
                hv = hnum[:, :, :, :].rearrange("p t h d -> p (t h) d")
                link(TT(hv, hv, spread(den[:, 2].rearrange("p t h -> p (t h)"), DH), ALU.mult))
                hs = hnum[:, :, 0:4, :].rearrange("p t h d -> p t (h d)")
                TT(hs, hs, hnum[:, :, 4:8, :].rearrange("p t h d -> p t (h d)"), ALU.add).then_inc(ml_hsum.sem, 1)
                dve.wait_ge(ml_hsq.sem, ml_hsq.at(l, 1))
                link(V.tensor_reduce(den[:, 0, :, 0:4], hsq[:, :, :].rearrange("p (t h) d -> p t h d", h=4), AX.X, ALU.add))
                TS(den[:, 1, :, 0:4], den[:, 0, :, 0:4], 1.0 / DH, EPS, ALU.mult, ALU.add).then_inc(ml_var.sem, 1)
                dve.wait_ge(ml_root.sem, ml_root.at(l, 1))
                link(V.reciprocal(den[:, 0, :, 0:4], den[:, 2, :, 0:4]))
                TT(hnum[:, :, 0:4, :], hnum[:, :, 0:4, :], spread(den[:, 0, :, 0:4], DH), ALU.mult).then_inc(ml_h.sem, 1)
                dve.wait_ge(ml_ht.sem, ml_ht.at(l, 1))
                dve.wait_ge(ml_og.sem, ml_og.at(l, 2))
                for c in range(2):
                    if c:
                        own.inc(ins)
                        own.settle()
                    STT(yt[:, :], flat[:, 1536 * c:1536 * c + TOK], vecs[:, V_MNG + c:V_MNG + c + 1], zc(Z_O + c),
                        ALU.mult, ALU.mult).then_inc(ml_y.sem, 1)
                    dve.wait_ge(ml_yhi.sem, ml_yhi.at(l, c + 1))
                    ins = TT(a_lo[:, c, :], yt[:, :], a_hi[:, c, :].bitcast(F32), ALU.subtract)
                ins.then_inc(ml_done.sem, 1)

                dve.wait_ge(ml_done.sem, ml_done.at(l, 1))
                dve.wait_ge(at_in.sem, at_in.at(l, 32))
                V.memset(kh[QK:QK + 1, :].bitcast(F32), 1.0)
                V.memset(kl[QK:QK + 1, :].bitcast(F32), 0.0)
                V.memset(va[:, :, V_DIM:P], 1.0).then_inc(at_k1.sem, 1)
                dve.wait_ge(kr_t.sem, kr_t.at(l, 1))
                V.tensor_copy(krt[:, 0:TILES, :].rearrange("p t (g c) -> p t g c", g=2),
                              row.rearrange("p (t q c) -> p t q c", q=4, c=32)[:, :, 0:2, 4:20]).then_inc(at_krt.sem, 1)
                with dve.Fori(0, H // 2) as i:
                    own.enter(i, 128)
                    for e in range(2):
                        def at_(s, n, k):
                            return s.at(l, (i * 2 + e) * n + k)

                        dve.wait_ge(at_proj.sem, at_(at_proj, 1, 1))
                        kv = flat[:, 1024:1024 + KTILES * P].rearrange("p (t n) -> p t n", n=P)
                        dve.wait_ge(at_krt.sem, at_krt.at(l, 1))
                        V.tensor_copy(kt_[:, :, NOPE:QK], krt[:, :, :])
                        dve.wait_ge(at_tok.sem, at_(at_tok, 1, 1))
                        V.tensor_copy(va[:, :, 0:V_DIM], kv[:, :, NOPE:P]).then_inc(at_ktok.sem, 1)
                        dve.wait_ge(at_sq.sem, at_(at_sq, 1, 1))
                        link(V.tensor_reduce(small[:, 0:19], sq_[:, :, :], AX.X, ALU.add))
                        TS(small[:, 0:19], small[:, 0:19], 1.0 / QK, EPS, ALU.mult, ALU.add).then_inc(at_var.sem, 1)
                        dve.wait_ge(at_root.sem, at_(at_root, 1, 1))
                        link(V.reciprocal(small[:, 40:59], small[:, 20:39]))
                        for ap, r0, g0, tl in ((qt_, 40, V_QN, TILES), (kt_, 49, V_KN, KTILES)):
                            own.inc(TT(ap[:, :, :], ap[:, :, :], spread(small[:, r0:r0 + tl], QK), ALU.mult))
                        for ap, r0, g0, tl in ((qt_, 40, V_QN, TILES), (kt_, 49, V_KN, KTILES)):
                            own.settle(1)
                            own.inc(TT(ap[:, :, :], ap[:, :, :], vecs[:, g0:g0 + QK].unsqueeze(1).to_broadcast([P, tl, QK]), ALU.mult))
                        for ap in (qt_, kt_):
                            own.settle(1 if ap is qt_ else 0)
                            pair = ap[:, 1:TILES, NOPE:QK].rearrange("p t (a b c) -> p t a b c", a=2, b=2)
                            x1, x2 = pair[:, :, :, 0, :], pair[:, :, :, 1, :]
                            tab = cst[:, C_ROPE:C_ROPE + 256].rearrange("p (t w a c) -> p t w a c", w=2, a=2, c=8)
                            cos, sin = tab[:, :, 0], tab[:, :, 1]
                            t4 = [rp[:, j].rearrange("p t (a c) -> p t a c", a=2) for j in range(4)]
                            TT(t4[0], x1, cos, ALU.mult)
                            TT(t4[1], x2, sin, ALU.mult)
                            TT(t4[2], x1, sin, ALU.mult)
                            link(TT(t4[3], x2, cos, ALU.mult))
                            TT(x1, t4[0], t4[1], ALU.subtract)
                            ins = TT(x2, t4[2], t4[3], ALU.add)
                            if ap is qt_:
                                link(ins)
                        ins.then_inc(at_rope.sem, 1)
                        dve.wait_ge(at_hi.sem, at_(at_hi, 1, 1))
                        TT(ql[0:QK, :], flat[0:QK, 0:TOK], qh[0:QK, :].bitcast(F32), ALU.subtract)
                        TT(kl[0:QK, :], flat[0:QK, 1536:1536 + KEYS], kh[0:QK, :].bitcast(F32), ALU.subtract).then_inc(at_lo.sem, 1)
                        for t in range(TILES):
                            dve.wait_ge(at_s.sem, at_(at_s, TILES, t + 1))
                            src = ps[:, 0, 0:SEQ] if t == 0 else banks(3 * (t % 2))
                            V.tensor_reduce(nmx[:, t:t + 1], src, AX.X if t == 0 else AX.XY, ALU.max, negate=True).then_inc(at_mx.sem, 1)
                        dve.wait_ge(at_mhi.sem, at_(at_mhi, 1, 1))
                        TT(ql[QK:QK + 1, :], flat[QK:QK + 1, 0:TOK], qh[QK:QK + 1, :].bitcast(F32), ALU.subtract).then_inc(at_mlo.sem, 1)
                        half = slice(DH * e, DH * e + DH)
                        for o, (q0, n, last) in enumerate(((0, SEQ, 1), (SEQ, 512, 10), (SEQ + 512, 512, 19))):
                            dve.wait_ge(at_pv.sem, at_(at_pv, STEPS, last))
                            bank = 6 + o % 2
                            link(V.reciprocal(rec[0:DH, 0:n], ps[DH:P, bank, 0:n]))
                            if o:
                                dve.wait_ge(at_done.sem, at_(at_done, 3, o))
                            TT(ya[half, 0:n], ps[0:DH, bank, 0:n], rec[0:DH, 0:n], ALU.mult).then_inc(at_y.sem, 1)
                            dve.wait_ge(at_yhi.sem, at_(at_yhi, 3, o + 1))
                            TT(a_lo[half, bass.ds(i + 4, 1), q0:q0 + n], ya[half, 0:n].unsqueeze(1),
                               a_hi[half, bass.ds(i + 4, 1), q0:q0 + n].bitcast(F32), ALU.subtract).then_inc(at_done.sem, 1)
                    own.leave(H // 2)

                dve.wait_ge(x_back.sem, x_back.at(l, 16))
                def residual(dst, bank0, gate, sem):
                    STT(dst[:, 0:SEQ], ps[:, bank0, 0:SEQ], gate[:, 0:1], dst[:, 0:SEQ], ALU.mult, ALU.add)
                    STT(dst[:, SEQ:BLK], ps[:, bank0, SEQ:BLK], gate[:, 1:2], dst[:, SEQ:BLK], ALU.mult, ALU.add)
                    STT(blocks(dst[:, BLK:TOK]), banks(bank0 + 1, 2), gate[:, 1:2], blocks(dst[:, BLK:TOK]),
                        ALU.mult, ALU.add).then_inc(sem, 1)

                w_low(16)
                w_low(17)
                for n in range(16, 24):
                    dve.wait_ge(w_used.sem, w_used.at(l, n + 1))
                    residual(x[:, n - 16, :], 3 * (n % 2), mod[:, 16 + n - 16, :], z_free_d.sem)
                    if n + 2 < 24:
                        w_low(n + 2)
                dve.wait_ge(z_free_d.sem, z_free_d.at(l, 10))
                norm(1)

                def f_low(slot, count, dst, hi):
                    dve.wait_ge(f_hi_ok.sem, f_hi_ok.at(l, count))
                    TT(dst, f_raw[:, slot], hi.bitcast(F32), ALU.subtract).then_inc(f_lo_ok.sem, 1)

                def product(v, g):
                    f, b = v // NB, slice((v % NB) * BLK, (v % NB + 1) * BLK)
                    dve.wait_ge(f_silu.sem, f_silu.at(l, g * 6 + (v + 1)))
                    link(TT(at[:, v % 2, :], ps[:, 2 * (v % 2) + 1, 0:BLK], sg[:, v % 2, :], ALU.mult))
                    link(V.tensor_copy(g_hi[:, f, b], at[:, v % 2, :]))
                    TT(g_lo[:, f, b], at[:, v % 2, :], g_hi[:, f, b].bitcast(F32), ALU.subtract).then_inc(f_act.sem, 1)

                def fold(g):
                    for o in range(KC):
                        gate = mod[:, 40 + o, :]
                        for b in range(NB):
                            n = o * NB + b
                            dve.wait_ge(f_dn.sem, f_dn.at(l, g * 24 + (n + 1)))
                            bank = 4 + n % 4
                            if b == 0:
                                STT(x[:, o, 0:SEQ], ps[:, bank, 0:SEQ], gate[:, 0:1], x[:, o, 0:SEQ], ALU.mult, ALU.add)
                                ins = STT(x[:, o, SEQ:BLK], ps[:, bank, SEQ:BLK], gate[:, 1:2], x[:, o, SEQ:BLK], ALU.mult, ALU.add)
                            else:
                                bs = slice(b * BLK, (b + 1) * BLK)
                                ins = STT(x[:, o, bs], ps[:, bank, 0:BLK], gate[:, 1:2], x[:, o, bs], ALU.mult, ALU.add)
                            ins.then_inc(f_res.sem, 1)

                dve.wait_ge(alo_ok.sem, alo_ok.at(l, 2 * KC))
                for n in range(4):
                    f_low(n % 2, n + 1, gu_lo[:, n // 2, n % 2].rearrange("p k n -> p (k n)"), gu_hi[:, n // 2, n % 2].rearrange("p k n -> p (k n)"))
                product(0, 0)
                with dve.Fori(0, NG - 1) as g:
                    own.enter(g, 16)
                    for n in range(2):
                        f_low(n, 4 + g * 6 + n + 1, d_lo[:, n], d_hi[:, n])
                    product(1, g)
                    product(2, g)
                    for n in range(2):
                        f_low(n, 6 + g * 6 + n + 1, gu_lo[:, 0, n].rearrange("p k n -> p (k n)"), gu_hi[:, 0, n].rearrange("p k n -> p (k n)"))
                    for v in range(3, 6):
                        product(v, g)
                    for n in range(2):
                        f_low(n, 8 + g * 6 + n + 1, gu_lo[:, 1, n].rearrange("p k n -> p (k n)"), gu_hi[:, 1, n].rearrange("p k n -> p (k n)"))
                    fold(g)
                    product(0, g + 1)
                    own.leave(NG - 1)
                for n in range(2):
                    f_low(n, 4 + (NG - 1) * 6 + n + 1, d_lo[:, n], d_hi[:, n])
                for v in range(1, 6):
                    product(v, NG - 1)
                fold(NG - 1)
                dve.wait_ge(f_res.sem, f_res.at(l + 1, 0))
                own.end_layer()

        @block.gpsimd
        def _(pool):
            with pool.Fori(0, DEPTH) as l:
                pool.wait_ge(ml_cols.sem, ml_cols.at(l, 1))
                pool.wait_ge(ml_kv_a.sem, ml_kv_a.at(l, TILES))
                for i in range(TILES):
                    for d, t in enumerate((i, (TILES - i) % TILES)):
                        if i:
                            pool.wait_ge(ml_pv.sem, ml_pv.at(l, 2 * (i - 1) + d + 1))
                        nc.gpsimd.tensor_tensor(kw[:, d], kt[:, t, :].rearrange("p (h d) -> p h d", h=HEADS_M),
                                                spread(cols[:, 1, t, 4 * d:4 * d + 4], DH), ALU.mult).then_inc(ml_kw.sem, 1)


def constants():
    cst = np.zeros((P, NCONST), np.float32)
    cst[:, C_ID:C_ID + P] = np.eye(P)
    cst[:, C_ONE:C_ONE + P] = 1.0
    quarter = ROPE // 4
    freqs = np.float32(ROPE_BASE) ** (-np.arange(quarter, dtype=np.float32) / np.float32(quarter))
    t = np.arange(DEC_SEQ)
    ang = np.stack([(t // GRID_W).astype(np.float32)[:, None] * freqs, (t % GRID_W).astype(np.float32)[:, None] * freqs], 1)
    tab = np.stack([np.cos(ang), np.sin(ang)], 1).reshape(8, P, 32).transpose(1, 0, 2)
    cst[:, C_ROPE:C_ROPE + 256] = tab.reshape(P, 256)
    mc = np.zeros((P, NMC), np.float32)
    s, q = np.arange(P)[:, None], np.arange(P)[None, :]
    mc[:, M_MASK:M_MASK + P] = np.where(s <= q, 0.0, NEG)
    mc[:, M_MASK + P:M_MASK + 2 * P] = np.where(s >= q, 0.0, NEG)
    for d in range(2):
        for h in range(HEADS_M):
            at = M_SEL + (4 * d + h) * P
            mc[32 * d + h, at:at + P] = 1.0
            at = M_PAIR + (2 * d + h // 2) * P + DH * (h % 2)
            mc[32 * d + h, at:at + DH] = 1.0
    reset = np.ones((DH, TILES, P), np.float32)
    reset[0:32, :, 0] = 0.0
    reset[32:64, :, P - 1] = 0.0
    mc[0:DH, M_RESET:NMC] = reset.reshape(DH, TOK)
    return cst, mc


def kernel(**inputs):
    import concourse.bacc as bacc
    from concourse.bass_utils import run_bass_kernel_spmd as run

    g = {k: np.asarray(v) for k, v in inputs.items()}
    f32 = np.float32
    L = DEPTH

    def fm(a):
        return a.T.reshape(-1, P, a.shape[0]).transpose(1, 0, 2)

    arr = {}
    arr["xin"] = fm(np.concatenate([g["x_prompt"][0], g["x_sample"][0]], 0))
    arr["cvec"] = np.stack([g["c_ctx"], g["c"][0]], 1).reshape(KC, P, 2).transpose(1, 0, 2)
    vec = np.zeros((L, P, NVEC), f32)

    def put(at, a):
        a = a.reshape(L, -1, P).transpose(0, 2, 1)
        vec[:, :, at:at + a.shape[2]] = a

    put(V_BADA, g["b_ada"]); put(V_N1, g["norm1_g"]); put(V_N2, g["norm2_g"]); put(V_MNG, g["mlstm_norm_g"])
    put(V_DWB, g["conv_dw_b"]); put(V_LNG, g["conv_ln_g"]); put(V_LNB, g["conv_ln_b"])
    put(V_CQG, g["mla_cq_g"]); put(V_CKVG, g["mla_ckv_g"])
    vec[:, :, V_DW:V_DW + 2 * CONV_WIDTH] = g["conv_dw_w"].reshape(L, CONV_WIDTH, 2, P).transpose(0, 3, 2, 1).reshape(L, P, -1)
    gates = {0: 0, 64: 4, 32: 8, 96: 12}
    for part, col in gates.items():
        vec[:, part:part + 4, V_BG] = g["b_gates"][:, col:col + 4]
    for d in range(2):
        vec[:, 32 * d:32 * d + 4, V_M0] = g["state_m"][0, :, d, :]
    vec[:, :, V_QN:V_QN + QK] = g["mla_qn_g"][:, None, :]
    vec[:, :, V_KN:V_KN + QK] = g["mla_kn_g"][:, None, :]
    arr["vec"] = vec
    arr["const"], arr["mconst"] = constants()

    def tiles(w):
        n = w.shape[2] // P
        return w.reshape(L, -1, P, n, P).transpose(0, 3, 2, 1, 4)

    wa = tiles(g["w_ada"])
    arr["wada"] = wa.reshape(L, 12, 4, P, KC, P).transpose(0, 1, 3, 2, 4, 5)
    w = g["w_in"]
    misc = np.zeros((L, D_MODEL, P), f32)
    for part, col in gates.items():
        misc[:, :, part:part + 4] = w[:, :, 1024 + col:1028 + col]
    misc[:, :, 4:20], misc[:, :, 36:52] = w[:, :, 1936:1952], w[:, :, 1952:1968]
    conv = w[:, :, 1040:1552]
    cols = [conv[:, :, 256:384], conv[:, :, 0:128], conv[:, :, 384:512], conv[:, :, 128:256],
            w[:, :, 0:1024], w[:, :, 1552:1936], misc]
    arr["win"] = tiles(np.concatenate(cols, 2)).reshape(L, 16, P, KC * P)
    arr["wout"] = tiles(g["w_out"]).reshape(L, KC, P, KC * P)
    gu = tiles(g["ffn_w_gu"])
    arr["wgu"] = np.stack([gu[:, 0:FC], gu[:, FC:]], 3).reshape(L, FC, P, 2, KC * P)
    arr["wdn"] = g["ffn_w_down"].reshape(L, FC, P, D_MODEL)
    arr["pww"] = g["conv_pw_w"].reshape(L, 2, P, 2, P).transpose(0, 2, 1, 3, 4)
    wq = g["mla_w_uq"].reshape(L, 2, P, HEADS_A, QK).transpose(0, 3, 2, 1, 4).reshape(L, HEADS_A, P, 2 * QK)
    wkv = g["mla_w_ukv"].reshape(L, P, HEADS_A, P).transpose(0, 2, 1, 3)
    arr["whd"] = np.concatenate([wq, wkv], 3)
    arr["ctx_ckv"] = g["cache_ckv"][0].transpose(0, 2, 1)
    arr["ctx_kr"] = g["cache_krope"][0]
    cn = np.concatenate([g["state_C"][0], g["state_n"][0][..., None]], -1)
    arr["c0"] = cn.reshape(L, 2, 2, 2, DH, DH + 1).transpose(0, 3, 4, 1, 2, 5).reshape(L, P, 2, 2, DH + 1)
    arr = {k: np.ascontiguousarray(v) for k, v in arr.items()}

    outs = {"yout": (P, KC, TOK), "o_ckv": (L, P, SEQ), "o_kr": (L, 2, 16, SEQ), "o_c": (L, P, 2, 2, DH + 1), "o_m": (L, 2, 4, 1)}
    nc = bacc.Bacc("TRN2", target_bir_lowering=False, num_devices=1)
    aps = [nc.dram_tensor(k, v.shape, F32, kind="ExternalInput").ap() for k, v in arr.items()]
    aps += [nc.dram_tensor(k, s, F32, kind="ExternalOutput").ap() for k, s in outs.items()]
    aps.append(nc.dram_tensor("spill", (P, KC, TOK), F32, kind="Internal").ap())
    build(nc, *aps)
    r = run(nc, [arr], core_ids=[0]).results[0]

    y = r["yout"].transpose(2, 1, 0).reshape(TOK, D_MODEL)
    ckv = r["o_ckv"].transpose(0, 2, 1)[None]
    kr = r["o_kr"].reshape(L, ROPE, SEQ).transpose(0, 2, 1)[None]
    cn = r["o_c"].reshape(L, 2, DH, 2, 2, DH + 1).transpose(0, 3, 4, 1, 2, 5).reshape(L, 2, HEADS_M, DH, DH + 1)
    return tuple(np.ascontiguousarray(v) for v in (
        y[None, :SEQ], y[None, SEQ:], ckv, kr, cn[None, ..., :DH], cn[None, ..., DH], r["o_m"].reshape(1, L, 2, HEADS_M)))
```

```python
from contextlib import ExitStack

import concourse.bass as bass
import numpy as np
from concourse import mybir

F32 = mybir.dt.float32
F32R = mybir.dt.float32r
ACT = mybir.ActivationFunctionType
ALU = mybir.AluOpType
AX = mybir.AxisListType

P = 128
D_MODEL = 1024
SEQ = 128
DEC_SEQ = 1024
PAST = 128
DEPTH = 2
GRID_W = 64
HEADS_M = 4
DH = 64
CONV_CH = 256
CONV_WIDTH = 31
CONV_PAD = CONV_WIDTH // 2
HEADS_A = 8
NOPE = 64
ROPE = 32
QK = NOPE + ROPE
V_DIM = 64
Q_RANK = 256
KV_RANK = 128
ROPE_BASE = 10000.0
D_FF = 2816
EPS = 1e-6
NEG = -1e30

TOK = SEQ + DEC_SEQ
TILES = TOK // P
KC = D_MODEL // P
BLK = 384
NB = TOK // BLK
FC = D_FF // P
KEYS = TOK + PAST
KTILES = KEYS // P
SEG = P + 2 * CONV_PAD
U_LEN = SEG + DEC_SEQ + 2 * CONV_PAD
Y_LEN = U_LEN - 2 * CONV_PAD
SCALE_A = float(QK) ** -0.5
SCALE_M = float(DH) ** -0.5

V_BADA, V_N1, V_N2, V_MNG, V_DWB, V_LNG, V_LNB, V_CQG, V_CKVG, V_DW = 0, 48, 56, 64, 66, 68, 70, 72, 74, 75
V_M0 = V_DW + 2 * CONV_WIDTH
V_BG = V_M0 + 1
V_QN = V_BG + 1
V_KN = V_QN + QK
V_QC = V_KN + QK
V_KC = V_QC + 1
NVEC = V_KC + 1
C_ID, C_ONE, C_EPS, C_ROPE = 0, P, 2 * P, 2 * P + 1
NCONST = C_ROPE + 2 * KTILES * ROPE
M_MASK, M_SEL, M_PAIR, M_RESET = 0, 2 * P, 2 * P + 8 * P, 2 * P + 12 * P
NMC = M_RESET + TOK
Z_Q, Z_K, Z_V, Z_O, Z_CQ, Z_CKV, Z_MISC = 0, 2, 4, 6, 8, 10, 11
NZ = 12
STRIDE = 4096


class Chain:

    def __init__(self, eng, sem, layer):
        self.eng, self.sem, self.base, self.n = eng, sem, layer * STRIDE, 0

    def inc(self, ins):
        self.n += 1
        ins.then_inc(self.sem, 1)

    def settle(self, back=0):
        self.eng.wait_ge(self.sem, self.base + (self.n - back))

    def link(self, ins):
        self.inc(ins)
        self.settle()

    def enter(self, i, size):
        self.outer, self.size = (self.base, self.n), size
        self.base, self.n = self.base + self.n + i * size, 0

    def leave(self, count):
        self.settle()
        if self.size > self.n:
            self.eng.sem_inc(self.sem, self.size - self.n)
        self.base, self.n = self.outer[0], self.outer[1] + count * self.size

    def end_layer(self):
        self.settle()
        assert self.n <= STRIDE, self.n
        if STRIDE > self.n:
            self.eng.sem_inc(self.sem, STRIDE - self.n)


class Signal:

    def __init__(self, sem, per_layer, first=0):
        self.sem, self.per, self.first = sem, per_layer, first

    def at(self, layer, k):
        return layer * self.per + (k + self.first)


def build(nc, xin, cvec, vec, const, mconst, wada, win, wout, wgu, wdn, pww, whd, ctx_ckv, ctx_kr,
          c0, yout, o_ckv, o_kr, o_c, o_m, spill):
    ctx = ExitStack()
    with ctx:
        def sb(name, shape, dt=F32, where=ctx):
            return where.enter_context(nc.sbuf_tensor(name, shape, dt))

        cst = sb("cst", [P, C_ROPE])
        ident, ones, eps = cst[:, C_ID:C_ID + P], cst[:, C_ONE:C_ONE + P], cst[:, C_EPS:C_EPS + 1]
        vecs = sb("vecs", [P, NVEC])
        cond = sb("cond", [P, KC, 2])
        mod = sb("mod", [P, 48, 2])
        gain = sb("gain", [P, 2, KC, 2])
        small = sb("small", [P, 64])
        diag = sb("diag", [P, TILES, P])

        hx = ExitStack()
        sb("hnum_at", [P, 4, TOK], F32, hx)
        hnum = sb("hnum", [P, TILES, 8, DH], F32, hx)
        hx.close()
        a_hi = sb("a_hi", [P, KC, TOK], F32R)
        a_lo = sb("a_lo", [P, KC, TOK], F32R)
        zx = ExitStack()

        def operands(e, where):
            return (sb(f"qh{e}", [P, TOK], F32R, where), sb(f"ql{e}", [P, TOK], F32R, where),
                    sb(f"kh{e}", [P, KEYS], F32R, where), sb(f"kl{e}", [P, KEYS], F32R, where),
                    sb(f"va{e}", [P, KTILES, P], F32, where))

        ops0 = operands(0, zx)
        rope_in = sb("rope_in", [P, 2, KTILES, ROPE], F32, zx)
        zx.close()
        z = sb("z", [P, 8, TOK])
        x = z
        rest = ExitStack()
        z2 = sb("z2", [P, 4, TOK], F32, rest)

        def zc(c):
            return z[:, c, :] if c < 8 else z2[:, c - 8, :]

        s0 = ExitStack()
        wada_sb = sb("wada_sb", [P, 2, 4, KC, P], F32, s0)
        s0.close()
        s1 = ExitStack()
        nsq = sb("nsq", [P, 2, TOK], F32, s1)
        nt = sb("nt", [P, 2, TOK], F32, s1)
        s1.close()
        s2 = ExitStack()
        w_raw = sb("w_raw", [P, 2, KC * P], F32, s2)
        w_hi = sb("w_hi", [P, 2, KC * P], F32R, s2)
        w_lo = sb("w_lo", [P, 2, KC * P], F32R, s2)
        u = sb("u", [P, 2, U_LEN], F32, s2)
        sigb = sb("sigb", [P, TOK], F32, s2)
        yc = sb("yc", [P, 2, U_LEN], F32, s2)
        csq = sb("csq", [P, 2, TOK], F32, s2)
        s2.close()
        s2b = ExitStack()
        pw = sb("pw", [P, 2, 2, P], F32, s2b)
        s2b.close()
        s4 = ExitStack()
        mc = sb("mc", [P, M_RESET], F32, s4)
        reset = sb("reset", [DH, TOK], F32, s4)
        ra = sb("ra", [P, TOK], F32, s4)
        rb = sb("rb", [P, TOK], F32, s4)
        rr = sb("rr", [DH, TOK], F32, s4)
        lf = sb("lf", [DH, TOK], F32, s4)
        kt = sb("kt", [P, TILES, 2 * P], F32, s4)
        vaug = sb("vaug", [P, TILES, HEADS_M, DH + 1], F32, s4)
        em = sb("em", [P, 2, HEADS_M, P], F32, s4)
        sp_ = sb("sp_", [P, 2, HEADS_M, P], F32, s4)
        kw = sb("kw", [P, 2, HEADS_M, DH], F32, s4)
        ni = sb("ni", [P, 2, HEADS_M, DH + 1], F32, s4)
        cols = sb("cols", [P, 4, TILES, 8], F32, s4)
        den = sb("den", [P, 3, TILES, 8], F32, s4)
        mrow = sb("mrow", [DH, 4, TILES], F32, s4)
        dcol = sb("dcol", [P, 4, TILES], F32, s4)
        cst_st = sb("cst_st", [P, 2, 2, 2, DH + 1], F32, s4)
        s4.close()
        s4b = ExitStack()
        sb("s4b_at", [P, M_RESET], F32, s4b)
        hsq = sb("hsq", [P, TILES * HEADS_M, DH], F32, s4b)
        yt = sb("yt", [P, TOK], F32, s4b)
        s4b.close()
        s5 = ExitStack()
        krt = sb("krt", [P, KTILES, ROPE], F32, s5)
        ctxk = sb("ctxk", [P, PAST], F32, s5)
        hw = sb("hw", [P, 2, 320], F32, s5)
        qk = sb("qk", [P, TILES + KTILES, QK], F32, s5)
        sq_ = sb("sq_", [P, TILES + KTILES, QK], F32, s5)
        rope = sb("rope", [P, 2, TILES + KTILES, ROPE], F32, s5)
        vt = sb("vt", [P, KTILES, V_DIM], F32, s5)
        ops1 = operands(1, s5)
        pmx = sb("pmx", [P, TILES, NB], F32, s5)
        nmx = sb("nmx", [P, TILES], F32, s5)
        pt = sb("pt", [P, 3, 512], F32, s5)
        rec = sb("rec", [P, 512], F32, s5)
        ya = sb("ya", [P, 2, 512], F32, s5)
        qh, ql, kh, kl, va = zip(ops0, ops1)
        s5.close()
        rest.close()
        s8 = ExitStack()
        g_hi = sb("g_hi", [P, 2, TOK], F32R, s8)
        g_lo = sb("g_lo", [P, 2, TOK], F32R, s8)
        f_raw = sb("f_raw", [P, 2, KC * P], F32, s8)
        gu_hi = sb("gu_hi", [P, 2, 2, KC, P], F32R, s8)
        gu_lo = sb("gu_lo", [P, 2, 2, KC, P], F32R, s8)
        d_hi = sb("d_hi", [P, 2, D_MODEL], F32R, s8)
        d_lo = sb("d_lo", [P, 2, D_MODEL], F32R, s8)
        sg = sb("sg", [P, 2, BLK], F32, s8)
        at = sb("at", [P, 2, BLK], F32, s8)
        s8.close()

        ps = ctx.enter_context(nc.psum_tensor("ps", [P, 8, 512], F32))
        flat = ps[:, :, :].rearrange("p b n -> p (b n)")

        def banks(b, n=NB):
            return ps[:, b:b + n, 0:BLK]

        def blocks(ap):
            return ap.rearrange("p (b n) -> p b n", n=BLK)

        def spread(ap, n):
            return ap.unsqueeze(len(ap.shape)).to_broadcast([*ap.shape, n])

        def sig(name, per, first=0):
            return Signal(ctx.enter_context(nc.semaphore(name)), per, first)

        NG = FC // 2
        const_in = sig("const_in", 0)
        cond_ok = sig("cond_ok", 0)
        x_in = sig("x_in", 16)
        vec_in = sig("vec_in", 16)
        ada_in = [sig(f"ada_in{i}", 6 * 16) for i in range(2)]
        ada_used = sig("ada_used", 12)
        mod_ok = sig("mod_ok", 1)
        sq_ok = sig("sq_ok", 2 * KC)
        sq_used = sig("sq_used", 2 * KC)
        rs_var = sig("rs_var", 5)
        rs_root = sig("rs_root", 5)
        rs_diag = sig("rs_diag", 2)
        rs_row = sig("rs_row", 2)
        nh_ok = sig("nh_ok", 2 * KC)
        ahi_ok = sig("ahi_ok", 2 * KC)
        alo_ok = sig("alo_ok", 2 * KC)
        spilled = sig("spilled", 32)
        w_in_ = [sig(f"w_in{i}", 12 * 16) for i in range(2)]
        w_hi_ok = sig("w_hi_ok", 24)
        w_lo_ok = sig("w_lo_ok", 24)
        w_used = sig("w_used", 24)
        z_free_a = sig("z_free_a", 14)
        z_free_d = sig("z_free_d", 10)
        sigb_ok = sig("sigb_ok", 2)
        u_zero = sig("u_zero", 1)
        c_sq = sig("c_sq", 3)
        c_sum = sig("c_sum", 2)
        c_diag = sig("c_diag", 2)
        c_row = sig("c_row", 2)
        cq_ok = sig("cq_ok", 1)
        ckv_out = sig("ckv_out", 48)
        pw_in = sig("pw_in", 16)
        cv_y = sig("cv_y", 1)
        cv_sum = sig("cv_sum", 2)
        cv_xc = sig("cv_xc", 1)
        cv_sq = sig("cv_sq", 1)
        cv_diag = sig("cv_diag", 1)
        cv_row = sig("cv_row", 1)
        cv_n = sig("cv_n", 1)
        cv_act = sig("cv_act", 1)
        cv_pw = sig("cv_pw", 1)
        cv_hi = sig("cv_hi", 2)
        cv_done = sig("cv_done", 1)
        ml_in = sig("ml_in", 48)
        ml_gate = sig("ml_gate", 1)
        ml_ln = sig("ml_ln", 1)
        ml_rows = sig("ml_rows", 1)
        ml_dexp = sig("ml_dexp", 1)
        ml_tr = sig("ml_tr", 3)
        ml_cols = sig("ml_cols", 1)
        ml_dcol = sig("ml_dcol", 1)
        ml_kvt = sig("ml_kvt", TILES)
        ml_kv_a = sig("ml_kv_a", TILES)
        ml_kv_v = sig("ml_kv_v", TILES)
        ml_zero = sig("ml_zero", 1)
        ml_bc = sig("ml_bc", 2 * TILES)
        ml_qk = sig("ml_qk", TILES)
        ml_em = sig("ml_em", 2 * TILES)
        ml_exp = sig("ml_exp", 2 * TILES)
        ml_s = sig("ml_s", 2 * TILES)
        ml_kw = sig("ml_kw", 2 * TILES)
        ml_pv = sig("ml_pv", 2 * TILES)
        ml_out = sig("ml_out", 2 * TILES)
        ml_hsum = sig("ml_hsum", 1)
        ml_hsq = sig("ml_hsq", 1)
        ml_var = sig("ml_var", 1)
        ml_root = sig("ml_root", 1)
        ml_h = sig("ml_h", 1)
        ml_og = sig("ml_og", 2)
        ml_ht = sig("ml_ht", 1)
        ml_y = sig("ml_y", 2)
        ml_yhi = sig("ml_yhi", 2)
        ml_done = sig("ml_done", 1)
        st_out = sig("st_out", 48)
        x_back = sig("x_back", 16)
        H = HEADS_A
        STEPS = 19
        UNITS = 1 + (TILES - 1) * NB
        at_in = sig("at_in", 48)
        at_k1 = sig("at_k1", 1)
        at_tab = sig("at_tab", 1)
        at_krt = sig("at_krt", 1)
        kr_t = sig("kr_t", 1)
        hw_in = [sig(f"hw_in{i}", 4 * 16) for i in range(2)]
        at_pq = sig("at_pq", H)
        at_pk = sig("at_pk", H)
        at_tq = sig("at_tq", H)
        at_tk = sig("at_tk", H)
        at_sq = sig("at_sq", H)
        at_sum = sig("at_sum", H)
        at_root = sig("at_root", H)
        at_inv = sig("at_inv", H)
        at_rope = sig("at_rope", H)
        at_trq = sig("at_trq", H)
        at_hq = sig("at_hq", H)
        at_lq = sig("at_lq", H)
        at_trk = sig("at_trk", H)
        at_hk = sig("at_hk", H)
        at_lk = sig("at_lk", H)
        at_va = sig("at_va", H)
        at_s = sig("at_s", UNITS * H)
        at_mx = sig("at_mx", UNITS * H)
        at_nm = sig("at_nm", H)
        at_mrow = sig("at_mrow", H)
        at_mhi = sig("at_mhi", H)
        at_mlo = sig("at_mlo", H)
        at_st = sig("at_st", STEPS * H)
        at_exp = sig("at_exp", STEPS * H)
        at_pv = sig("at_pv", STEPS * H, first=1)
        at_y = sig("at_y", 3 * H, first=2)
        at_yhi = sig("at_yhi", 3 * H)
        at_done = sig("at_done", 3 * H, first=2)
        f_in = [sig(f"f_in{i}", 3 * NG * 16) for i in range(2)]
        f_hi_ok = sig("f_hi_ok", 6 * NG)
        f_lo_ok = sig("f_lo_ok", 6 * NG)
        f_gu = sig("f_gu", 6 * NG)
        f_silu = sig("f_silu", 6 * NG)
        f_act = sig("f_act", 6 * NG, first=1)
        f_dn = sig("f_dn", 24 * NG, first=1)
        f_res = sig("f_res", 24 * NG, first=1)
        y_out = sig("y_out", 0)
        act_own = ctx.enter_context(nc.semaphore("act_own"))
        dve_own = ctx.enter_context(nc.semaphore("dve_own"))
        pool_own = ctx.enter_context(nc.semaphore("pool_own"))

        A = nc.scalar.activation
        V = nc.vector
        MM = nc.tensor.matmul

        FIRST, LATER = range(0, 4), range(4, STEPS)
        S_TRQ, S_TRK, S_PQ, S_PK, S_MAX, S_ROOT, S_ROW = 0, 2, 4, 5, 6, 9, 13
        U_SUM, U_INV = 8, 16
        PARTS = ((0, SEQ), (SEQ, 512), (SEQ + 512, 512))

        def units_beside(s):
            return range(4 * (s - S_MAX), min(4 * (s - S_MAX) + 4, UNITS)) if s >= S_MAX else range(0)

        def at_head(signal, per_head, l, h, k):
            return signal.at(l, h * per_head + k)

        block = ctx.enter_context(nc.Block())

        @block.sync
        def _(sp):
            sp.dma_start(cst[:, :], const[:, 0:C_ROPE]).then_inc(const_in.sem, 16)
            sp.dma_start(cond[:, :, :], cvec).then_inc(const_in.sem, 16)
            sp.dma_start(x[:, :, :], xin).then_inc(const_in.sem, 16)
            with sp.Fori(0, DEPTH) as l:
                sp.wait_ge(f_res.sem, f_res.at(l, 0))
                sp.dma_start(vecs[:, :], vec[bass.ds(l, 1)].rearrange("a p n -> (a p) n")).then_inc(vec_in.sem, 16)
                for p in range(12):
                    if p >= 2:
                        sp.wait_ge(ada_used.sem, ada_used.at(l, p - 1))
                    sp.dma_start(wada_sb[:, p % 2], wada[bass.ds(l, 1), p].rearrange("a p j k n -> (a p) j k n")) \
                        .then_inc(ada_in[p % 2].sem, 16)
                sp.wait_ge(const_in.sem, 48)
                sp.dma_start(spill, x[:, :, :]).then_inc(spilled.sem, 32)
                sp.wait_ge(alo_ok.sem, alo_ok.at(l, KC))
                sp.wait_ge(spilled.sem, spilled.at(l, 32))
                for n in range(16):
                    if n >= 2:
                        sp.wait_ge(w_hi_ok.sem, w_hi_ok.at(l, n - 1))
                        sp.wait_ge(w_lo_ok.sem, w_lo_ok.at(l, n - 1))
                    sp.dma_start(w_raw[:, n % 2], win[bass.ds(l, 1), n].rearrange("a p n -> (a p) n")) \
                        .then_inc(w_in_[n % 2].sem, 16)
                sp.wait_ge(w_used.sem, w_used.at(l, 16))
                sp.dma_start(pw[:, :, :, :], pww[bass.ds(l, 1)].rearrange("a p k o n -> (a p) k o n")).then_inc(pw_in.sem, 16)
                sp.wait_ge(cq_ok.sem, cq_ok.at(l, 1))
                sp.dma_start(o_ckv[bass.ds(l, 1)].rearrange("a p n -> (a p) n"), zc(Z_CKV)[:, 0:SEQ]).then_inc(ckv_out.sem, 16)
                for g in range(2):
                    sp.dma_start(o_kr[bass.ds(l, 1), g].rearrange("a p n -> (a p) n"),
                                 zc(Z_MISC)[4 + 32 * g:20 + 32 * g, 0:SEQ]).then_inc(ckv_out.sem, 16)
                sp.wait_ge(cv_done.sem, cv_done.at(l, 1))
                sp.dma_start(mc[:, :], mconst[:, 0:M_RESET]).then_inc(ml_in.sem, 16)
                sp.dma_start(reset[:, :], mconst[0:DH, M_RESET:NMC]).then_inc(ml_in.sem, 16)
                sp.dma_start(cst_st[:, 1], c0[bass.ds(l, 1)].rearrange("a p d j n -> (a p) d j n")).then_inc(ml_in.sem, 16)
                sp.wait_ge(ml_out.sem, ml_out.at(l, 2))
                sp.dma_start(o_c[bass.ds(l, 1)].rearrange("a p d j n -> (a p) d j n"), cst_st[:, 0]).then_inc(st_out.sem, 16)
                sp.dma_start(o_m[bass.ds(l, 1), 0].rearrange("a p n -> (a p) n"), rb[DH:DH + 4, SEQ - 1:SEQ]).then_inc(st_out.sem, 16)
                sp.dma_start(o_m[bass.ds(l, 1), 1].rearrange("a p n -> (a p) n"), rb[DH + 32:DH + 36, 0:1]).then_inc(st_out.sem, 16)
                sp.wait_ge(ml_done.sem, ml_done.at(l, 1))
                sp.wait_ge(st_out.sem, st_out.at(l, 48))
                sp.dma_start(ctxk[:, :], ctx_ckv[bass.ds(l, 1)].rearrange("a p n -> (a p) n")).then_inc(at_in.sem, 16)
                sp.dma_start(krt[:, TILES, :], ctx_kr[bass.ds(l, 1)].rearrange("a p n -> (a p) n")).then_inc(at_in.sem, 16)
                sp.dma_start(rope_in[:, :, :, :], const[:, C_ROPE:NCONST].rearrange("p (w t n) -> p w t n", w=2, n=ROPE)).then_inc(at_in.sem, 16)
                for h in range(2):
                    sp.dma_start(hw[:, h], whd[bass.ds(l, 1), h].rearrange("a p n -> (a p) n")).then_inc(hw_in[h].sem, 16)
                with sp.Fori(0, H // 2 - 1) as i:
                    for e in range(2):
                        sp.wait_ge(at_pk.sem, at_pk.at(l, i * 2 + (e + 1)))
                        sp.dma_start(hw[:, e], whd[bass.ds(l, 1), bass.ds(i * 2 + (e + 2), 1)]
                                     .rearrange("a b p n -> (a b p) n")).then_inc(hw_in[e].sem, 16)
                sp.wait_ge(at_trk.sem, at_trk.at(l, H))
                sp.wait_ge(at_va.sem, at_va.at(l, H))
                for n in range(16, 24):
                    if n >= 18:
                        sp.wait_ge(w_hi_ok.sem, w_hi_ok.at(l, n - 1))
                        sp.wait_ge(w_lo_ok.sem, w_lo_ok.at(l, n - 1))
                    sp.dma_start(w_raw[:, n % 2], wout[bass.ds(l, 1), n - 16].rearrange("a p n -> (a p) n")) \
                        .then_inc(w_in_[n % 2].sem, 16)
                    if n == 17:
                        sp.wait_ge(at_pv.sem, at_pv.at(l, STEPS * (H - 1)))
                        sp.dma_start(x[:, :, :], spill).then_inc(x_back.sem, 16)
                sp.wait_ge(alo_ok.sem, alo_ok.at(l, 2 * KC))

                def ff(slot, before, src):
                    if before is not None:
                        sp.wait_ge(f_hi_ok.sem, before)
                        sp.wait_ge(f_lo_ok.sem, before)
                    sp.dma_start(f_raw[:, slot], src).then_inc(f_in[slot].sem, 16)

                def gu_src(f, part):
                    return wgu[bass.ds(l, 1), f, :, part].rearrange("a p n -> (a p) n")

                for n in range(4):
                    ff(n % 2, f_hi_ok.at(l, n - 1) if n >= 2 else None, gu_src(n // 2, n % 2))
                with sp.Fori(0, NG - 1) as g:
                    base = f_hi_ok.at(l, g * 6)
                    for n in range(2):
                        ff(n, base + 4 + n - 1, wdn[bass.ds(l, 1), bass.ds(g * 2 + n, 1)].rearrange("a b p n -> (a b p) n"))
                    for n in range(4):
                        ff(n % 2, base + 6 + n - 1,
                           wgu[bass.ds(l, 1), bass.ds(g * 2 + (2 + n // 2), 1), :, n % 2].rearrange("a b p n -> (a b p) n"))
                for n in range(2):
                    ff(n, f_hi_ok.at(l, 6 * (NG - 1) + 4 + n - 1), wdn[bass.ds(l, 1), 2 * (NG - 1) + n].rearrange("a p n -> (a p) n"))
            sp.wait_ge(f_res.sem, f_res.at(DEPTH, 0))
            sp.dma_start(yout, x[:, :, :]).then_inc(y_out.sem, 16)
            sp.wait_ge(y_out.sem, 16)
            sp.wait_ge(ckv_out.sem, ckv_out.at(DEPTH, 0))
            sp.wait_ge(st_out.sem, st_out.at(DEPTH, 0))
            sp.wait_ge(spilled.sem, spilled.at(DEPTH, 0))

        @block.tensor
        def _(pe):
            for s in (f_dn, at_pv):
                pe.sem_inc(s.sem, s.first)
            pe.wait_ge(const_in.sem, 48)
            pe.wait_ge(cond_ok.sem, 1)
            with pe.Fori(0, DEPTH) as l:
                pe.wait_ge(f_res.sem, f_res.at(l, 0))
                for p in range(12):
                    pe.wait_ge(ada_in[p % 2].sem, ada_in[0].at(l, 16 * (p // 2 + 1)))
                    for j in range(4):
                        for k in range(KC):
                            mm = MM(ps[:, 7, (4 * p + j) * 2:(4 * p + j) * 2 + 2], wada_sb[:, p % 2, j, k, :], cond[:, k, :],
                                    start=(k == 0), stop=(k == KC - 1))
                    mm.then_inc(ada_used.sem, 1)

                def norm(which):
                    for c in range(KC):
                        pe.wait_ge(sq_ok.sem, sq_ok.at(l, which * KC + c + 1))
                        for t in range(TILES):
                            mm = MM(ps[:, 6, t:t + 1], nsq[:, c % 2, t * P:(t + 1) * P], ones[:, 0:1],
                                    start=(c == 0 and t == 0), stop=(c == KC - 1), skip_group_check=True)
                        mm.then_inc(sq_used.sem, 1)
                    pe.wait_ge(rs_diag.sem, rs_diag.at(l, which + 1))
                    for t in range(TILES):
                        mm = MM(flat[:, t * P:(t + 1) * P], ones, diag[:, t, :], start=True, stop=True)
                    mm.then_inc(rs_row.sem, 1)

                def chunk3(n):
                    pe.wait_ge(w_lo_ok.sem, w_lo_ok.at(l, n + 1))
                    if n in (3, 5):
                        pe.wait_ge(z_free_d.sem, z_free_d.at(l, n // 2))
                    elif n >= 18:
                        pe.wait_ge(z_free_d.sem, z_free_d.at(l, n - 15))
                    elif n >= 2:
                        pe.wait_ge(z_free_a.sem, z_free_a.at(l, n // 2 if n < 6 else n - 3))
                    for k in range(KC):
                        if n == 16 and k == KC - 1:
                            pe.wait_ge(at_done.sem, at_done.at(l, 3 * H))
                        whi, wlo = w_hi[:, n % 2, k * P:(k + 1) * P], w_lo[:, n % 2, k * P:(k + 1) * P]
                        for w, a, first, last in ((whi, a_hi, True, False), (whi, a_lo, False, False), (wlo, a_hi, False, True)):
                            for b in range(NB):
                                mm = MM(ps[:, 3 * (n % 2) + b, 0:BLK], w, a[:, k, b * BLK:(b + 1) * BLK],
                                        start=(k == 0 and first), stop=(k == KC - 1 and last))
                    mm.then_inc(w_used.sem, 1)

                norm(0)
                pe.wait_ge(alo_ok.sem, alo_ok.at(l, KC))
                for n in range(16):
                    chunk3(n)

                pe.wait_ge(z_free_a.sem, z_free_a.at(l, 14))
                for i, cs in enumerate(((0, 1), (2,))):
                    for c in cs:
                        pe.wait_ge(c_sq.sem, c_sq.at(l, c + 1))
                        for t in range(TILES):
                            sq = csq[:, c % 2, t * P:(t + 1) * P]
                            mm = MM(ps[:, 6, 16 * i + t:16 * i + t + 1], sq, ones[:, 0:1],
                                    start=(c == cs[0] and t == 0), stop=(c == cs[-1]), skip_group_check=True)
                    mm.then_inc(c_sum.sem, 1)
                    pe.wait_ge(c_diag.sem, c_diag.at(l, i + 1))
                    for t in range(TILES):
                        mm = MM(flat[:, t * P:(t + 1) * P], ones, diag[:, t, :], start=True, stop=True)
                    mm.then_inc(c_row.sem, 1)

                pe.wait_ge(cv_y.sem, cv_y.at(l, 1))
                for b in range(NB):
                    for c in range(2):
                        mm = MM(ps[:, 3 + b, 0:BLK], ones, csq[:, c, b * BLK:(b + 1) * BLK], start=(c == 0), stop=(c == 1))
                mm.then_inc(cv_sum.sem, 1)
                pe.wait_ge(cv_sq.sem, cv_sq.at(l, 1))
                for c in range(2):
                    for t in range(TILES):
                        mm = MM(ps[:, 6, 32 + t:33 + t], csq[:, c, t * P:(t + 1) * P], ones[:, 0:1],
                                start=(c == 0 and t == 0), stop=(c == 1), skip_group_check=True)
                mm.then_inc(cv_sum.sem, 1)
                pe.wait_ge(cv_diag.sem, cv_diag.at(l, 1))
                for t in range(TILES):
                    mm = MM(flat[:, t * P:(t + 1) * P], ones, diag[:, t, :], start=True, stop=True)
                mm.then_inc(cv_row.sem, 1)
                pe.wait_ge(cv_act.sem, cv_act.at(l, 1))
                pe.wait_ge(pw_in.sem, pw_in.at(l, 16))
                for o in range(2):
                    for b in range(NB):
                        for c in range(2):
                            mm = MM(ps[:, 3 * o + b, 0:BLK], pw[:, c, o, :], csq[:, c, b * BLK:(b + 1) * BLK],
                                    start=(c == 0), stop=(c == 1))
                mm.then_inc(cv_pw.sem, 1)

                pe.wait_ge(ml_dexp.sem, ml_dexp.at(l, 1))
                pe.wait_ge(cv_done.sem, cv_done.at(l, 1))
                for dj in range(4):
                    mm = MM(ps[:, 7, dj * TILES:(dj + 1) * TILES], mc[0:DH, M_PAIR + dj * P:M_PAIR + (dj + 1) * P],
                            mrow[:, 3, :], start=True, stop=True)
                mm.then_inc(ml_tr.sem, 1)
                for t in range(TILES):
                    mm = nc.tensor.transpose(flat[:, t * P:(t + 1) * P], ra[:, t * P:(t + 1) * P], ident)
                mm.then_inc(ml_tr.sem, 1)
                for t in range(TILES):
                    mm = nc.tensor.transpose(flat[:, 1536 + t * P:1536 + (t + 1) * P], rb[:, t * P:(t + 1) * P], ident)
                mm.then_inc(ml_tr.sem, 1)
                pe.wait_ge(ml_cols.sem, ml_cols.at(l, 1))
                pe.wait_ge(ml_dcol.sem, ml_dcol.at(l, 1))
                for t in range(TILES):
                    if t >= 2:
                        pe.wait_ge(ml_kv_a.sem, ml_kv_a.at(l, t - 1))
                        pe.wait_ge(ml_kv_v.sem, ml_kv_v.at(l, t - 1))
                    for c in range(4):
                        mm = nc.tensor.transpose(ps[:, t % 2 + 2 * (c // 2), (c % 2) * P:(c % 2 + 1) * P], zc(Z_K + c)[:, t * P:(t + 1) * P], ident)
                    mm.then_inc(ml_kvt.sem, 1)
                pe.wait_ge(ml_kv_v.sem, ml_kv_v.at(l, TILES))
                pe.wait_ge(ml_kv_a.sem, ml_kv_a.at(l, TILES))
                pe.wait_ge(ml_zero.sem, ml_zero.at(l, 1))
                for i in range(TILES):
                    tiles = (i, (TILES - i) % TILES)
                    if i:
                        pe.wait_ge(ml_s.sem, ml_s.at(l, 2 * i))
                    for d, t in enumerate(tiles):
                        ts = slice(t * P, (t + 1) * P)
                        for h in range(HEADS_M):
                            sel = mc[0:DH, M_SEL + (4 * d + h) * P:M_SEL + (4 * d + h + 1) * P]
                            mm = MM(ps[:, d, h * P:(h + 1) * P], sel, rr[:, ts], start=True, stop=True)
                        mm.then_inc(ml_bc.sem, 1)
                    for d, t in enumerate(tiles):
                        ts = slice(t * P, (t + 1) * P)
                        for h in range(HEADS_M):
                            half, at0 = slice(DH * (h % 2), DH * (h % 2) + DH), 2 * P * d + P * (h // 2)
                            mm = MM(ps[:, 2 + h % 2, at0:at0 + P], zc(Z_K + h // 2)[half, ts], zc(Z_Q + h // 2)[half, ts],
                                    start=True, stop=True)
                    mm.then_inc(ml_qk.sem, 1)
                    if i:
                        pe.wait_ge(ml_out.sem, ml_out.at(l, 2 * i))
                    for d, t in enumerate(tiles):
                        for h in range(HEADS_M):
                            half, at0 = slice(DH * (h % 2), DH * (h % 2) + DH), 130 * d + 65 * (h // 2)
                            MM(ps[:, 4 + h % 2, at0:at0 + 65], zc(Z_Q + h // 2)[half, t * P:(t + 1) * P],
                               cst_st[half, min(i, 1), d, h // 2, :], start=True, stop=True)
                    for d, t in enumerate(tiles):
                        pe.wait_ge(ml_kw.sem, ml_kw.at(l, 2 * i + d + 1))
                        for h in range(HEADS_M):
                            half = slice(DH * (h % 2), DH * (h % 2) + DH)
                            MM(ps[half, 6 + d, 260 + 65 * (h // 2):325 + 65 * (h // 2)], kw[:, d, h, :], vaug[:, t, h, :],
                               start=True, stop=True)
                        pe.wait_ge(ml_s.sem, ml_s.at(l, 2 * i + d + 1))
                        for h in range(HEADS_M):
                            mm = MM(ps[:, 6 + d, h * 65:(h + 1) * 65], sp_[:, d, h, :], vaug[:, t, h, :], start=True, stop=True)
                        mm.then_inc(ml_pv.sem, 1)
                pe.wait_ge(ml_h.sem, ml_h.at(l, 1))
                for c in range(2):
                    for t in range(TILES):
                        mm = nc.tensor.transpose(flat[:, 1536 * c + t * P:1536 * c + (t + 1) * P],
                                                 hnum[:, t, 2 * c:2 * c + 2, :].rearrange("p h d -> p (h d)"), ident)
                mm.then_inc(ml_ht.sem, 1)

                pe.wait_ge(ml_done.sem, ml_done.at(l, 1))
                for t in range(TILES):
                    mm = nc.tensor.transpose(flat[:, t * P:(t + 1) * P], zc(Z_MISC)[:, t * P:(t + 1) * P], ident)
                mm.then_inc(kr_t.sem, 1)

                def proj_q(h, e, j):
                    pe.wait_ge(hw_in[e].sem, hw_in[e].at(l, j * 16 + 16))
                    if isinstance(h, int) and h == 0:
                        pe.wait_ge(at_in.sem, at_in.at(l, 48))
                        pe.wait_ge(at_krt.sem, at_krt.at(l, 1))
                    else:
                        pe.wait_ge(at_lk.sem, at_lk.at(l, h))
                    for t in range(TILES):
                        for c in range(2):
                            mm = MM(ps[:, t // 5, (t % 5) * QK:(t % 5 + 1) * QK], zc(Z_CQ + c)[:, t * P:(t + 1) * P],
                                    hw[:, e, c * QK:(c + 1) * QK], start=(c == 0), stop=(c == 1))
                    mm.then_inc(at_pq.sem, 1)

                def proj_k(h, e):
                    pe.wait_ge(at_tq.sem, at_tq.at(l, h + 1))
                    for t in range(KTILES):
                        lat = zc(Z_CKV)[:, t * P:(t + 1) * P] if t < TILES else ctxk[:, :]
                        mm = MM(flat[:, t * P:(t + 1) * P], lat, hw[:, e, 2 * QK:2 * QK + P], start=True, stop=True)
                    mm.then_inc(at_pk.sem, 1)

                def turn_q(h):
                    pe.wait_ge(at_rope.sem, at_rope.at(l, h + 1))
                    for t in range(TILES):
                        mm = nc.tensor.transpose(flat[0:QK, t * P:(t + 1) * P], qk[:, t, :], ident)
                    mm.then_inc(at_trq.sem, 1)

                def turn_k(h):
                    pe.wait_ge(at_lq.sem, at_lq.at(l, h + 1))
                    for t in range(KTILES):
                        mm = nc.tensor.transpose(flat[0:QK, t * P:(t + 1) * P], qk[:, TILES + t, :], ident)
                    mm.then_inc(at_trk.sem, 1)

                def max_unit(h, e, u, more):
                    if u < 3:
                        pe.wait_ge(at_lk.sem, at_lk.at(l, h + 1))
                        if more:
                            pe.wait_ge(at_tk.sem, at_tk.at(l, h + 2))
                    else:
                        pe.wait_ge(at_mx.sem, at_head(at_mx, UNITS, l, h, u - 2))
                    t = (u + NB - 1) // NB
                    keys = slice(0, SEQ) if t == 0 else slice(SEQ + (u - 1) % NB * BLK, SEQ + ((u - 1) % NB + 1) * BLK)
                    MM(ps[:, u % 3, 0:keys.stop - keys.start], qh[e][0:QK, t * P:(t + 1) * P], kh[e][0:QK, keys],
                       start=True, stop=True).then_inc(at_s.sem, 1)

                def max_rows(h):
                    pe.wait_ge(at_nm.sem, at_nm.at(l, h + 1))
                    for t in range(TILES):
                        mm = MM(flat[QK:QK + 1, t * P:(t + 1) * P], nmx[:, t:t + 1], ident, start=True, stop=True)
                    mm.then_inc(at_mrow.sem, 1)

                steps = [(0, 0, SEQ, 0)] + [(1 + qb, *PARTS[1 + qb], kt0) for qb in range(2) for kt0 in range(1, KTILES)]

                def head(h, e, part, i1, i2):
                    def pv(s):
                        o, _, n, kt0 = steps[s]
                        if kt0 <= 1:
                            pe.wait_ge(at_y.sem, at_head(at_y, 3, l, h, o - 1))
                        if s == 0:
                            pe.wait_ge(at_va.sem, at_va.at(l, h + 1))
                        pe.wait_ge(at_exp.sem, at_head(at_exp, STEPS, l, h, s + 1))
                        MM(ps[:, 6 + (e + o) % 2, 0:n], va[e][:, kt0, :], pt[:, s % 3, 0:n], start=(kt0 <= 1),
                           stop=(kt0 == 0 or kt0 == KTILES - 1)).then_inc(at_pv.sem, 1)

                    if part is FIRST:
                        pe.wait_ge(at_mlo.sem, at_mlo.at(l, h + 1))
                        pe.wait_ge(at_mhi.sem, at_mhi.at(l, h + 1))
                    for s in part:
                        o, q0, n, kt0 = steps[s]
                        if s >= 3:
                            pe.wait_ge(at_exp.sem, at_head(at_exp, STEPS, l, h, s - 2))
                        ks, qs = slice(kt0 * P, (kt0 + 1) * P), slice(q0, q0 + n)
                        MM(ps[:, 3 + s % 3, 0:n], kh[e][0:QK + 1, ks], qh[e][0:QK + 1, qs], start=True, stop=False)
                        MM(ps[:, 3 + s % 3, 0:n], kh[e][0:QK + 1, ks], ql[e][0:QK + 1, qs], start=False, stop=False)
                        MM(ps[:, 3 + s % 3, 0:n], kl[e][0:QK + 1, ks], qh[e][0:QK + 1, qs], start=False, stop=True).then_inc(at_st.sem, 1)
                        if i1 and s == S_TRQ:
                            turn_q(h + 1)
                        if i1 and s == S_TRK:
                            turn_k(h + 1)
                        if i2 is not None and s == S_PQ:
                            proj_q(h + 2, e, i2)
                        if i2 is not None and s == S_PK:
                            proj_k(h + 2, e)
                        units = units_beside(s) if i1 else ()
                        for u in units[:len(units) // 2]:
                            max_unit(h + 1, 1 - e, u, i2 is not None)
                        if i1 and s == S_ROW:
                            max_rows(h + 1)
                        if s >= 2:
                            pv(s - 2)
                        for u in units[len(units) // 2:]:
                            max_unit(h + 1, 1 - e, u, i2 is not None)
                    if part is LATER:
                        pv(STEPS - 2)
                        pv(STEPS - 1)

                proj_q(0, 0, 0)
                proj_k(0, 0)
                pe.wait_ge(at_k1.sem, at_k1.at(l, 1))
                turn_q(0)
                turn_k(0)
                proj_q(1, 1, 0)
                proj_k(1, 1)
                for u in range(UNITS):
                    max_unit(0, 0, u, True)
                max_rows(0)
                head(0, 0, FIRST, True, 1)
                with pe.Fori(0, H // 2 - 1) as i:
                    for e in range(2):
                        head(i * 2 + e, e, LATER, True, i + 1)
                        head(i * 2 + (e + 1), 1 - e, FIRST, True, None)
                head(H - 2, 0, LATER, True, None)
                head(H - 1, 1, FIRST, False, None)
                head(H - 1, 1, LATER, False, None)

                for n in range(16, 24):
                    chunk3(n)
                pe.wait_ge(z_free_d.sem, z_free_d.at(l, 10))
                norm(1)
                pe.wait_ge(alo_ok.sem, alo_ok.at(l, 2 * KC))

                def unit(v, g):
                    f, b = v // NB, v % NB
                    pe.wait_ge(f_lo_ok.sem, f_lo_ok.at(l, g * 6 + 2 * (f + 1)))
                    pe.wait_ge(f_hi_ok.sem, f_hi_ok.at(l, g * 6 + 2 * (f + 1)))
                    if v >= 1 or not isinstance(g, int):
                        pe.wait_ge(f_act.sem, f_act.at(l, g * 6 + (v - 1)))
                    for part in range(2):
                        for k in range(KC):
                            whi, wlo = gu_hi[:, f, part, k, :], gu_lo[:, f, part, k, :]
                            for j, (w, a) in enumerate(((whi, a_hi), (whi, a_lo), (wlo, a_hi))):
                                mm = MM(ps[:, 2 * (v % 2) + part, 0:BLK], w, a[:, k, b * BLK:(b + 1) * BLK],
                                        start=(k == 0 and j == 0), stop=(k == KC - 1 and j == 2))
                    mm.then_inc(f_gu.sem, 1)

                def down(g):
                    pe.wait_ge(f_act.sem, f_act.at(l, g * 6 + 6))
                    pe.wait_ge(f_lo_ok.sem, f_lo_ok.at(l, g * 6 + 6))
                    pe.wait_ge(f_hi_ok.sem, f_hi_ok.at(l, g * 6 + 6))
                    for o in range(KC):
                        for b in range(NB):
                            n = o * NB + b
                            pe.wait_ge(f_res.sem, f_res.at(l, g * 24 + max(n - 3, 0)))
                            bs, os_ = slice(b * BLK, (b + 1) * BLK), slice(o * P, (o + 1) * P)
                            for f in range(2):
                                for j, (w, a) in enumerate(((d_hi, g_hi), (d_hi, g_lo), (d_lo, g_hi))):
                                    mm = MM(ps[:, 4 + n % 4, 0:BLK], w[:, f, os_], a[:, f, bs],
                                            start=(f == 0 and j == 0), stop=(f == 1 and j == 2))
                            mm.then_inc(f_dn.sem, 1)

                unit(0, 0)
                with pe.Fori(0, NG - 1) as g:
                    for v in range(1, 6):
                        unit(v, g)
                    unit(0, g + 1)
                    down(g)
                for v in range(1, 6):
                    unit(v, NG - 1)
                down(NG - 1)

        @block.scalar
        def _(act):
            act.wait_ge(const_in.sem, 48)
            A(cond[:, :, :], cond[:, :, :], ACT.Silu).then_inc(cond_ok.sem, 1)
            with act.Fori(0, DEPTH) as l:
                own = Chain(act, act_own, l)

                def root(src, dst, k):
                    act.wait_ge(rs_var.sem, rs_var.at(l, k))
                    A(dst, src, ACT.Sqrt).then_inc(rs_root.sem, 1)

                def norm(which):
                    for c in range(KC):
                        if which:
                            act.wait_ge(z_free_d.sem, z_free_d.at(l, 2 + c + 1))
                        if c >= 2:
                            act.wait_ge(sq_used.sem, sq_used.at(l, which * KC + c - 1))
                        A(nsq[:, c % 2, :], x[:, c, :], ACT.Square).then_inc(sq_ok.sem, 1)
                    root(small[:, 0:TILES], small[:, 9:9 + TILES], (1, 5)[which])
                    for c in range(KC):
                        act.wait_ge(nh_ok.sem, nh_ok.at(l, which * KC + c + 1))
                        A(a_hi[:, c, :], nt[:, c % 2, :], ACT.Copy).then_inc(ahi_ok.sem, 1)

                def w_high(n):
                    act.wait_ge(w_in_[n % 2].sem, w_in_[0].at(l, 16 * (n // 2 + 1)))
                    if n >= 2:
                        act.wait_ge(w_used.sem, w_used.at(l, n - 1))
                    A(w_hi[:, n % 2, :], w_raw[:, n % 2, :], ACT.Copy).then_inc(w_hi_ok.sem, 1)

                act.wait_ge(ada_used.sem, ada_used.at(l, 12))
                norm(0)
                w_high(0)
                w_high(1)
                for n in range(16):
                    src = banks(3 * (n % 2))
                    if n < 4:
                        if n % 2 == 0:
                            act.wait_ge(w_used.sem, w_used.at(l, n + 1))
                            if n:
                                act.wait_ge(z_free_d.sem, z_free_d.at(l, 1))
                            A(blocks(sigb[:, :]), src, ACT.Sigmoid).then_inc(z_free_a.sem, 1)
                    else:
                        act.wait_ge(w_used.sem, w_used.at(l, n + 1))
                        if n == 4:
                            act.wait_ge(spilled.sem, spilled.at(l, 32))
                        A(blocks(zc(n - 4)), src, ACT.Copy, scale=SCALE_M if n - 4 < Z_K else 1.0).then_inc(z_free_a.sem, 1)
                    if n + 2 < 16:
                        w_high(n + 2)

                act.wait_ge(z_free_a.sem, z_free_a.at(l, 14))
                for c in range(3):
                    if c == 2:
                        act.wait_ge(c_sum.sem, c_sum.at(l, 1))
                    A(csq[:, c % 2, :], zc(Z_CQ + c), ACT.Square).then_inc(c_sq.sem, 1)
                    if c:
                        root(small[:, 0:TILES], small[:, 9:9 + TILES], 1 + c)

                act.wait_ge(cv_xc.sem, cv_xc.at(l, 1))
                A(csq[:, :, :], yc[:, :, 0:TOK], ACT.Square).then_inc(cv_sq.sem, 1)
                root(small[:, 0:TILES], small[:, 9:9 + TILES], 4)
                act.wait_ge(cv_n.sem, cv_n.at(l, 1))
                for c in range(2):
                    aa = A(csq[:, c, :], yc[:, c, 0:TOK], ACT.Silu, bias=vecs[:, V_LNB + c:V_LNB + c + 1],
                           scale=vecs[:, V_LNG + c:V_LNG + c + 1])
                aa.then_inc(cv_act.sem, 1)
                act.wait_ge(cv_pw.sem, cv_pw.at(l, 1))
                for o in range(2):
                    A(blocks(a_hi[:, 2 + o, :]), banks(3 * o), ACT.Copy).then_inc(cv_hi.sem, 1)

                act.wait_ge(cv_done.sem, cv_done.at(l, 1))
                misc = zc(Z_MISC)
                bg = vecs[:, V_BG:V_BG + 1]
                A(rb[0:DH, :], misc[0:DH, :], ACT.Identity, bias=bg[0:DH, :])
                own.link(A(ra[0:DH, :], misc[DH:P, :], ACT.Abs, bias=bg[DH:P, :]))
                own.link(A(ra[0:DH, :], ra[0:DH, :], ACT.Exp, scale=-1.0))
                A(lf[:, :], ra[0:DH, :], ACT.Ln, bias=ones[0:DH, 0:1]).then_inc(ml_ln.sem, 1)
                act.wait_ge(ml_rows.sem, ml_rows.at(l, 1))
                A(mrow[:, 3, :], mrow[:, 2, :], ACT.Exp).then_inc(ml_dexp.sem, 1)

                def turned(half, row):
                    return flat[:, 1536 * half:1536 * half + TOK].rearrange("p (t q c) -> p t q c", q=4, c=32)[
                        :, :, 2 * row:2 * row + 2, 0:HEADS_M]

                def by_head(ap):
                    return ap.rearrange("p t (d h) -> p t d h", d=2)

                act.wait_ge(ml_tr.sem, ml_tr.at(l, 3))
                A(by_head(cols[:, 0]), turned(0, 0), ACT.Copy)
                A(by_head(cols[:, 1]), turned(0, 1), ACT.Exp)
                A(by_head(cols[:, 2]), turned(1, 0), ACT.Exp)
                A(by_head(cols[:, 3]), turned(1, 1), ACT.Exp, scale=-1.0).then_inc(ml_cols.sem, 1)
                for t in range(TILES):
                    act.wait_ge(ml_kvt.sem, ml_kvt.at(l, t + 1))
                    A(kt[:, t, :], ps[:, t % 2, 0:2 * P], ACT.Copy).then_inc(ml_kv_a.sem, 1)
                act.wait_ge(ml_cols.sem, ml_cols.at(l, 1))
                for i in range(TILES):
                    for d, t in enumerate((i, (TILES - i) % TILES)):
                        act.wait_ge(ml_em.sem, ml_em.at(l, 2 * i + d + 1))
                        for h in range(HEADS_M):
                            aa = A(em[:, d, h, :], em[:, d, h, :], ACT.Exp, bias=cols[:, 0, t, 4 * d + h:4 * d + h + 1])
                        aa.then_inc(ml_exp.sem, 1)
                for c in range(2):
                    A(zc(Z_O + c), zc(Z_O + c), ACT.Sigmoid).then_inc(ml_og.sem, 1)
                act.wait_ge(ml_hsum.sem, ml_hsum.at(l, 1))
                A(hsq[:, :, :].rearrange("p (t h) d -> p t (h d)", h=4), hnum[:, :, 0:4, :].rearrange("p t h d -> p t (h d)"),
                  ACT.Square).then_inc(ml_hsq.sem, 1)
                act.wait_ge(ml_var.sem, ml_var.at(l, 1))
                A(den[:, 2, :, 0:4], den[:, 1, :, 0:4], ACT.Sqrt).then_inc(ml_root.sem, 1)
                for c in range(2):
                    act.wait_ge(ml_y.sem, ml_y.at(l, c + 1))
                    A(a_hi[:, c, :], yt[:, :], ACT.Copy).then_inc(ml_yhi.sem, 1)

                act.wait_ge(at_krt.sem, at_krt.at(l, 1))

                def first_q(h):
                    act.wait_ge(at_pq.sem, at_pq.at(l, h + 1))
                    A(qk[:, 0:5, :], ps[:, 0, 0:5 * QK].rearrange("p (t n) -> p t n", n=QK), ACT.Copy)
                    A(qk[:, 5:9, :], ps[:, 1, 0:4 * QK].rearrange("p (t n) -> p t n", n=QK), ACT.Copy).then_inc(at_tq.sem, 1)

                def first_k(h):
                    act.wait_ge(at_pk.sem, at_pk.at(l, h + 1))
                    kv = flat[:, 0:KEYS].rearrange("p (t n) -> p t n", n=P)
                    A(qk[:, TILES:, NOPE:QK], krt[:, :, :], ACT.Copy)
                    own.inc(A(qk[:, TILES:, 0:NOPE], kv[:, :, 0:NOPE], ACT.Copy))
                    A(vt[:, :, :], kv[:, :, NOPE:P], ACT.Copy).then_inc(at_tk.sem, 1)
                    own.settle()
                    A(sq_[:, :, :], qk[:, :, :], ACT.Square).then_inc(at_sq.sem, 1)

                def values(h, e):
                    act.wait_ge(at_tk.sem, at_tk.at(l, h + 1))
                    if not isinstance(h, int) or h >= 2:
                        act.wait_ge(at_pv.sem, at_head(at_pv, STEPS, l, h, -STEPS))
                    A(va[e][:, :, 0:V_DIM], vt[:, :, :], ACT.Copy).then_inc(at_va.sem, 1)

                def first_root(h):
                    act.wait_ge(at_sum.sem, at_sum.at(l, h + 1))
                    own.link(A(small[:, 20:39], small[:, 0:19], ACT.Ln))
                    A(small[:, 40:59], small[:, 20:39], ACT.Exp, scale=-0.5).then_inc(at_root.sem, 1)

                def high_q(h, e):
                    act.wait_ge(at_trq.sem, at_trq.at(l, h + 1))
                    A(qh[e][0:QK, :], flat[0:QK, 0:TOK], ACT.Copy, scale=vecs[0:QK, V_QC:V_QC + 1]).then_inc(at_hq.sem, 1)

                def high_k(h, e):
                    act.wait_ge(at_trk.sem, at_trk.at(l, h + 1))
                    A(kh[e][0:QK, :], flat[0:QK, 0:KEYS], ACT.Copy, scale=vecs[0:QK, V_KC:V_KC + 1]).then_inc(at_hk.sem, 1)

                def high_rows(h, e):
                    act.wait_ge(at_mrow.sem, at_mrow.at(l, h + 1))
                    A(qh[e][QK:QK + 1, :], flat[QK:QK + 1, 0:TOK], ACT.Copy).then_inc(at_mhi.sem, 1)

                def yhigh(h, e, i0, o):
                    act.wait_ge(at_y.sem, at_head(at_y, 3, l, h, o + 1))
                    q0, n = PARTS[o]
                    half = slice(DH * e, DH * e + DH)
                    A(a_hi[half, bass.ds(i0 + 4, 1), q0:q0 + n], ya[half, (e + o) % 2, 0:n].unsqueeze(1), ACT.Copy).then_inc(at_yhi.sem, 1)

                def head(h, e, i0, part, i1, i2, before=None):
                    for s in part:
                        n = SEQ if s == 0 else 512
                        act.wait_ge(at_st.sem, at_head(at_st, STEPS, l, h, s + 1))
                        act.wait_ge(at_pv.sem, at_head(at_pv, STEPS, l, h, max(s - 2, 0)))
                        A(pt[:, s % 3, 0:n], ps[:, 3 + s % 3, 0:n], ACT.Exp, scale=SCALE_A).then_inc(at_exp.sem, 1)
                        if i1 and s == S_TRQ:
                            high_q(h + 1, 1 - e)
                            values(h + 1, 1 - e)
                        if before is not None and s == 2:
                            yhigh(h - 1, 1 - e, before, 2)
                        if i1 and s == S_TRK:
                            high_k(h + 1, 1 - e)
                        if i1 and s == S_ROW:
                            high_rows(h + 1, 1 - e)
                        if i2 and s == S_PQ:
                            first_q(h + 2)
                        if i2 and s == S_PK:
                            first_k(h + 2)
                        if i2 and s == S_ROOT:
                            first_root(h + 2)
                        if s == 6:
                            yhigh(h, e, i0, 0)
                        if s == 16:
                            yhigh(h, e, i0, 1)
                        if isinstance(h, int) and h == H - 1 and s in (8, 11):
                            w_high(16 + s // 11)

                first_q(0)
                first_k(0)
                first_root(0)
                act.wait_ge(at_k1.sem, at_k1.at(l, 1))
                values(0, 0)
                high_q(0, 0)
                high_k(0, 0)
                first_q(1)
                first_k(1)
                first_root(1)
                high_rows(0, 0)
                head(0, 0, 0, FIRST, True, True)
                with act.Fori(0, H // 2 - 1) as i:
                    own.enter(i, 16)
                    for e in range(2):
                        head(i * 2 + e, e, i, LATER, True, True)
                        head(i * 2 + (e + 1), 1 - e, i, FIRST, True, True, before=i)
                    own.leave(H // 2 - 1)
                head(H - 2, 0, H // 2 - 1, LATER, True, False)
                head(H - 1, 1, H // 2 - 1, FIRST, False, False, before=H // 2 - 1)
                head(H - 1, 1, H // 2 - 1, LATER, False, False)
                yhigh(H - 1, 1, H // 2 - 1, 2)

                for n in range(18, 24):
                    w_high(n)
                act.wait_ge(w_used.sem, w_used.at(l, 24))
                norm(1)

                def f_high(slot, count, dst, used_sem, used):
                    act.wait_ge(f_in[slot].sem, f_in[0].at(l, count))
                    if used_sem is not None:
                        act.wait_ge(used_sem.sem, used)
                    A(dst, f_raw[:, slot], ACT.Copy).then_inc(f_hi_ok.sem, 1)

                def silu(v, g):
                    act.wait_ge(f_gu.sem, f_gu.at(l, g * 6 + (v + 1)))
                    if v >= 1 or not isinstance(g, int):
                        act.wait_ge(f_act.sem, f_act.at(l, g * 6 + (v - 1)))
                    A(sg[:, v % 2, :], ps[:, 2 * (v % 2), 0:BLK], ACT.Silu).then_inc(f_silu.sem, 1)

                act.wait_ge(alo_ok.sem, alo_ok.at(l, 2 * KC))
                for n in range(4):
                    f_high(n % 2, 16 * (n // 2 + 1), gu_hi[:, n // 2, n % 2], None, None)
                silu(0, 0)
                with act.Fori(0, NG - 1) as g:
                    for n in range(2):
                        f_high(n, 32 + g * 48 + 16, d_hi[:, n], f_dn, f_dn.at(l, g * 24))
                    silu(1, g)
                    silu(2, g)
                    for n in range(2):
                        f_high(n, 32 + g * 48 + 32, gu_hi[:, 0, n], f_gu, f_gu.at(l, g * 6 + 3))
                    for v in range(3, 6):
                        silu(v, g)
                    for n in range(2):
                        f_high(n, 32 + g * 48 + 48, gu_hi[:, 1, n], f_gu, f_gu.at(l, g * 6 + 6))
                    silu(0, g + 1)
                for n in range(2):
                    f_high(n, 32 + (NG - 1) * 48 + 16, d_hi[:, n], f_dn, f_dn.at(l, (NG - 1) * 24))
                for v in range(1, 6):
                    silu(v, NG - 1)
                own.end_layer()

        @block.vector
        def _(dve):
            for s in (f_res, at_y, f_act):
                dve.sem_inc(s.sem, s.first)
            dve.wait_ge(const_in.sem, 48)
            with dve.Fori(0, DEPTH) as l:
                own = Chain(dve, dve_own, l)
                link = own.link
                TT, TS, STT = V.tensor_tensor, V.tensor_scalar, V.scalar_tensor_tensor

                dve.wait_ge(vec_in.sem, vec_in.at(l, 16))
                dve.wait_ge(ada_used.sem, ada_used.at(l, 12))
                link(TT(mod[:, :, :], ps[:, 7, 0:96].rearrange("p (j s) -> p j s", s=2), spread(vecs[:, V_BADA:V_BADA + 48], 2), ALU.add))
                for w, vn in ((0, V_N1), (1, V_N2)):
                    scale = mod[:, 8 + 24 * w:16 + 24 * w, :]
                    link(STT(gain[:, w], scale, 1.0, spread(vecs[:, vn:vn + KC], 2), ALU.add, ALU.mult))

                def root(sums, n, width, k):
                    TS(small[:, 0:n], sums, 1.0 / width, EPS, ALU.mult, ALU.add).then_inc(rs_var.sem, 1)
                    dve.wait_ge(rs_root.sem, rs_root.at(l, k))
                    link(V.reciprocal(small[:, 40:40 + n], small[:, 9:9 + n]))

                def diagonals():
                    return TT(diag[:, :, :], ident.unsqueeze(1).to_broadcast([P, TILES, P]), spread(small[:, 40:40 + TILES], P), ALU.mult)

                row = flat[:, 0:TOK]

                def norm(which):
                    dve.wait_ge(sq_used.sem, sq_used.at(l, (which + 1) * KC))
                    root(ps[:, 6, 0:TILES], TILES, D_MODEL, (1, 5)[which])
                    diagonals().then_inc(rs_diag.sem, 1)
                    dve.wait_ge(rs_row.sem, rs_row.at(l, which + 1))

                    def low(c):
                        dve.wait_ge(ahi_ok.sem, ahi_ok.at(l, which * KC + c + 1))
                        TT(a_lo[:, c, :], nt[:, c % 2, :], a_hi[:, c, :].bitcast(F32), ALU.subtract).then_inc(alo_ok.sem, 1)

                    for c in range(KC):
                        if c >= 2:
                            dve.wait_ge(alo_ok.sem, alo_ok.at(l, which * KC + c - 1))
                        link(TT(nt[:, c % 2, :], x[:, c, :], row, ALU.mult))
                        for s, part in ((0, slice(0, SEQ)), (1, slice(SEQ, TOK))):
                            ins = TS(nt[:, c % 2, part], nt[:, c % 2, part], gain[:, which, c, s:s + 1],
                                     mod[:, 24 * which + c, s:s + 1], ALU.mult, ALU.add)
                        ins.then_inc(nh_ok.sem, 1)
                        if c:
                            low(c - 1)
                    low(KC - 1)

                norm(0)
                dve.wait_ge(alo_ok.sem, alo_ok.at(l, KC))
                link(V.memset(u[:, :, :], 0.0))
                for c in range(2):
                    dve.wait_ge(w_used.sem, w_used.at(l, 2 * c + 2))
                    dve.wait_ge(z_free_a.sem, z_free_a.at(l, c + 1))
                    b0, at0 = 3, SEG + CONV_PAD
                    TT(u[:, c, CONV_PAD:CONV_PAD + SEQ], ps[:, b0, 0:SEQ], sigb[:, 0:SEQ], ALU.mult)
                    TT(u[:, c, at0:at0 + BLK - SEQ], ps[:, b0, SEQ:BLK], sigb[:, SEQ:BLK], ALU.mult)
                    TT(blocks(u[:, c, at0 + BLK - SEQ:at0 + DEC_SEQ]), banks(b0 + 1, 2), blocks(sigb[:, BLK:TOK]),
                       ALU.mult).then_inc(z_free_d.sem, 1)

                for i, (cs, width, vg) in enumerate((((0, 1), Q_RANK, V_CQG), ((2,), KV_RANK, V_CKVG))):
                    dve.wait_ge(c_sum.sem, c_sum.at(l, i + 1))
                    root(ps[:, 6, 16 * i:16 * i + TILES], TILES, width, 2 + i)
                    diagonals().then_inc(c_diag.sem, 1)
                    dve.wait_ge(c_row.sem, c_row.at(l, i + 1))
                    for c in cs:
                        ins = STT(zc(Z_CQ + c), zc(Z_CQ + c), vecs[:, vg + c - cs[0]:vg + c - cs[0] + 1], row, ALU.mult, ALU.mult)
                    if i:
                        ins.then_inc(cq_ok.sem, 1)

                dve.wait_ge(z_free_d.sem, z_free_d.at(l, 2))
                for k in range(CONV_WIDTH):
                    for c in range(2):
                        tap = vecs[:, V_DW + c * CONV_WIDTH + k:V_DW + c * CONV_WIDTH + k + 1]
                        if k == 0:
                            own.inc(TS(yc[:, c, 0:Y_LEN], u[:, c, 0:Y_LEN], tap, vecs[:, V_DWB + c:V_DWB + c + 1], ALU.mult, ALU.add))
                        elif k < CONV_WIDTH - 1:
                            own.settle(1)
                            own.inc(STT(yc[:, c, 0:Y_LEN], u[:, c, k:k + Y_LEN], tap, yc[:, c, 0:Y_LEN], ALU.mult, ALU.add))
                        else:
                            own.settle()
                            STT(csq[:, c, 0:SEQ], u[:, c, k:k + SEQ], tap, yc[:, c, 0:SEQ], ALU.mult, ALU.add)
                            ins = STT(csq[:, c, SEQ:TOK], u[:, c, SEG + k:SEG + k + DEC_SEQ], tap, yc[:, c, SEG:SEG + DEC_SEQ],
                                      ALU.mult, ALU.add)
                ins.then_inc(cv_y.sem, 1)
                dve.wait_ge(cv_sum.sem, cv_sum.at(l, 1))
                for c in range(2):
                    ins = STT(blocks(yc[:, c, 0:TOK]), banks(3), -1.0 / CONV_CH, blocks(csq[:, c, :]), ALU.mult, ALU.add)
                ins.then_inc(cv_xc.sem, 1)
                dve.wait_ge(cv_sum.sem, cv_sum.at(l, 2))
                root(ps[:, 6, 32:32 + TILES], TILES, CONV_CH, 4)
                diagonals().then_inc(cv_diag.sem, 1)
                dve.wait_ge(cv_row.sem, cv_row.at(l, 1))
                for c in range(2):
                    ins = TT(yc[:, c, 0:TOK], yc[:, c, 0:TOK], row, ALU.mult)
                ins.then_inc(cv_n.sem, 1)
                for o in range(2):
                    dve.wait_ge(cv_hi.sem, cv_hi.at(l, o + 1))
                    ins = TT(blocks(a_lo[:, 2 + o, :]), banks(3 * o), blocks(a_hi[:, 2 + o, :].bitcast(F32)), ALU.subtract)
                ins.then_inc(cv_done.sem, 1)

                dve.wait_ge(cv_done.sem, cv_done.at(l, 1))
                dve.wait_ge(ml_in.sem, ml_in.at(l, 48))
                dve.wait_ge(ml_ln.sem, ml_ln.at(l, 1))
                V.memset(cst_st[:, 0], 0.0)
                V.memset(vaug[:, :, :, DH:DH + 1], 1.0)
                V.memset(mrow[:, 0:2, :], 0.0)
                V.memset(rr[:, :], 0.0).then_inc(ml_zero.sem, 1)
                link(TS(ra[0:DH, :], zc(Z_MISC)[DH:P, :], vecs[DH:P, V_BG:V_BG + 1], 0.0, ALU.add, ALU.min))
                link(TT(lf[:, :], ra[0:DH, :], lf[:, :], ALU.subtract))
                for r0, back in ((0, False), (32, True)):
                    rows = slice(r0, r0 + HEADS_M)

                    def way(ap):
                        return ap[:, ::-1] if back else ap

                    V.tensor_tensor_scan(way(ra[rows, :]), way(reset[rows, :]), way(lf[rows, :]), 0.0, ALU.mult, ALU.add)
                    V.tensor_tensor_scan(way(rr[rows, 0:SEQ]), way(lf[rows, 0:SEQ]), way(rb[rows, 0:SEQ]), 0.0, ALU.add, ALU.max)
                    ins = V.tensor_tensor_scan(way(rr[rows, SEQ:TOK]), way(lf[rows, SEQ:TOK]), way(rb[rows, SEQ:TOK]),
                                               vecs[rows, V_M0:V_M0 + 1], ALU.add, ALU.max)
                link(ins)

                def tiled(ap):
                    return ap.rearrange("p (t n) -> p t n", n=P)

                fw, bw = slice(0, HEADS_M), slice(32, 32 + HEADS_M)
                V.tensor_copy(rb[DH:P, :], rr[:, :])
                V.tensor_copy(mrow[fw, 0, 1:2], vecs[fw, V_M0:V_M0 + 1])
                V.tensor_copy(mrow[bw, 0, TILES - 1:TILES], vecs[bw, V_M0:V_M0 + 1])
                V.tensor_copy(mrow[fw, 0, 2:TILES], tiled(rr[fw, :])[:, 1:TILES - 1, P - 1])
                link(V.tensor_copy(mrow[bw, 0, 1:TILES - 1], tiled(rr[bw, :])[:, 2:TILES, 0]))
                link(TT(rr[:, :], ra[0:DH, :], rr[:, :], ALU.subtract))
                V.tensor_copy(mrow[fw, 1, :], tiled(rr[fw, :])[:, :, P - 1])
                V.tensor_copy(mrow[bw, 1, :], tiled(rr[bw, :])[:, :, 0])
                link(TT(ra[0:DH, :], rb[0:DH, :], ra[0:DH, :], ALU.subtract))
                TT(mrow[:, 2, :], mrow[:, 0, :], mrow[:, 1, :], ALU.add)
                TT(tiled(ra[DH:P, :]), tiled(ra[0:DH, :]), spread(mrow[:, 1, :], P), ALU.add)
                TT(tiled(rb[0:DH, :]), tiled(rr[:, :]), spread(mrow[:, 0, :], P), ALU.add).then_inc(ml_rows.sem, 1)
                dve.wait_ge(ml_tr.sem, ml_tr.at(l, 2))
                V.tensor_copy(dcol[:, :, :], ps[:, 7, 0:4 * TILES].rearrange("p (j t) -> p j t", t=TILES)).then_inc(ml_dcol.sem, 1)
                for t in range(TILES):
                    dve.wait_ge(ml_kvt.sem, ml_kvt.at(l, t + 1))
                    V.tensor_copy(vaug[:, t, :, 0:DH], ps[:, 2 + t % 2, 0:2 * P].rearrange("p (h d) -> p h d", h=HEADS_M)) \
                        .then_inc(ml_kv_v.sem, 1)
                dve.wait_ge(ml_dcol.sem, ml_dcol.at(l, 1))
                dve.wait_ge(ml_cols.sem, ml_cols.at(l, 1))
                for i in range(TILES):
                    tiles = (i, (TILES - i) % TILES)
                    for d in range(2):
                        dve.wait_ge(ml_bc.sem, ml_bc.at(l, 2 * i + d + 1))
                        TT(em[:, d], ps[:, d, :].rearrange("p (h n) -> p h n", h=HEADS_M),
                           mc[:, M_MASK + d * P:M_MASK + (d + 1) * P].unsqueeze(1).to_broadcast([P, HEADS_M, P]),
                           ALU.add).then_inc(ml_em.sem, 1)
                    for d in range(2):
                        dve.wait_ge(ml_exp.sem, ml_exp.at(l, 2 * i + d + 1))
                        dve.wait_ge(ml_qk.sem, ml_qk.at(l, i + 1))
                        if i:
                            dve.wait_ge(ml_pv.sem, ml_pv.at(l, 2 * (i - 1) + d + 1))
                        TT(sp_[:, d].rearrange("p (j e) n -> p j e n", e=2),
                           ps[:, 2:4, 2 * P * d:2 * P * (d + 1)].rearrange("p e (j n) -> p j e n", j=2),
                           em[:, d].rearrange("p (j e) n -> p j e n", e=2), ALU.mult).then_inc(ml_s.sem, 1)
                    for d, t in enumerate(tiles):
                        dve.wait_ge(ml_pv.sem, ml_pv.at(l, 2 * i + d + 1))
                        ds = slice(4 * d, 4 * d + 4)
                        link(TT(ni[:, d].rearrange("p (j e) n -> p j e n", e=2),
                                ps[:, 4:6, 130 * d:130 * (d + 1)].rearrange("p e (j n) -> p j e n", j=2),
                                spread(cols[:, 2, t, ds].rearrange("p (j e) -> p j e", e=2), DH + 1), ALU.mult))
                        out = ps[:, 6 + d, 0:260].rearrange("p (h n) -> p h n", n=DH + 1)
                        TT(hnum[:, t, ds, :], out[:, :, 0:DH], ni[:, d, :, 0:DH], ALU.add)
                        TT(den[:, 0, t, ds], out[:, :, DH], ni[:, d, :, DH], ALU.add)
                        st = cst_st[:, min(i, 1), d]
                        for j in range(2):
                            ins = STT(st[:, j, :], st[:, j, :], dcol[:, 2 * d + j, t:t + 1], ps[:, 6 + d, 260 + 65 * j:325 + 65 * j],
                                      ALU.mult, ALU.add)
                        ins.then_inc(ml_out.sem, 1)
                dve.wait_ge(ml_out.sem, ml_out.at(l, 2 * TILES))
                dve.wait_ge(st_out.sem, st_out.at(l, 48))
                link(STT(den[:, 1], den[:, 0], -1.0, den[:, 0], ALU.mult, ALU.max))
                link(TT(den[:, 1], den[:, 1], cols[:, 3], ALU.max))
                link(V.reciprocal(den[:, 2], den[:, 1]))
                hv = hnum[:, :, :, :].rearrange("p t h d -> p (t h) d")
                link(TT(hv, hv, spread(den[:, 2].rearrange("p t h -> p (t h)"), DH), ALU.mult))
                hs = hnum[:, :, 0:4, :].rearrange("p t h d -> p t (h d)")
                TT(hs, hs, hnum[:, :, 4:8, :].rearrange("p t h d -> p t (h d)"), ALU.add).then_inc(ml_hsum.sem, 1)
                dve.wait_ge(ml_hsq.sem, ml_hsq.at(l, 1))
                link(V.tensor_reduce(den[:, 0, :, 0:4], hsq[:, :, :].rearrange("p (t h) d -> p t h d", h=4), AX.X, ALU.add))
                TS(den[:, 1, :, 0:4], den[:, 0, :, 0:4], 1.0 / DH, EPS, ALU.mult, ALU.add).then_inc(ml_var.sem, 1)
                dve.wait_ge(ml_root.sem, ml_root.at(l, 1))
                link(V.reciprocal(den[:, 0, :, 0:4], den[:, 2, :, 0:4]))
                TT(hnum[:, :, 0:4, :], hnum[:, :, 0:4, :], spread(den[:, 0, :, 0:4], DH), ALU.mult).then_inc(ml_h.sem, 1)
                dve.wait_ge(ml_ht.sem, ml_ht.at(l, 1))
                dve.wait_ge(ml_og.sem, ml_og.at(l, 2))
                for c in range(2):
                    if c:
                        own.inc(ins)
                        own.settle()
                    STT(yt[:, :], flat[:, 1536 * c:1536 * c + TOK], vecs[:, V_MNG + c:V_MNG + c + 1], zc(Z_O + c),
                        ALU.mult, ALU.mult).then_inc(ml_y.sem, 1)
                    dve.wait_ge(ml_yhi.sem, ml_yhi.at(l, c + 1))
                    ins = TT(a_lo[:, c, :], yt[:, :], a_hi[:, c, :].bitcast(F32), ALU.subtract)
                ins.then_inc(ml_done.sem, 1)

                dve.wait_ge(ml_done.sem, ml_done.at(l, 1))
                dve.wait_ge(at_in.sem, at_in.at(l, 48))
                for e in range(2):
                    V.memset(kh[e][QK:QK + 1, :].bitcast(F32), 1.0)
                    V.memset(kl[e][QK:QK + 1, :].bitcast(F32), 0.0)
                    ins = V.memset(va[e][:, :, V_DIM:P], 1.0)
                ins.then_inc(at_k1.sem, 1)
                dve.wait_ge(kr_t.sem, kr_t.at(l, 1))
                V.tensor_copy(krt[:, 0:TILES, :].rearrange("p t (g c) -> p t g c", g=2),
                              row.rearrange("p (t q c) -> p t q c", q=4, c=32)[:, :, 0:2, 4:20]).then_inc(at_krt.sem, 1)

                def sums(h):
                    dve.wait_ge(at_sq.sem, at_sq.at(l, h + 1))
                    link(V.tensor_reduce(small[:, 0:19], sq_[:, :, :], AX.X, ALU.add))
                    TS(small[:, 0:19], small[:, 0:19], 1.0 / QK, EPS, ALU.mult, ALU.add).then_inc(at_sum.sem, 1)

                def inverse(h):
                    dve.wait_ge(at_root.sem, at_root.at(l, h + 1))
                    v_, y_, t_ = small[:, 0:19], small[:, 40:59], small[:, 20:39]
                    link(TT(t_, y_, y_, ALU.mult))
                    link(STT(t_, t_, -0.5, v_, ALU.mult, ALU.mult))
                    STT(y_, t_, 1.5, y_, ALU.add, ALU.mult).then_inc(at_inv.sem, 1)

                def low_q(h, e):
                    dve.wait_ge(at_hq.sem, at_hq.at(l, h + 1))
                    STT(ql[e][0:QK, :], flat[0:QK, 0:TOK], vecs[0:QK, V_QC:V_QC + 1], qh[e][0:QK, :].bitcast(F32),
                        ALU.mult, ALU.subtract).then_inc(at_lq.sem, 1)

                def low_k(h, e):
                    dve.wait_ge(at_hk.sem, at_hk.at(l, h + 1))
                    STT(kl[e][0:QK, :], flat[0:QK, 0:KEYS], vecs[0:QK, V_KC:V_KC + 1], kh[e][0:QK, :].bitcast(F32),
                        ALU.mult, ALU.subtract).then_inc(at_lk.sem, 1)

                def max_rows(h, e, more):
                    for u in range(UNITS):
                        if more and u == U_SUM:
                            sums(h + 1)
                        if more and u == U_INV:
                            inverse(h + 1)
                        t, b = (u + NB - 1) // NB, (u + NB - 1) % NB
                        dve.wait_ge(at_s.sem, at_head(at_s, UNITS, l, h, u + 1))
                        out, src = (pmx[:, 0, 0:1], ps[:, 0, 0:SEQ]) if t == 0 else (pmx[:, t, b:b + 1], ps[:, u % 3, 0:BLK])
                        V.tensor_reduce(out, src, AX.X, ALU.max).then_inc(at_mx.sem, 1)
                    dve.wait_ge(at_mx.sem, at_head(at_mx, UNITS, l, h, UNITS))
                    TS(nmx[:, 0:1], pmx[:, 0, 0:1], -1.0, None, ALU.mult)
                    V.tensor_reduce(nmx[:, 1:TILES], pmx[:, 1:TILES, :], AX.X, ALU.max, negate=True).then_inc(at_nm.sem, 1)

                def low_rows(h, e):
                    dve.wait_ge(at_mhi.sem, at_mhi.at(l, h + 1))
                    TT(ql[e][QK:QK + 1, :], flat[QK:QK + 1, 0:TOK], qh[e][QK:QK + 1, :].bitcast(F32), ALU.subtract).then_inc(at_mlo.sem, 1)

                def output(h, e, o):
                    half, n = slice(DH * e, DH * e + DH), PARTS[o][1]
                    dve.wait_ge(at_pv.sem, at_head(at_pv, STEPS, l, h, (1, 10, 19)[o]))
                    dve.wait_ge(at_y.sem, at_head(at_y, 3, l, h, o))
                    bank = 6 + (e + o) % 2
                    link(V.reciprocal(rec[0:DH, 0:n], ps[DH:P, bank, 0:n]))
                    dve.wait_ge(at_done.sem, at_head(at_done, 3, l, h, o - 1))
                    TT(ya[half, (e + o) % 2, 0:n], ps[0:DH, bank, 0:n], rec[0:DH, 0:n], ALU.mult).then_inc(at_y.sem, 1)

                def split(h, e):
                    low_q(h, e)
                    low_k(h, e)

                def head(h, e, i1, i2):
                    output(h, e, 0)
                    if i1:
                        max_rows(h + 1, 1 - e, i2)
                    output(h, e, 1)
                    if i1:
                        low_rows(h + 1, 1 - e)
                    output(h, e, 2)

                sums(0)
                inverse(0)
                split(0, 0)
                max_rows(0, 0, True)
                low_rows(0, 0)
                split(1, 1)
                with dve.Fori(0, H // 2 - 1) as i:
                    own.enter(i, 32)
                    for e in range(2):
                        head(i * 2 + e, e, True, True)
                        split(i * 2 + (e + 2), e)
                    own.leave(H // 2 - 1)
                head(H - 2, 0, True, False)
                head(H - 1, 1, False, False)

                dve.wait_ge(x_back.sem, x_back.at(l, 16))
                def residual(dst, bank0, gate, sem):
                    STT(dst[:, 0:SEQ], ps[:, bank0, 0:SEQ], gate[:, 0:1], dst[:, 0:SEQ], ALU.mult, ALU.add)
                    STT(dst[:, SEQ:BLK], ps[:, bank0, SEQ:BLK], gate[:, 1:2], dst[:, SEQ:BLK], ALU.mult, ALU.add)
                    STT(blocks(dst[:, BLK:TOK]), banks(bank0 + 1, 2), gate[:, 1:2], blocks(dst[:, BLK:TOK]),
                        ALU.mult, ALU.add).then_inc(sem, 1)

                for n in range(16, 24):
                    dve.wait_ge(w_used.sem, w_used.at(l, n + 1))
                    residual(x[:, n - 16, :], 3 * (n % 2), mod[:, n, :], z_free_d.sem)
                dve.wait_ge(z_free_d.sem, z_free_d.at(l, 10))
                norm(1)

                def f_low(slot, count, dst, hi):
                    dve.wait_ge(f_hi_ok.sem, f_hi_ok.at(l, count))
                    TT(dst, f_raw[:, slot], hi.bitcast(F32), ALU.subtract).then_inc(f_lo_ok.sem, 1)

                def product(v, g):
                    f, b = v // NB, slice((v % NB) * BLK, (v % NB + 1) * BLK)
                    dve.wait_ge(f_silu.sem, f_silu.at(l, g * 6 + (v + 1)))
                    link(TT(at[:, v % 2, :], ps[:, 2 * (v % 2) + 1, 0:BLK], sg[:, v % 2, :], ALU.mult))
                    link(V.tensor_copy(g_hi[:, f, b], at[:, v % 2, :]))
                    TT(g_lo[:, f, b], at[:, v % 2, :], g_hi[:, f, b].bitcast(F32), ALU.subtract).then_inc(f_act.sem, 1)

                def fold(g):
                    for o in range(KC):
                        gate = mod[:, 40 + o, :]
                        for b in range(NB):
                            n = o * NB + b
                            dve.wait_ge(f_dn.sem, f_dn.at(l, g * 24 + (n + 1)))
                            bank = 4 + n % 4
                            if b == 0:
                                STT(x[:, o, 0:SEQ], ps[:, bank, 0:SEQ], gate[:, 0:1], x[:, o, 0:SEQ], ALU.mult, ALU.add)
                                ins = STT(x[:, o, SEQ:BLK], ps[:, bank, SEQ:BLK], gate[:, 1:2], x[:, o, SEQ:BLK], ALU.mult, ALU.add)
                            else:
                                bs = slice(b * BLK, (b + 1) * BLK)
                                ins = STT(x[:, o, bs], ps[:, bank, 0:BLK], gate[:, 1:2], x[:, o, bs], ALU.mult, ALU.add)
                            ins.then_inc(f_res.sem, 1)

                dve.wait_ge(alo_ok.sem, alo_ok.at(l, 2 * KC))
                for n in range(4):
                    f_low(n % 2, n + 1, gu_lo[:, n // 2, n % 2].rearrange("p k n -> p (k n)"), gu_hi[:, n // 2, n % 2].rearrange("p k n -> p (k n)"))
                product(0, 0)
                with dve.Fori(0, NG - 1) as g:
                    own.enter(g, 16)
                    for n in range(2):
                        f_low(n, 4 + g * 6 + n + 1, d_lo[:, n], d_hi[:, n])
                    product(1, g)
                    product(2, g)
                    for n in range(2):
                        f_low(n, 6 + g * 6 + n + 1, gu_lo[:, 0, n].rearrange("p k n -> p (k n)"), gu_hi[:, 0, n].rearrange("p k n -> p (k n)"))
                    for v in range(3, 6):
                        product(v, g)
                    for n in range(2):
                        f_low(n, 8 + g * 6 + n + 1, gu_lo[:, 1, n].rearrange("p k n -> p (k n)"), gu_hi[:, 1, n].rearrange("p k n -> p (k n)"))
                    fold(g)
                    product(0, g + 1)
                    own.leave(NG - 1)
                for n in range(2):
                    f_low(n, 4 + (NG - 1) * 6 + n + 1, d_lo[:, n], d_hi[:, n])
                for v in range(1, 6):
                    product(v, NG - 1)
                fold(NG - 1)
                dve.wait_ge(f_res.sem, f_res.at(l + 1, 0))
                own.end_layer()

        @block.gpsimd
        def _(pool):
            pool.sem_inc(at_done.sem, at_done.first)
            G = nc.gpsimd
            with pool.Fori(0, DEPTH) as l:
                own = Chain(pool, pool_own, l)
                link = own.link

                def w_low(n):
                    pool.wait_ge(w_hi_ok.sem, w_hi_ok.at(l, n + 1))
                    G.tensor_tensor(w_lo[:, n % 2, :], w_raw[:, n % 2, :], w_hi[:, n % 2, :].bitcast(F32), ALU.subtract).then_inc(w_lo_ok.sem, 1)

                for n in range(16):
                    w_low(n)
                pool.wait_ge(ml_cols.sem, ml_cols.at(l, 1))
                pool.wait_ge(ml_kv_a.sem, ml_kv_a.at(l, TILES))
                for i in range(TILES):
                    for d, t in enumerate((i, (TILES - i) % TILES)):
                        if i:
                            pool.wait_ge(ml_pv.sem, ml_pv.at(l, 2 * (i - 1) + d + 1))
                        G.tensor_tensor(kw[:, d], kt[:, t, :].rearrange("p (h d) -> p h d", h=HEADS_M),
                                        spread(cols[:, 1, t, 4 * d:4 * d + 4], DH), ALU.mult).then_inc(ml_kw.sem, 1)

                pool.wait_ge(at_in.sem, at_in.at(l, 48))
                for t0, tl, vg in ((0, TILES, V_QN), (TILES, KTILES, V_KN)):
                    g = vecs[:, vg + NOPE:vg + QK]
                    G.tensor_tensor(rope[:, 0, t0:t0 + tl, :], rope_in[:, 0, 0:tl, :], g.unsqueeze(1).to_broadcast([P, tl, ROPE]), ALU.mult)
                    pairs = [ap.rearrange("p t (a b c) -> p t a b c", a=2, b=2) for ap in (rope[:, 1, t0:t0 + tl, :], rope_in[:, 1, 0:tl, :])]
                    gp = g.rearrange("p (a b c) -> p a b c", a=2, b=2)
                    for b in range(2):
                        ins = G.tensor_tensor(pairs[0][:, :, :, b, :], pairs[1][:, :, :, b, :],
                                              gp[:, :, 1 - b, :].unsqueeze(1).to_broadcast([P, tl, 2, 8]), ALU.mult)
                ins.then_inc(at_tab.sem, 1)

                def first(h):
                    pool.wait_ge(at_inv.sem, at_inv.at(l, h + 1))
                    link(G.tensor_tensor(qk[:, :, :], qk[:, :, :], spread(small[:, 40:59], QK), ALU.mult))
                    plain = qk[:, :, NOPE:QK]
                    by_cos, by_sin = sq_[:, :, 0:ROPE], sq_[:, :, ROPE:2 * ROPE]
                    x_, s_, sines = (ap.rearrange("p t (a b c) -> p t a b c", a=2, b=2) for ap in (plain, by_sin, rope[:, 1]))
                    G.tensor_tensor(by_cos, plain, rope[:, 0], ALU.mult)
                    for b in range(2):
                        ins = G.tensor_tensor(s_[:, :, :, b, :], x_[:, :, :, 1 - b, :], sines[:, :, :, b, :], ALU.mult)
                    link(ins)
                    G.tensor_tensor(plain, by_cos, by_sin, ALU.add).then_inc(at_rope.sem, 1)

                def low(h, e, i0, o):
                    q0, n = PARTS[o]
                    half, chunk = slice(DH * e, DH * e + DH), bass.ds(i0 + 4, 1)
                    pool.wait_ge(at_done.sem, at_head(at_done, 3, l, h, o))
                    pool.wait_ge(at_yhi.sem, at_head(at_yhi, 3, l, h, o + 1))
                    G.tensor_tensor(a_lo[half, chunk, q0:q0 + n], ya[half, (e + o) % 2, 0:n].unsqueeze(1),
                                    a_hi[half, chunk, q0:q0 + n].bitcast(F32), ALU.subtract).then_inc(at_done.sem, 1)

                def head(h, e, i0, i2):
                    low(h, e, i0, 0)
                    if i2:
                        pool.wait_ge(at_done.sem, at_head(at_done, 3, l, h, 1))
                        first(h + 2)
                        pool.wait_ge(at_rope.sem, at_rope.at(l, h + 3))
                    low(h, e, i0, 1)
                    if isinstance(h, int) and h == H - 1:
                        pool.wait_ge(at_done.sem, at_done.at(l, 3 * H - 1))
                        w_low(16)
                        w_low(17)
                        pool.wait_ge(w_lo_ok.sem, w_lo_ok.at(l, 18))
                    low(h, e, i0, 2)

                pool.wait_ge(at_tab.sem, at_tab.at(l, 1))
                first(0)
                first(1)
                with pool.Fori(0, H // 2 - 1) as i:
                    own.enter(i, 8)
                    for e in range(2):
                        pool.wait_ge(at_rope.sem, at_rope.at(l, i * 2 + (e + 2)))
                        head(i * 2 + e, e, i, True)
                    own.leave(H // 2 - 1)
                head(H - 2, 0, H // 2 - 1, False)
                head(H - 1, 1, H // 2 - 1, False)
                pool.wait_ge(at_done.sem, at_done.at(l, 3 * H))
                for n in range(18, 24):
                    w_low(n)
                own.end_layer()


def constants():
    cst = np.zeros((P, NCONST), np.float32)
    cst[:, C_ID:C_ID + P] = np.eye(P)
    cst[:, C_ONE:C_ONE + P] = 1.0
    quarter = ROPE // 4
    freqs = np.float32(ROPE_BASE) ** (-np.arange(quarter, dtype=np.float32) / np.float32(quarter))
    t = np.arange(DEC_SEQ)
    ang = np.stack([(t // GRID_W).astype(np.float32)[:, None] * freqs, (t % GRID_W).astype(np.float32)[:, None] * freqs], 1)
    tab = np.zeros((2, KTILES, P, 2, 2, quarter), np.float32)
    tab[0] = 1.0
    tab[0, 1:TILES] = np.cos(ang).reshape(8, P, 2, 1, quarter)
    tab[1, 1:TILES] = np.sin(ang).reshape(8, P, 2, 1, quarter) * np.array([-1, 1], np.float32)[:, None]
    cst[:, C_ROPE:NCONST] = tab.transpose(2, 0, 1, 3, 4, 5).reshape(P, -1)
    cst[:, C_EPS] = EPS
    mc = np.zeros((P, NMC), np.float32)
    s, q = np.arange(P)[:, None], np.arange(P)[None, :]
    mc[:, M_MASK:M_MASK + P] = np.where(s <= q, 0.0, NEG)
    mc[:, M_MASK + P:M_MASK + 2 * P] = np.where(s >= q, 0.0, NEG)
    for d in range(2):
        for h in range(HEADS_M):
            at = M_SEL + (4 * d + h) * P
            mc[32 * d + h, at:at + P] = 1.0
            at = M_PAIR + (2 * d + h // 2) * P + DH * (h % 2)
            mc[32 * d + h, at:at + DH] = 1.0
    reset = np.ones((DH, TILES, P), np.float32)
    reset[0:32, :, 0] = 0.0
    reset[32:64, :, P - 1] = 0.0
    mc[0:DH, M_RESET:NMC] = reset.reshape(DH, TOK)
    return cst, mc


def kernel(**inputs):
    import concourse.bacc as bacc
    from concourse.bass_utils import run_bass_kernel_spmd as run

    g = {k: np.asarray(v) for k, v in inputs.items()}
    f32 = np.float32
    L = DEPTH

    def fm(a):
        return a.T.reshape(-1, P, a.shape[0]).transpose(1, 0, 2)

    arr = {}
    arr["xin"] = fm(np.concatenate([g["x_prompt"][0], g["x_sample"][0]], 0))
    arr["cvec"] = np.stack([g["c_ctx"], g["c"][0]], 1).reshape(KC, P, 2).transpose(1, 0, 2)
    vec = np.zeros((L, P, NVEC), f32)

    def put(at, a):
        a = a.reshape(L, -1, P).transpose(0, 2, 1)
        vec[:, :, at:at + a.shape[2]] = a

    put(V_BADA, g["b_ada"]); put(V_N1, g["norm1_g"]); put(V_N2, g["norm2_g"]); put(V_MNG, g["mlstm_norm_g"])
    put(V_DWB, g["conv_dw_b"]); put(V_LNG, g["conv_ln_g"]); put(V_LNB, g["conv_ln_b"])
    put(V_CQG, g["mla_cq_g"]); put(V_CKVG, g["mla_ckv_g"])
    vec[:, :, V_DW:V_DW + 2 * CONV_WIDTH] = g["conv_dw_w"].reshape(L, CONV_WIDTH, 2, P).transpose(0, 3, 2, 1).reshape(L, P, -1)
    gates = {0: 0, 64: 4, 32: 8, 96: 12}
    for part, col in gates.items():
        vec[:, part:part + 4, V_BG] = g["b_gates"][:, col:col + 4]
    for d in range(2):
        vec[:, 32 * d:32 * d + 4, V_M0] = g["state_m"][0, :, d, :]
    vec[:, :, V_QN:V_QN + QK] = g["mla_qn_g"][:, None, :]
    vec[:, :, V_KN:V_KN + QK] = g["mla_kn_g"][:, None, :]
    for at, name in ((V_QC, "mla_qn_g"), (V_KC, "mla_kn_g")):
        vec[:, 0:NOPE, at], vec[:, NOPE:, at] = g[name][:, 0:NOPE], 1.0
    arr["vec"] = vec
    arr["const"], arr["mconst"] = constants()

    def tiles(w):
        n = w.shape[2] // P
        return w.reshape(L, -1, P, n, P).transpose(0, 3, 2, 1, 4)

    wa = tiles(g["w_ada"])
    arr["wada"] = wa.reshape(L, 12, 4, P, KC, P).transpose(0, 1, 3, 2, 4, 5)
    w = g["w_in"]
    misc = np.zeros((L, D_MODEL, P), f32)
    for part, col in gates.items():
        misc[:, :, part:part + 4] = w[:, :, 1024 + col:1028 + col]
    misc[:, :, 4:20], misc[:, :, 36:52] = w[:, :, 1936:1952], w[:, :, 1952:1968]
    conv = w[:, :, 1040:1552]
    cols = [conv[:, :, 256:384], conv[:, :, 0:128], conv[:, :, 384:512], conv[:, :, 128:256],
            w[:, :, 0:1024], w[:, :, 1552:1936], misc]
    arr["win"] = tiles(np.concatenate(cols, 2)).reshape(L, 16, P, KC * P)
    arr["wout"] = tiles(g["w_out"]).reshape(L, KC, P, KC * P)
    gu = tiles(g["ffn_w_gu"])
    arr["wgu"] = np.stack([gu[:, 0:FC], gu[:, FC:]], 3).reshape(L, FC, P, 2, KC * P)
    arr["wdn"] = g["ffn_w_down"].reshape(L, FC, P, D_MODEL)
    arr["pww"] = g["conv_pw_w"].reshape(L, 2, P, 2, P).transpose(0, 2, 1, 3, 4)
    wq = g["mla_w_uq"].reshape(L, 2, P, HEADS_A, QK).transpose(0, 3, 2, 1, 4).reshape(L, HEADS_A, P, 2 * QK)
    wkv = g["mla_w_ukv"].reshape(L, P, HEADS_A, P).transpose(0, 2, 1, 3)
    arr["whd"] = np.concatenate([wq, wkv], 3)
    arr["ctx_ckv"] = g["cache_ckv"][0].transpose(0, 2, 1)
    arr["ctx_kr"] = g["cache_krope"][0]
    cn = np.concatenate([g["state_C"][0], g["state_n"][0][..., None]], -1)
    arr["c0"] = cn.reshape(L, 2, 2, 2, DH, DH + 1).transpose(0, 3, 4, 1, 2, 5).reshape(L, P, 2, 2, DH + 1)
    arr = {k: np.ascontiguousarray(v) for k, v in arr.items()}

    outs = {"yout": (P, KC, TOK), "o_ckv": (L, P, SEQ), "o_kr": (L, 2, 16, SEQ), "o_c": (L, P, 2, 2, DH + 1), "o_m": (L, 2, 4, 1)}
    nc = bacc.Bacc("TRN2", target_bir_lowering=False, num_devices=1)
    aps = [nc.dram_tensor(k, v.shape, F32, kind="ExternalInput").ap() for k, v in arr.items()]
    aps += [nc.dram_tensor(k, s, F32, kind="ExternalOutput").ap() for k, s in outs.items()]
    aps.append(nc.dram_tensor("spill", (P, KC, TOK), F32, kind="Internal").ap())
    build(nc, *aps)
    r = run(nc, [arr], core_ids=[0]).results[0]

    y = r["yout"].transpose(2, 1, 0).reshape(TOK, D_MODEL)
    ckv = r["o_ckv"].transpose(0, 2, 1)[None]
    kr = r["o_kr"].reshape(L, ROPE, SEQ).transpose(0, 2, 1)[None]
    cn = r["o_c"].reshape(L, 2, DH, 2, 2, DH + 1).transpose(0, 3, 4, 1, 2, 5).reshape(L, 2, HEADS_M, DH, DH + 1)
    return tuple(np.ascontiguousarray(v) for v in (
        y[None, :SEQ], y[None, SEQ:], ckv, kr, cn[None, ..., :DH], cn[None, ..., DH], r["o_m"].reshape(1, L, 2, HEADS_M)))
```

```python
from contextlib import ExitStack

import concourse.bass as bass
import numpy as np
from concourse import mybir

F32 = mybir.dt.float32
F32R = mybir.dt.float32r
ACT = mybir.ActivationFunctionType
ALU = mybir.AluOpType
AX = mybir.AxisListType

P = 128
D_MODEL = 1024
SEQ = 128
DEC_SEQ = 1024
PAST = 128
DEPTH = 2
GRID_W = 64
HEADS_M = 4
DH = 64
CONV_CH = 256
CONV_WIDTH = 31
CONV_PAD = CONV_WIDTH // 2
HEADS_A = 8
NOPE = 64
ROPE = 32
QK = NOPE + ROPE
V_DIM = 64
Q_RANK = 256
KV_RANK = 128
ROPE_BASE = 10000.0
D_FF = 2816
EPS = 1e-6
NEG = -1e30

TOK = SEQ + DEC_SEQ
TILES = TOK // P
KC = D_MODEL // P
BLK = 384
NB = TOK // BLK
FC = D_FF // P
KEYS = TOK + PAST
KTILES = KEYS // P
SEG = P + 2 * CONV_PAD
U_LEN = SEG + DEC_SEQ + 2 * CONV_PAD
Y_LEN = U_LEN - 2 * CONV_PAD
SCALE_A = float(QK) ** -0.5
SCALE_M = float(DH) ** -0.5

V_BADA, V_N1, V_N2, V_MNG, V_DWB, V_LNG, V_LNB, V_CQG, V_CKVG, V_DW = 0, 48, 56, 64, 66, 68, 70, 72, 74, 75
V_M0 = V_DW + 2 * CONV_WIDTH
V_BG = V_M0 + 1
V_QN = V_BG + 1
V_KN = V_QN + QK
V_QC = V_KN + QK
V_KC = V_QC + 1
NVEC = V_KC + 1
C_ID, C_ONE, C_EPS, C_ROPE = 0, P, 2 * P, 2 * P + 1
NCONST = C_ROPE + 2 * KTILES * ROPE
M_MASK, M_SEL, M_PAIR, M_RESET = 0, 2 * P, 2 * P + 8 * P, 2 * P + 12 * P
NMC = M_RESET + TOK
Z_Q, Z_K, Z_V, Z_O, Z_CQ, Z_CKV, Z_MISC = 0, 2, 4, 6, 8, 10, 11
ADA_PE = 6
ADA_CUTS = (0, 7, 10)
LATE = 24
LAST = 48 - 16 - LATE
STRIDE = 4096


class Chain:

    def __init__(self, eng, sem, layer):
        self.eng, self.sem, self.base, self.n = eng, sem, layer * STRIDE, 0

    def inc(self, ins):
        self.n += 1
        ins.then_inc(self.sem, 1)

    def settle(self, back=0):
        self.eng.wait_ge(self.sem, self.base + (self.n - back))

    def link(self, ins):
        self.inc(ins)
        self.settle()

    def enter(self, i, size):
        self.outer, self.size = (self.base, self.n), size
        self.base, self.n = self.base + self.n + i * size, 0

    def leave(self, count):
        self.settle()
        if self.size > self.n:
            self.eng.sem_inc(self.sem, self.size - self.n)
        self.base, self.n = self.outer[0], self.outer[1] + count * self.size

    def end_layer(self):
        self.settle()
        assert self.n <= STRIDE, self.n
        if STRIDE > self.n:
            self.eng.sem_inc(self.sem, STRIDE - self.n)


class Signal:

    def __init__(self, sem, per_layer, first=0):
        self.sem, self.per, self.first = sem, per_layer, first

    def at(self, layer, k):
        return layer * self.per + (k + self.first)


def build(nc, xin, cvec, crow_d, vec, const, mconst, wada_a, wada_b, win, wout, wgu, wdn, pww, whd, ctx_ckv, ctx_kr,
          c0, yout, o_ckv, o_kr, o_c, o_m, spill):
    ctx = ExitStack()
    with ctx:
        def sb(name, shape, dt=F32, where=ctx):
            return where.enter_context(nc.sbuf_tensor(name, shape, dt))

        cst = sb("cst", [P, C_ROPE])
        ident, ones, eps = cst[:, C_ID:C_ID + P], cst[:, C_ONE:C_ONE + P], cst[:, C_EPS:C_EPS + 1]
        vecs = sb("vecs", [P, NVEC])
        cond = sb("cond", [P, KC, 2])
        mod = sb("mod", [P, 48, 2])
        gain = sb("gain", [P, 2, KC, 2])
        small = sb("small", [P, 64])
        diag = sb("diag", [P, TILES, P])
        krt = sb("krt", [P, KTILES, ROPE])
        normed = diag[0:32 * NB, :, :].rearrange("p t n -> p (t n)").rearrange("p (i n) -> p i n", n=BLK)
        mrow = sb("mrow", [DH, 4, TILES])

        wx = ExitStack()
        wada_p = sb("wada_p", [P, ADA_PE, KC, P], F32, wx)
        wada_v = sb("wada_v", [P, 16 - ADA_PE, D_MODEL], F32, wx)
        wx.close()
        hx = ExitStack()
        lsq_a = sb("lsq_a", [P, TOK], F32, hx)
        diag2 = sb("diag2", [P, TILES, P], F32, hx)
        hx.close()
        hx = ExitStack()
        sb("hx_at", [P, 2, TOK], F32, hx)
        cvsq = sb("cvsq", [P, 2, TOK], F32, hx)
        hnum = sb("hnum", [P, TILES, 8, DH], F32, hx)
        hx.close()
        a_hi = sb("a_hi", [P, KC, TOK], F32R)
        lx = ExitStack()
        lsq_b = sb("lsq_b", [P, 2, TOK], F32, lx)
        sb("lx_at", [P, 2, TOK], F32, lx)
        lx2 = ExitStack()
        pw = sb("pw", [P, 2, 2, P], F32, lx2)
        wada_l = sb("wada_l", [P, 4, KC, P], F32, lx2)
        lx2.close()
        kt = sb("kt", [P, TILES, 2 * P], F32, lx)
        em = sb("em", [P, 2, HEADS_M, P], F32, lx)
        sp_ = sb("sp_", [P, 2, HEADS_M, P], F32, lx)
        lx.close()
        a_lo = sb("a_lo", [P, KC, TOK], F32R)
        zx = ExitStack()

        def queries(e, where):
            return sb(f"qh{e}", [P, TOK], F32R, where), sb(f"ql{e}", [P, TOK], F32R, where)

        def keys_values(e, where):
            return (sb(f"kh{e}", [P, KEYS], F32R, where), sb(f"kl{e}", [P, KEYS], F32R, where),
                    sb(f"va{e}", [P, KTILES, P], F32, where))

        ops0 = queries(0, zx) + keys_values(0, zx)
        rope_in = sb("rope_in", [P, 2, KTILES, ROPE], F32, zx)
        zx.close()
        zx = ExitStack()
        sb("zx_at", [P, 4, TOK], F32, zx)
        wada_z = sb("wada_z", [P, 4, TOK], F32, zx)
        zx.close()
        z = sb("z", [P, 8, TOK])
        x = z
        rest = ExitStack()
        z2 = sb("z2", [P, 4, TOK], F32, rest)

        def zc(c):
            return z[:, c, :] if c < 8 else z2[:, c - 8, :]

        s2 = ExitStack()
        w_raw = sb("w_raw", [P, 2, KC * P], F32, s2)
        w_hi = sb("w_hi", [P, 2, KC * P], F32R, s2)
        w_lo = sb("w_lo", [P, 2, KC * P], F32R, s2)
        mc = sb("mc", [P, M_RESET], F32, s2)
        sb("s2_at", [P, 2 * KC * P - M_RESET], F32, s2)
        s1 = ExitStack()
        nsq = sb("nsq", [P, 2, TOK], F32, s1)
        nt = sb("nt", [P, 2, TOK], F32, s1)
        inv_rows = sb("inv_rows", [P, TOK], F32, s1)
        s1.close()
        s4r = ExitStack()
        reset = sb("reset", [DH, TOK], F32, s4r)
        ra = sb("ra", [P, TOK], F32, s4r)
        rb = sb("rb", [P, TOK], F32, s4r)
        rr = sb("rr", [DH, TOK], F32, s4r)
        lf = sb("lf", [DH, TOK], F32, s4r)
        s4r.close()
        u = sb("u", [P, 2, U_LEN], F32, s2)
        sigb = sb("sigb", [P, TOK], F32, s2)
        yc = sb("yc", [P, 2, U_LEN], F32, s2)
        cx = ExitStack()
        crow = sb("crow", [P, 2, D_MODEL], F32, cx)
        cx.close()
        csq = sb("csq", [P, 2, TOK], F32, s2)
        s2.close()
        s4 = ExitStack()
        vaug = sb("vaug", [P, TILES, HEADS_M, DH + 1], F32, s4)
        kw = sb("kw", [P, 2, HEADS_M, DH], F32, s4)
        ni = sb("ni", [P, 2, HEADS_M, DH + 1], F32, s4)
        cols = sb("cols", [P, 4, TILES, 8], F32, s4)
        den = sb("den", [P, 3, TILES, 8], F32, s4)
        dcol = sb("dcol", [P, 4, TILES], F32, s4)
        cst_st = sb("cst_st", [P, 2, 2, 2, DH + 1], F32, s4)
        s4.close()
        s4b = ExitStack()
        sb("s4b_at", [P, 8 * KC * P], F32, s4b)
        hsq = sb("hsq", [P, TILES * HEADS_M, DH], F32, s4b)
        yt = sb("yt", [P, TOK], F32, s4b)
        s4b.close()
        s5 = ExitStack()
        ctxk = sb("ctxk", [P, PAST], F32, s5)
        hw = sb("hw", [P, 2, 320], F32, s5)
        qk = sb("qk", [P, TILES + KTILES, QK], F32, s5)
        sq_ = sb("sq_", [P, TILES + KTILES, QK], F32, s5)
        rope = sb("rope", [P, 2, TILES + KTILES, ROPE], F32, s5)
        vt = sb("vt", [P, KTILES, V_DIM], F32, s5)
        kv1 = keys_values(1, s5)
        pmx = sb("pmx", [P, TILES, NB], F32, s5)
        nmx = sb("nmx", [P, TILES], F32, s5)
        pt = sb("pt", [P, 3, 512], F32, s5)
        rec = sb("rec", [P, 512], F32, s5)
        ya = sb("ya", [P, 2, 512], F32, s5)
        used = (PAST + 640 + (TILES + KTILES) * 2 * (QK + ROPE) + KTILES * V_DIM + 2 * KEYS + KTILES * P
                + TILES * (NB + 1) + 6 * 512)
        sb("s5_at", [P, 8 * KC * P + 4 * U_LEN + TOK - used], F32, s5)
        qh, ql, kh, kl, va = zip(ops0, queries(1, s5) + kv1)
        s5.close()
        rest.close()
        s8 = ExitStack()
        f_raw = sb("f_raw", [P, 2, KC * P], F32, s8)
        gu_hi = sb("gu_hi", [P, 2, 2, KC, P], F32R, s8)
        gu_lo = sb("gu_lo", [P, 2, 2, KC, P], F32R, s8)
        g_hi = sb("g_hi", [P, 2, TOK], F32R, s8)
        g_lo = sb("g_lo", [P, 2, TOK], F32R, s8)
        d_hi = sb("d_hi", [P, 2, D_MODEL], F32R, s8)
        d_lo = sb("d_lo", [P, 2, D_MODEL], F32R, s8)
        sg = sb("sg", [P, 2, BLK], F32, s8)
        at = sb("at", [P, 2, BLK], F32, s8)
        s8.close()

        ps = ctx.enter_context(nc.psum_tensor("ps", [P, 8, 512], F32))
        flat = ps[:, :, :].rearrange("p b n -> p (b n)")

        def banks(b, n=NB):
            return ps[:, b:b + n, 0:BLK]

        def blocks(ap):
            return ap.rearrange("p (b n) -> p b n", n=BLK)

        def spread(ap, n):
            return ap.unsqueeze(len(ap.shape)).to_broadcast([*ap.shape, n])

        def sig(name, per, first=0):
            return Signal(ctx.enter_context(nc.semaphore(name)), per, first)

        NG = FC // 2
        const_in = sig("const_in", 0)
        cond_ok = sig("cond_ok", 0)
        vec_in = sig("vec_in", 16)
        crow_in = sig("crow_in", 16)
        crow_ok = sig("crow_ok", 1)
        ada1_in = sig("ada1_in", 16)
        ada1_vin = [sig(f"ada1_vin{i}", 16) for i in range(2)]
        ada1_used = sig("ada1_used", 1)
        ada2_in = [sig(f"ada2_in{i}", LATE // 4 * 16) for i in range(4)]
        ada2_used = sig("ada2_used", LATE)
        ada3_in = [sig(f"ada3_in{i}", LAST // 4 * 16) for i in range(4)]
        ada3_used = sig("ada3_used", LAST)
        mod_ok = sig("mod_ok", 1)
        sq_ok = sig("sq_ok", 2 * KC)
        sq_used = sig("sq_used", 2 * KC)
        rs_var = sig("rs_var", 4)
        rs_root = sig("rs_root", 4)
        rs_inv = sig("rs_inv", 2)
        rs_row = sig("rs_row", 2)
        rs_rows = sig("rs_rows", 2)
        nh_ok = sig("nh_ok", 2 * KC)
        ahi_ok = sig("ahi_ok", 2 * KC)
        alo_ok = [sig("alo_even", KC), sig("alo_odd", KC)]
        spilled = sig("spilled", 32)
        w_in_ = [sig(f"w_in{i}", 12 * 16) for i in range(2)]
        w_hi_ok = sig("w_hi_ok", 24)
        w_lo_ok = sig("w_lo_ok", 24)
        w_used = sig("w_used", 24)
        z_free_a = sig("z_free_a", 14)
        z_free_d = sig("z_free_d", 10)
        c_sq = sig("c_sq", 2)
        c_sum = sig("c_sum", 1)
        c_diag = sig("c_diag", 2)
        c_row = sig("c_row", 2)
        cq_ok = sig("cq_ok", 2)
        ckv_out = sig("ckv_out", 48)
        pw_in = sig("pw_in", 16)
        cv_y = sig("cv_y", 1)
        cv_sum = sig("cv_sum", 2)
        cv_xc = sig("cv_xc", 1)
        cv_sq = sig("cv_sq", 1)
        cv_diag = sig("cv_diag", 1)
        cv_row = sig("cv_row", 1)
        cv_n = sig("cv_n", 1)
        cv_act = sig("cv_act", 1)
        cv_pw = sig("cv_pw", 2)
        cv_hi = sig("cv_hi", 2)
        cv_done = sig("cv_done", 2)
        ml_reset = sig("ml_reset", 16)
        ml_in = sig("ml_in", 16)
        ml_dmm = sig("ml_dmm", 1)
        ml_c0 = sig("ml_c0", 16)
        ml_ln = sig("ml_ln", 1)
        ml_rows = sig("ml_rows", 1)
        ml_dexp = sig("ml_dexp", 1)
        ml_tr = sig("ml_tr", 2)
        ml_cols = sig("ml_cols", 1)
        ml_dcol = sig("ml_dcol", 1)
        ml_kvt = sig("ml_kvt", TILES)
        ml_kv_a = sig("ml_kv_a", TILES)
        ml_kv_v = sig("ml_kv_v", TILES)
        ml_zero = sig("ml_zero", 1)
        ml_bc = sig("ml_bc", 2 * TILES)
        ml_qk = sig("ml_qk", TILES)
        ml_em = sig("ml_em", 2 * TILES)
        ml_exp = sig("ml_exp", 2 * TILES)
        ml_s = sig("ml_s", 2 * TILES)
        ml_kw = sig("ml_kw", 2 * TILES)
        ml_pv = sig("ml_pv", 2 * TILES)
        ml_out = sig("ml_out", 2 * TILES)
        ml_hsum = sig("ml_hsum", 1)
        ml_hsq = sig("ml_hsq", 1)
        ml_var = sig("ml_var", 1)
        ml_root = sig("ml_root", 1)
        ml_h = sig("ml_h", 1)
        ml_og = sig("ml_og", 2)
        ml_ht = sig("ml_ht", 1)
        ml_y = sig("ml_y", 2)
        ml_yhi = sig("ml_yhi", 2)
        ml_done = sig("ml_done", 1)
        st_out = sig("st_out", 48)
        x_back = sig("x_back", 16)
        H = HEADS_A
        STEPS = 19
        UNITS = 1 + (TILES - 1) * NB
        at_in = sig("at_in", 48)
        at_k1 = sig("at_k1", 1)
        at_tab = sig("at_tab", 1)
        at_krt = sig("at_krt", 1)
        kr_t = sig("kr_t", 1)
        hw_in = [sig(f"hw_in{i}", 4 * 16) for i in range(2)]
        at_pq = sig("at_pq", H)
        at_pk = sig("at_pk", H)
        at_tq = sig("at_tq", H)
        at_tk = sig("at_tk", H)
        at_sq = sig("at_sq", H)
        at_sum = sig("at_sum", H)
        at_root = sig("at_root", H)
        at_inv = sig("at_inv", H)
        at_rope = sig("at_rope", H)
        at_trq = sig("at_trq", H)
        at_hq = sig("at_hq", H)
        at_lq = sig("at_lq", H)
        at_trk = sig("at_trk", H)
        at_hk = sig("at_hk", H)
        at_lk = sig("at_lk", H)
        at_va = sig("at_va", H)
        at_s = sig("at_s", UNITS * H)
        at_mx = sig("at_mx", UNITS * H)
        at_nm = sig("at_nm", H)
        at_mrow = sig("at_mrow", H)
        at_mhi = sig("at_mhi", H)
        at_mlo = sig("at_mlo", H)
        at_st = sig("at_st", STEPS * H)
        at_exp = sig("at_exp", STEPS * H)
        at_pv = sig("at_pv", STEPS * H, first=1)
        at_y = sig("at_y", 3 * H, first=2)
        at_yhi = sig("at_yhi", 3 * H)
        at_done = sig("at_done", 3 * H, first=2)
        f_in = [sig(f"f_in{i}", 3 * NG * 16) for i in range(2)]
        f_hi_ok = sig("f_hi_ok", 6 * NG)
        f_lo_ok = sig("f_lo_ok", 6 * NG)
        f_gu = sig("f_gu", 6 * NG, first=1)
        f_silu = sig("f_silu", 6 * NG)
        f_act = sig("f_act", 6 * NG, first=1)
        f_dn = sig("f_dn", 24 * NG, first=1)
        f_res = sig("f_res", 24 * NG, first=1)
        y_out = sig("y_out", 0)
        act_own = ctx.enter_context(nc.semaphore("act_own"))
        dve_own = ctx.enter_context(nc.semaphore("dve_own"))
        pool_own = ctx.enter_context(nc.semaphore("pool_own"))

        A = nc.scalar.activation
        V = nc.vector
        MM = nc.tensor.matmul

        FIRST, LATER = range(0, 4), range(4, STEPS)
        S_TRQ, S_TRK, S_PQ, S_PK, S_MAX, S_ROOT, S_ROW = 0, 2, 4, 5, 6, 9, 14
        U_SUM, U_INV = 6, 20
        PARTS = ((0, SEQ), (SEQ, 512), (SEQ + 512, 512))

        def units_beside(s):
            return range(4 * (s - S_MAX), min(4 * (s - S_MAX) + 4, UNITS)) if s >= S_MAX else range(0)

        REQUESTS = ((0, slice(0, SEQ)), (1, slice(SEQ, TOK)))

        def at_head(signal, per_head, l, h, k):
            return signal.at(l, h * per_head + k)

        block = ctx.enter_context(nc.Block())

        @block.sync
        def _(sp):
            sp.dma_start(cst[:, :], const[:, 0:C_ROPE]).then_inc(const_in.sem, 16)
            sp.dma_start(cond[:, :, :], cvec).then_inc(const_in.sem, 16)
            sp.dma_start(x[:, :, :], xin).then_inc(const_in.sem, 16)
            with sp.Fori(0, DEPTH) as l:
                sp.wait_ge(f_gu.sem, f_gu.at(l, 0))
                sp.dma_start(vecs[:, :], vec[bass.ds(l, 1)].rearrange("a p n -> (a p) n")).then_inc(vec_in.sem, 16)
                for p in range(2):
                    part = slice(ADA_CUTS[p], ADA_CUTS[p + 1])
                    sp.dma_start(wada_v[:, part], wada_b[bass.ds(l, 1), :, part]
                                 .rearrange("a p c n -> (a p) c n")).then_inc(ada1_vin[p].sem, 16)
                    if p == 0:
                        sp.wait_ge(f_res.sem, f_res.at(l, 0))
                        sp.dma_start(crow[:, :, :], crow_d).then_inc(crow_in.sem, 16)
                        sp.dma_start(wada_p[:, :, :, :], wada_a[bass.ds(l, 1), :, 0:ADA_PE].rearrange("a p c k n -> (a p) c k n")).then_inc(ada1_in.sem, 16)
                sp.wait_ge(const_in.sem, 48)
                sp.dma_start(spill, x[:, :, :]).then_inc(spilled.sem, 32)
                sp.dma_start(mc[:, :], mconst[:, 0:M_RESET]).then_inc(ml_in.sem, 16)

                def ada2(first, last):
                    for m in range(first, last):
                        if m >= 4:
                            sp.wait_ge(ada2_used.sem, ada2_used.at(l, m - 3))
                        sp.dma_start(wada_z[:, m % 4, 0:D_MODEL], wada_b[bass.ds(l, 1), :, 16 - ADA_PE + m].rearrange("a p n -> (a p) n")) \
                            .then_inc(ada2_in[m % 4].sem, 16)

                for n in range(16):
                    if n >= 2:
                        sp.wait_ge(w_hi_ok.sem, w_hi_ok.at(l, n - 1))
                        sp.wait_ge(w_lo_ok.sem, w_lo_ok.at(l, n - 1))
                    sp.dma_start(w_raw[:, n % 2], win[bass.ds(l, 1), n].rearrange("a p n -> (a p) n")) \
                        .then_inc(w_in_[n % 2].sem, 16)
                    if n == 3:
                        sp.wait_ge(nh_ok.sem, nh_ok.at(l, KC))
                        sp.wait_ge(spilled.sem, spilled.at(l, 32))
                    if 3 <= n < 9:
                        cuts = (0, 8, 12, 16, 20, 22, LATE)
                        ada2(cuts[n - 3], cuts[n - 2])
                sp.wait_ge(cv_y.sem, cv_y.at(l, 1))
                sp.dma_start(reset[:, :], mconst[0:DH, M_RESET:NMC]).then_inc(ml_reset.sem, 16)
                sp.wait_ge(w_used.sem, w_used.at(l, 16))
                sp.dma_start(cst_st[:, 1], c0[bass.ds(l, 1)].rearrange("a p d j n -> (a p) d j n")).then_inc(ml_c0.sem, 16)
                sp.wait_ge(cq_ok.sem, cq_ok.at(l, 2))
                sp.dma_start(o_ckv[bass.ds(l, 1)].rearrange("a p n -> (a p) n"), zc(Z_CKV)[:, 0:SEQ]).then_inc(ckv_out.sem, 16)
                for g in range(2):
                    sp.dma_start(o_kr[bass.ds(l, 1), g].rearrange("a p n -> (a p) n"),
                                 zc(Z_MISC)[4 + 32 * g:20 + 32 * g, 0:SEQ]).then_inc(ckv_out.sem, 16)
                sp.wait_ge(ml_out.sem, ml_out.at(l, 2))
                sp.dma_start(o_c[bass.ds(l, 1)].rearrange("a p d j n -> (a p) d j n"), cst_st[:, 0]).then_inc(st_out.sem, 16)
                sp.dma_start(o_m[bass.ds(l, 1), 0].rearrange("a p n -> (a p) n"), rb[DH:DH + 4, SEQ - 1:SEQ]).then_inc(st_out.sem, 16)
                sp.dma_start(o_m[bass.ds(l, 1), 1].rearrange("a p n -> (a p) n"), rb[DH + 32:DH + 36, 0:1]).then_inc(st_out.sem, 16)
                sp.wait_ge(ml_out.sem, ml_out.at(l, 2 * TILES))
                sp.dma_start(pw[:, :, :, :], pww[bass.ds(l, 1)].rearrange("a p k o n -> (a p) k o n")).then_inc(pw_in.sem, 16)
                for m in range(LAST):
                    if m >= 4:
                        sp.wait_ge(ada3_used.sem, ada3_used.at(l, m - 3))
                    sp.dma_start(wada_l[:, m % 4], wada_a[bass.ds(l, 1), :, ADA_PE + m].rearrange("a p k n -> (a p) k n")).then_inc(ada3_in[m % 4].sem, 16)
                sp.wait_ge(ml_done.sem, ml_done.at(l, 1))
                sp.wait_ge(st_out.sem, st_out.at(l, 48))
                sp.dma_start(ctxk[:, :], ctx_ckv[bass.ds(l, 1)].rearrange("a p n -> (a p) n")).then_inc(at_in.sem, 16)
                sp.dma_start(krt[:, TILES, :], ctx_kr[bass.ds(l, 1)].rearrange("a p n -> (a p) n")).then_inc(at_in.sem, 16)
                sp.dma_start(rope_in[:, :, :, :], const[:, C_ROPE:NCONST].rearrange("p (w t n) -> p w t n", w=2, n=ROPE)).then_inc(at_in.sem, 16)
                for h in range(2):
                    sp.dma_start(hw[:, h], whd[bass.ds(l, 1), h].rearrange("a p n -> (a p) n")).then_inc(hw_in[h].sem, 16)
                with sp.Fori(0, H // 2 - 1) as i:
                    for e in range(2):
                        sp.wait_ge(at_pk.sem, at_pk.at(l, i * 2 + (e + 1)))
                        sp.dma_start(hw[:, e], whd[bass.ds(l, 1), bass.ds(i * 2 + (e + 2), 1)]
                                     .rearrange("a b p n -> (a b p) n")).then_inc(hw_in[e].sem, 16)
                sp.wait_ge(at_trk.sem, at_trk.at(l, H))
                sp.wait_ge(at_va.sem, at_va.at(l, H))
                for n in range(16, 24):
                    if n >= 18:
                        sp.wait_ge(w_hi_ok.sem, w_hi_ok.at(l, n - 1))
                        sp.wait_ge(w_lo_ok.sem, w_lo_ok.at(l, n - 1))
                    sp.dma_start(w_raw[:, n % 2], wout[bass.ds(l, 1), n - 16].rearrange("a p n -> (a p) n")) \
                        .then_inc(w_in_[n % 2].sem, 16)
                    if n == 17:
                        sp.wait_ge(at_pv.sem, at_pv.at(l, STEPS * (H - 1)))
                        sp.dma_start(x[:, :, :], spill).then_inc(x_back.sem, 16)

                def ff(slot, before, src):
                    if before is not None:
                        sp.wait_ge(f_hi_ok.sem, before)
                        sp.wait_ge(f_lo_ok.sem, before)
                    sp.dma_start(f_raw[:, slot], src).then_inc(f_in[slot].sem, 16)

                def gu_src(f, part):
                    return wgu[bass.ds(l, 1), f, :, part].rearrange("a p n -> (a p) n")

                for n in range(4):
                    ff(n % 2, f_hi_ok.at(l, n - 1) if n >= 2 else None, gu_src(n // 2, n % 2))
                with sp.Fori(0, NG - 1) as g:
                    for n in range(2):
                        ff(n, f_hi_ok.at(l, g * 6 + (4 + n - 1)), wdn[bass.ds(l, 1), bass.ds(g * 2 + n, 1)].rearrange("a b p n -> (a b p) n"))
                    for n in range(4):
                        ff(n % 2, f_hi_ok.at(l, g * 6 + (6 + n - 1)),
                           wgu[bass.ds(l, 1), bass.ds(g * 2 + (2 + n // 2), 1), :, n % 2].rearrange("a b p n -> (a b p) n"))
                for n in range(2):
                    ff(n, f_hi_ok.at(l, 6 * (NG - 1) + 4 + n - 1), wdn[bass.ds(l, 1), 2 * (NG - 1) + n].rearrange("a p n -> (a p) n"))
            sp.wait_ge(f_res.sem, f_res.at(DEPTH, 0))
            sp.dma_start(yout, x[:, :, :]).then_inc(y_out.sem, 16)
            sp.wait_ge(y_out.sem, 16)
            sp.wait_ge(ckv_out.sem, ckv_out.at(DEPTH, 0))
            sp.wait_ge(st_out.sem, st_out.at(DEPTH, 0))
            sp.wait_ge(spilled.sem, spilled.at(DEPTH, 0))

        @block.tensor
        def _(pe):
            for s in (f_dn, at_pv, f_gu):
                pe.sem_inc(s.sem, s.first)
            pe.wait_ge(const_in.sem, 48)
            pe.wait_ge(cond_ok.sem, 1)
            with pe.Fori(0, DEPTH) as l:
                pe.wait_ge(f_res.sem, f_res.at(l, 0))

                def sums(which, c):
                    pe.wait_ge(sq_ok.sem, sq_ok.at(l, which * KC + c + 1))
                    for b in range(NB):
                        mm = MM(ps[32 * b:32 * b + 32, 6, 0:BLK], ones[:, 0:32], nsq[:, c % 2, b * BLK:(b + 1) * BLK],
                                start=(c == 0), stop=(c == KC - 1))
                    mm.then_inc(sq_used.sem, 1)

                def rows(which):
                    pe.wait_ge(rs_inv.sem, rs_inv.at(l, which + 1))
                    for b in range(NB):
                        mm = MM(ps[:, b, 0:BLK], ones[32 * b:32 * b + 1, :], normed[32 * b:32 * b + 1, 2, :], start=True, stop=True)
                    mm.then_inc(rs_row.sem, 1)

                def halves_ok(which, k):
                    s = alo_ok[k % 2]
                    pe.wait_ge(s.sem, s.at(l, which * KC // 2 + k // 2 + 1))

                def part3(n, k):
                    whi, wlo = w_hi[:, n % 2, k * P:(k + 1) * P], w_lo[:, n % 2, k * P:(k + 1) * P]
                    for w, a, first, last in ((whi, a_hi, True, False), (whi, a_lo, False, False), (wlo, a_hi, False, True)):
                        for b in range(NB):
                            mm = MM(ps[:, 3 * (n % 2) + b, 0:BLK], w, a[:, k, b * BLK:(b + 1) * BLK],
                                    start=(k == 0 and first), stop=(k == KC - 1 and last))
                    return mm

                def chunk3(n):
                    pe.wait_ge(w_lo_ok.sem, w_lo_ok.at(l, n + 1))
                    if n in (3, 5):
                        pe.wait_ge(z_free_d.sem, z_free_d.at(l, n // 2))
                    elif n >= 18:
                        pe.wait_ge(z_free_d.sem, z_free_d.at(l, n - 15))
                    elif n >= 2:
                        pe.wait_ge(z_free_a.sem, z_free_a.at(l, n // 2 if n < 6 else n - 3))
                    for k in range(KC):
                        if n == 16 and k == KC - 1:
                            pe.wait_ge(at_done.sem, at_done.at(l, 3 * H))
                        mm = part3(n, k)
                    mm.then_inc(w_used.sem, 1)

                for c in range(KC):
                    sums(0, c)
                def modulation(bank, c, weights):
                    for k in range(KC):
                        mm = MM(ps[:, bank, 2 * c:2 * c + 2], weights[:, k, :], cond[:, k, :], start=(k == 0), stop=(k == KC - 1))
                    return mm

                pe.wait_ge(ada1_in.sem, ada1_in.at(l, 16))
                for c in range(ADA_PE):
                    mm = modulation(7, c, wada_p[:, c])
                mm.then_inc(ada1_used.sem, 1)
                rows(0)
                pe.wait_ge(rs_rows.sem, rs_rows.at(l, 1))
                pe.wait_ge(w_lo_ok.sem, w_lo_ok.at(l, 2))
                for k in range(KC):
                    halves_ok(0, k)
                    for n in range(2):
                        mm = part3(n, k)
                        if k == KC - 1:
                            mm.then_inc(w_used.sem, 1)
                for n in range(2, 16):
                    chunk3(n)

                pe.wait_ge(z_free_a.sem, z_free_a.at(l, 14))
                pe.wait_ge(ml_rows.sem, ml_rows.at(l, 1))
                for t in range(TILES):
                    mm = nc.tensor.transpose(flat[:, t * P:(t + 1) * P], ra[:, t * P:(t + 1) * P], ident)
                mm.then_inc(ml_tr.sem, 1)
                for t in range(TILES):
                    mm = nc.tensor.transpose(flat[:, 1536 + t * P:1536 + (t + 1) * P], rb[:, t * P:(t + 1) * P], ident)
                mm.then_inc(ml_tr.sem, 1)
                for i, squares in enumerate(((lsq_b[:, 0], lsq_b[:, 1]), (lsq_a[:, :],))):
                    pe.wait_ge(c_sq.sem, c_sq.at(l, i + 1))
                    for c, sq in enumerate(squares):
                        for t in range(TILES):
                            mm = MM(ps[:, 6, 16 * i + t:16 * i + t + 1], sq[:, t * P:(t + 1) * P], ones[:, 0:1],
                                    start=(c == 0 and t == 0), stop=(c == len(squares) - 1), skip_group_check=True)
                mm.then_inc(c_sum.sem, 1)
                pe.wait_ge(ml_dexp.sem, ml_dexp.at(l, 1))
                pe.wait_ge(ml_in.sem, ml_in.at(l, 16))
                for dj in range(4):
                    mm = MM(ps[:, 7, dj * TILES:(dj + 1) * TILES], mc[0:DH, M_PAIR + dj * P:M_PAIR + (dj + 1) * P],
                            mrow[:, 3, :], start=True, stop=True)
                mm.then_inc(ml_dmm.sem, 1)
                pe.wait_ge(ml_cols.sem, ml_cols.at(l, 1))
                for t in range(TILES):
                    if t >= 2:
                        pe.wait_ge(ml_kv_a.sem, ml_kv_a.at(l, t - 1))
                        pe.wait_ge(ml_kv_v.sem, ml_kv_v.at(l, t - 1))
                    for c in range(4):
                        mm = nc.tensor.transpose(ps[:, t % 2 + 2 * (c // 2), (c % 2) * P:(c % 2 + 1) * P], zc(Z_K + c)[:, t * P:(t + 1) * P], ident)
                    mm.then_inc(ml_kvt.sem, 1)
                    if t == 1:
                        pe.wait_ge(c_diag.sem, c_diag.at(l, 1))
                        for t_ in range(TILES):
                            mm = MM(flat[:, 2048 + t_ * P:2048 + (t_ + 1) * P], ones, diag[:, t_, :], start=True, stop=True)
                        mm.then_inc(c_row.sem, 1)
                pe.wait_ge(cq_ok.sem, cq_ok.at(l, 1))
                for t in range(TILES):
                    mm = MM(flat[:, 2048 + t * P:2048 + (t + 1) * P], ones, diag2[:, t, :], start=True, stop=True)
                mm.then_inc(c_row.sem, 1)
                pe.wait_ge(ml_kv_v.sem, ml_kv_v.at(l, TILES))
                pe.wait_ge(ml_kv_a.sem, ml_kv_a.at(l, TILES))
                for t in range(TILES):
                    mm = nc.tensor.transpose(flat[:, t * P:(t + 1) * P], zc(Z_MISC)[:, t * P:(t + 1) * P], ident)
                mm.then_inc(kr_t.sem, 1)
                pe.wait_ge(at_krt.sem, at_krt.at(l, 1))
                pe.wait_ge(ml_kv_v.sem, ml_kv_v.at(l, TILES))
                pe.wait_ge(ml_kv_a.sem, ml_kv_a.at(l, TILES))
                pe.wait_ge(ml_zero.sem, ml_zero.at(l, 1))

                def both(i):
                    return enumerate((i, (TILES - i) % TILES))

                def offsets(i):
                    if i:
                        pe.wait_ge(ml_em.sem, ml_em.at(l, 2 * i))
                    for d, t in both(i):
                        for h in range(HEADS_M):
                            sel = mc[0:DH, M_SEL + (4 * d + h) * P:M_SEL + (4 * d + h + 1) * P]
                            mm = MM(ps[:, d, h * P:(h + 1) * P], sel, rr[:, t * P:(t + 1) * P], start=True, stop=True)
                        mm.then_inc(ml_bc.sem, 1)

                def key_query(i):
                    if i:
                        pe.wait_ge(ml_s.sem, ml_s.at(l, 2 * i))
                    for d, t in both(i):
                        ts = slice(t * P, (t + 1) * P)
                        for h in range(HEADS_M):
                            half, at0 = slice(DH * (h % 2), DH * (h % 2) + DH), 2 * P * d + P * (h // 2)
                            mm = MM(ps[:, 2 + h % 2, at0:at0 + P], zc(Z_K + h // 2)[half, ts], zc(Z_Q + h // 2)[half, ts],
                                    start=True, stop=True)
                    mm.then_inc(ml_qk.sem, 1)

                offsets(0)
                key_query(0)
                pe.wait_ge(ml_c0.sem, ml_c0.at(l, 16))
                for i in range(TILES):
                    if i:
                        pe.wait_ge(ml_out.sem, ml_out.at(l, 2 * i))
                    for d, t in both(i):
                        for h in range(HEADS_M):
                            half, at0 = slice(DH * (h % 2), DH * (h % 2) + DH), 130 * d + 65 * (h // 2)
                            MM(ps[:, 4 + h % 2, at0:at0 + 65], zc(Z_Q + h // 2)[half, t * P:(t + 1) * P],
                               cst_st[half, min(i, 1), d, h // 2, :], start=True, stop=True)
                    for d, t in both(i):
                        pe.wait_ge(ml_kw.sem, ml_kw.at(l, 2 * i + d + 1))
                        for h in range(HEADS_M):
                            half = slice(DH * (h % 2), DH * (h % 2) + DH)
                            MM(ps[half, 6 + d, 260 + 65 * (h // 2):325 + 65 * (h // 2)], kw[:, d, h, :], vaug[:, t, h, :],
                               start=True, stop=True)
                    if i + 1 < TILES:
                        offsets(i + 1)
                    for d, t in both(i):
                        pe.wait_ge(ml_s.sem, ml_s.at(l, 2 * i + d + 1))
                        for h in range(HEADS_M):
                            mm = MM(ps[:, 6 + d, h * 65:(h + 1) * 65], sp_[:, d, h, :], vaug[:, t, h, :], start=True, stop=True)
                        mm.then_inc(ml_pv.sem, 1)
                    if i + 1 < TILES:
                        key_query(i + 1)
                pe.wait_ge(ml_out.sem, ml_out.at(l, 2 * TILES))
                for b in range(NB):
                    for c in range(2):
                        mm = MM(ps[:, 5 + b, 0:BLK], ones, csq[:, c, b * BLK:(b + 1) * BLK], start=(c == 0), stop=(c == 1))
                mm.then_inc(cv_sum.sem, 1)

                def last_modulation(first, last):
                    for m in range(first, last):
                        pe.wait_ge(ada3_in[m % 4].sem, ada3_in[m % 4].at(l, 16 * (m // 4 + 1)))
                        modulation(3, m, wada_l[:, m % 4]).then_inc(ada3_used.sem, 1)

                pe.wait_ge(cv_sq.sem, cv_sq.at(l, 1))
                for c in range(2):
                    for t in range(TILES):
                        mm = MM(ps[:, 4, t:t + 1], cvsq[:, c, t * P:(t + 1) * P], ones[:, 0:1],
                                start=(c == 0 and t == 0), stop=(c == 1), skip_group_check=True)
                mm.then_inc(cv_sum.sem, 1)
                last_modulation(0, 2)
                pe.wait_ge(ml_h.sem, ml_h.at(l, 1))
                pe.wait_ge(cv_diag.sem, cv_diag.at(l, 1))
                for c in range(2):
                    for t in range(TILES):
                        mm = nc.tensor.transpose(flat[:, 2048 * c + t * P:2048 * c + (t + 1) * P],
                                                 hnum[:, t, 2 * c:2 * c + 2, :].rearrange("p h d -> p (h d)"), ident)
                mm.then_inc(ml_ht.sem, 1)
                last_modulation(2, 4)
                pe.wait_ge(ml_done.sem, ml_done.at(l, 1))
                for t in range(TILES):
                    mm = MM(flat[:, 2560 + t * P:2560 + (t + 1) * P], ones, diag[:, t, :], start=True, stop=True)
                mm.then_inc(cv_row.sem, 1)

                def pointwise(o):
                    if o == 0:
                        pe.wait_ge(cv_act.sem, cv_act.at(l, 1))
                        pe.wait_ge(pw_in.sem, pw_in.at(l, 16))
                    else:
                        pe.wait_ge(cv_done.sem, cv_done.at(l, 1))
                    for b in range(NB):
                        for c in range(2):
                            mm = MM(ps[:, 5 + b, 0:BLK], pw[:, c, o, :], csq[:, c, b * BLK:(b + 1) * BLK],
                                    start=(c == 0), stop=(c == 1))
                    mm.then_inc(cv_pw.sem, 1)


                def proj_q(h, e, j):
                    pe.wait_ge(hw_in[e].sem, hw_in[e].at(l, j * 16 + 16))
                    if isinstance(h, int) and h == 0:
                        pe.wait_ge(at_in.sem, at_in.at(l, 48))
                    else:
                        pe.wait_ge(at_lk.sem, at_lk.at(l, h))
                    for t in range(TILES):
                        for c in range(2):
                            mm = MM(ps[:, t // 5, (t % 5) * QK:(t % 5 + 1) * QK], zc(Z_CQ + c)[:, t * P:(t + 1) * P],
                                    hw[:, e, c * QK:(c + 1) * QK], start=(c == 0), stop=(c == 1))
                    mm.then_inc(at_pq.sem, 1)

                def proj_k(h, e):
                    pe.wait_ge(at_tq.sem, at_tq.at(l, h + 1))
                    for t in range(KTILES):
                        lat = zc(Z_CKV)[:, t * P:(t + 1) * P] if t < TILES else ctxk[:, :]
                        mm = MM(flat[:, t * P:(t + 1) * P], lat, hw[:, e, 2 * QK:2 * QK + P], start=True, stop=True)
                    mm.then_inc(at_pk.sem, 1)

                def turn_q(h):
                    pe.wait_ge(at_rope.sem, at_rope.at(l, h + 1))
                    for t in range(TILES):
                        mm = nc.tensor.transpose(flat[0:QK, t * P:(t + 1) * P], qk[:, t, :], ident)
                    mm.then_inc(at_trq.sem, 1)

                def turn_k(h):
                    pe.wait_ge(at_lq.sem, at_lq.at(l, h + 1))
                    for t in range(KTILES):
                        mm = nc.tensor.transpose(flat[0:QK, t * P:(t + 1) * P], qk[:, TILES + t, :], ident)
                    mm.then_inc(at_trk.sem, 1)

                def max_unit(h, e, u, more):
                    if u < 3:
                        pe.wait_ge(at_lk.sem, at_lk.at(l, h + 1))
                        if more:
                            pe.wait_ge(at_tk.sem, at_tk.at(l, h + 2))
                    else:
                        pe.wait_ge(at_mx.sem, at_head(at_mx, UNITS, l, h, u - 2))
                    t = (u + NB - 1) // NB
                    keys = slice(0, SEQ) if t == 0 else slice(SEQ + (u - 1) % NB * BLK, SEQ + ((u - 1) % NB + 1) * BLK)
                    MM(ps[:, u % 3, 0:keys.stop - keys.start], qh[e][0:QK, t * P:(t + 1) * P], kh[e][0:QK, keys],
                       start=True, stop=True).then_inc(at_s.sem, 1)

                def max_rows(h):
                    pe.wait_ge(at_nm.sem, at_nm.at(l, h + 1))
                    for t in range(TILES):
                        mm = MM(flat[QK:QK + 1, t * P:(t + 1) * P], nmx[:, t:t + 1], ident, start=True, stop=True)
                    mm.then_inc(at_mrow.sem, 1)

                steps = [(0, 0, SEQ, 0)] + [(1 + qb, *PARTS[1 + qb], kt0) for qb in range(2) for kt0 in range(1, KTILES)]

                def head(h, e, part, i1, i2):
                    def pv(s):
                        o, _, n, kt0 = steps[s]
                        if kt0 <= 1:
                            pe.wait_ge(at_y.sem, at_head(at_y, 3, l, h, o - 1))
                        if s == 0:
                            pe.wait_ge(at_va.sem, at_va.at(l, h + 1))
                        pe.wait_ge(at_exp.sem, at_head(at_exp, STEPS, l, h, s + 1))
                        MM(ps[:, 6 + (e + o) % 2, 0:n], va[e][:, kt0, :], pt[:, s % 3, 0:n], start=(kt0 <= 1),
                           stop=(kt0 == 0 or kt0 == KTILES - 1)).then_inc(at_pv.sem, 1)

                    if part is FIRST:
                        pe.wait_ge(at_mlo.sem, at_mlo.at(l, h + 1))
                        pe.wait_ge(at_mhi.sem, at_mhi.at(l, h + 1))
                    for s in part:
                        o, q0, n, kt0 = steps[s]
                        if s >= 3:
                            pe.wait_ge(at_exp.sem, at_head(at_exp, STEPS, l, h, s - 2))
                        ks, qs = slice(kt0 * P, (kt0 + 1) * P), slice(q0, q0 + n)
                        MM(ps[:, 3 + s % 3, 0:n], kh[e][0:QK + 1, ks], qh[e][0:QK + 1, qs], start=True, stop=False)
                        MM(ps[:, 3 + s % 3, 0:n], kh[e][0:QK + 1, ks], ql[e][0:QK + 1, qs], start=False, stop=False)
                        MM(ps[:, 3 + s % 3, 0:n], kl[e][0:QK + 1, ks], qh[e][0:QK + 1, qs], start=False, stop=True).then_inc(at_st.sem, 1)
                        if i1 and s == S_TRQ:
                            turn_q(h + 1)
                        if i1 and s == S_TRK:
                            turn_k(h + 1)
                        if i2 is not None and s == S_PQ:
                            proj_q(h + 2, e, i2)
                        if i2 is not None and s == S_PK:
                            proj_k(h + 2, e)
                        units = units_beside(s) if i1 else ()
                        for u in units[:len(units) // 2]:
                            max_unit(h + 1, 1 - e, u, i2 is not None)
                        if i1 and s == S_ROW:
                            max_rows(h + 1)
                        if s >= 2:
                            pv(s - 2)
                        for u in units[len(units) // 2:]:
                            max_unit(h + 1, 1 - e, u, i2 is not None)
                    if part is LATER:
                        pv(STEPS - 2)
                        pv(STEPS - 1)

                proj_q(0, 0, 0)
                pointwise(0)
                proj_k(0, 0)
                last_modulation(4, 6)
                pe.wait_ge(at_k1.sem, at_k1.at(l, 1))
                turn_q(0)
                last_modulation(6, 7)
                turn_k(0)
                last_modulation(7, LAST)
                pointwise(1)
                proj_q(1, 1, 0)
                proj_k(1, 1)
                for u in range(UNITS):
                    max_unit(0, 0, u, True)
                max_rows(0)
                pe.wait_ge(cv_done.sem, cv_done.at(l, 2))
                pe.wait_ge(mod_ok.sem, mod_ok.at(l, 1))
                head(0, 0, FIRST, True, 1)
                with pe.Fori(0, H // 2 - 1) as i:
                    for e in range(2):
                        head(i * 2 + e, e, LATER, True, i + 1)
                        head(i * 2 + (e + 1), 1 - e, FIRST, True, None)
                head(H - 2, 0, LATER, True, None)
                head(H - 1, 1, FIRST, False, None)
                head(H - 1, 1, LATER, False, None)

                for n in range(16, 24):
                    chunk3(n)
                    if n > 16:
                        sums(1, n - 17)
                sums(1, KC - 1)
                pe.wait_ge(z_free_d.sem, z_free_d.at(l, 10))
                rows(1)
                pe.wait_ge(rs_rows.sem, rs_rows.at(l, 2))

                def unit_part(v, part, k):
                    f, b = v // NB, v % NB
                    whi, wlo = gu_hi[:, f, part, k, :], gu_lo[:, f, part, k, :]
                    for j, (w, a) in enumerate(((whi, a_hi), (whi, a_lo), (wlo, a_hi))):
                        mm = MM(ps[:, 2 * (v % 2) + part, 0:BLK], w, a[:, k, b * BLK:(b + 1) * BLK],
                                start=(k == 0 and j == 0), stop=(k == KC - 1 and j == 2))
                    return mm

                def unit(v, g):
                    f = v // NB
                    pe.wait_ge(f_lo_ok.sem, f_lo_ok.at(l, g * 6 + 2 * (f + 1)))
                    pe.wait_ge(f_hi_ok.sem, f_hi_ok.at(l, g * 6 + 2 * (f + 1)))
                    if v or not isinstance(g, int) or g:
                        pe.wait_ge(f_act.sem, f_act.at(l, g * 6 + (v - 1)))
                    for part in range(2):
                        for k in range(KC):
                            mm = unit_part(v, part, k)
                    mm.then_inc(f_gu.sem, 1)

                def down(g):
                    pe.wait_ge(f_act.sem, f_act.at(l, g * 6 + 6))
                    pe.wait_ge(f_lo_ok.sem, f_lo_ok.at(l, g * 6 + 6))
                    pe.wait_ge(f_hi_ok.sem, f_hi_ok.at(l, g * 6 + 6))
                    for o in range(KC):
                        for b in range(NB):
                            n = o * NB + b
                            pe.wait_ge(f_res.sem, f_res.at(l, g * 24 + max(n - 3, 0)))
                            bs, os_ = slice(b * BLK, (b + 1) * BLK), slice(o * P, (o + 1) * P)
                            for f in range(2):
                                for j, (w, a) in enumerate(((d_hi, g_hi), (d_hi, g_lo), (d_lo, g_hi))):
                                    mm = MM(ps[:, 4 + n % 4, 0:BLK], w[:, f, os_], a[:, f, bs],
                                            start=(f == 0 and j == 0), stop=(f == 1 and j == 2))
                            mm.then_inc(f_dn.sem, 1)

                def group(g, v0):
                    for v in range(v0, 6):
                        unit(v, g)
                    unit(0, g + 1)
                    down(g)

                pe.wait_ge(f_lo_ok.sem, f_lo_ok.at(l, 2))
                for k in range(KC):
                    halves_ok(1, k)
                    for v in range(2):
                        for part in range(2):
                            mm = unit_part(v, part, k)
                        if k == KC - 1:
                            mm.then_inc(f_gu.sem, 1)
                group(0, 2)
                with pe.Fori(0, NG - 2) as g:
                    group(g + 1, 1)
                for v in range(1, 6):
                    unit(v, NG - 1)
                down(NG - 1)

        @block.scalar
        def _(act):
            act.wait_ge(const_in.sem, 48)
            A(cond[:, :, :], cond[:, :, :], ACT.Silu).then_inc(cond_ok.sem, 1)
            with act.Fori(0, DEPTH) as l:
                own = Chain(act, act_own, l)

                def root(n, k):
                    act.wait_ge(rs_var.sem, rs_var.at(l, k))
                    A(small[:, 20:20 + n], small[:, 0:n], ACT.Sqrt).then_inc(rs_root.sem, 1)

                def square(which, c):
                    if which:
                        act.wait_ge(z_free_d.sem, z_free_d.at(l, 2 + c + 1))
                    if c >= 2:
                        act.wait_ge(sq_used.sem, sq_used.at(l, which * KC + c - 1))
                    A(nsq[:, c % 2, :], x[:, c, :], ACT.Square).then_inc(sq_ok.sem, 1)

                def norm(which):
                    act.wait_ge(rs_var.sem, rs_var.at(l, (1, 4)[which]))
                    A(normed[:, 1, :], normed[:, 0, :], ACT.Sqrt).then_inc(rs_root.sem, 1)
                    act.wait_ge(rs_row.sem, rs_row.at(l, which + 1))
                    A(blocks(inv_rows[:, :]), banks(0), ACT.Copy).then_inc(rs_rows.sem, 1)

                def highs(which):
                    for c in range(KC):
                        act.wait_ge(nh_ok.sem, nh_ok.at(l, which * KC + c + 1))
                        if c % 2:
                            ins = A(a_hi[:, c, :], nt[:, 1, :], ACT.Copy)
                        else:
                            for s, part in REQUESTS:
                                ins = A(a_hi[:, c, part], nt[:, 0, part], ACT.Identity, bias=mod[:, 24 * which + c, s:s + 1])
                        ins.then_inc(ahi_ok.sem, 1)

                def w_high(n):
                    act.wait_ge(w_in_[n % 2].sem, w_in_[0].at(l, 16 * (n // 2 + 1)))
                    if n >= 2:
                        act.wait_ge(w_used.sem, w_used.at(l, n - 1))
                    A(w_hi[:, n % 2, :], w_raw[:, n % 2, :], ACT.Copy).then_inc(w_hi_ok.sem, 1)

                act.wait_ge(f_res.sem, f_res.at(l, 0))
                for c in range(KC):
                    square(0, c)
                    if c == 3:
                        act.wait_ge(crow_in.sem, crow_in.at(l, 16))
                        A(crow[:, :, :], crow[:, :, :], ACT.Silu).then_inc(crow_ok.sem, 1)
                norm(0)
                w_high(0)
                w_high(1)
                highs(0)
                for n in range(16):
                    src = banks(3 * (n % 2))
                    if n < 4:
                        if n % 2 == 0:
                            act.wait_ge(w_used.sem, w_used.at(l, n + 1))
                            if n:
                                act.wait_ge(z_free_d.sem, z_free_d.at(l, 1))
                            A(blocks(sigb[:, :]), src, ACT.Sigmoid).then_inc(z_free_a.sem, 1)
                    else:
                        act.wait_ge(w_used.sem, w_used.at(l, n + 1))
                        if n == 5:
                            act.wait_ge(spilled.sem, spilled.at(l, 32))
                        if n == 9:
                            act.wait_ge(ada2_used.sem, ada2_used.at(l, LATE))
                        c = Z_MISC if n == 4 else n - 5
                        A(blocks(zc(c)), src, ACT.Copy, scale=SCALE_M if c < Z_K else 1.0).then_inc(z_free_a.sem, 1)
                    if n + 2 < 16:
                        w_high(n + 2)
                    if n == 13:
                        act.wait_ge(cv_y.sem, cv_y.at(l, 1))
                        act.wait_ge(z_free_a.sem, z_free_a.at(l, 3))
                        misc = zc(Z_MISC)
                        bg = vecs[:, V_BG:V_BG + 1]
                        A(rb[0:DH, :], misc[0:DH, :], ACT.Identity, bias=bg[0:DH, :])
                        own.link(A(ra[0:DH, :], misc[DH:P, :], ACT.Abs, bias=bg[DH:P, :]))
                        own.link(A(ra[0:DH, :], ra[0:DH, :], ACT.Exp, scale=-1.0))
                        A(lf[:, :], ra[0:DH, :], ACT.Ln, bias=ones[0:DH, 0:1]).then_inc(ml_ln.sem, 1)

                act.wait_ge(w_used.sem, w_used.at(l, 16))
                act.wait_ge(z_free_a.sem, z_free_a.at(l, 14))
                A(lsq_b[:, :, :], z2[:, 0:2, :], ACT.Square).then_inc(c_sq.sem, 1)
                A(lsq_a[:, :], z2[:, 2, :], ACT.Square).then_inc(c_sq.sem, 1)
                act.wait_ge(ml_rows.sem, ml_rows.at(l, 1))
                A(mrow[:, 3, :], mrow[:, 2, :], ACT.Exp).then_inc(ml_dexp.sem, 1)

                def turned(half, row):
                    return flat[:, 1536 * half:1536 * half + TOK].rearrange("p (t q c) -> p t q c", q=4, c=32)[
                        :, :, 2 * row:2 * row + 2, 0:HEADS_M]

                def by_head(ap):
                    return ap.rearrange("p t (d h) -> p t d h", d=2)

                act.wait_ge(ml_tr.sem, ml_tr.at(l, 2))
                A(by_head(cols[:, 0]), turned(0, 0), ACT.Copy)
                A(by_head(cols[:, 1]), turned(0, 1), ACT.Exp)
                A(by_head(cols[:, 2]), turned(1, 0), ACT.Exp)
                A(by_head(cols[:, 3]), turned(1, 1), ACT.Exp, scale=-1.0).then_inc(ml_cols.sem, 1)
                root(2 * TILES, 2)
                for t in range(TILES):
                    act.wait_ge(ml_kvt.sem, ml_kvt.at(l, t + 1))
                    A(kt[:, t, :], ps[:, t % 2, 0:2 * P], ACT.Copy).then_inc(ml_kv_a.sem, 1)
                act.wait_ge(ml_cols.sem, ml_cols.at(l, 1))
                for i in range(TILES):
                    for d, t in enumerate((i, (TILES - i) % TILES)):
                        act.wait_ge(ml_em.sem, ml_em.at(l, 2 * i + d + 1))
                        for h in range(HEADS_M):
                            aa = A(em[:, d, h, :], em[:, d, h, :], ACT.Exp, bias=cols[:, 0, t, 4 * d + h:4 * d + h + 1])
                        aa.then_inc(ml_exp.sem, 1)
                for c in range(2):
                    A(zc(Z_O + c), zc(Z_O + c), ACT.Sigmoid).then_inc(ml_og.sem, 1)
                act.wait_ge(ml_hsum.sem, ml_hsum.at(l, 1))
                A(hsq[:, :, :].rearrange("p (t h) d -> p t (h d)", h=4), hnum[:, :, 0:4, :].rearrange("p t h d -> p t (h d)"),
                  ACT.Square).then_inc(ml_hsq.sem, 1)
                act.wait_ge(cv_xc.sem, cv_xc.at(l, 1))
                A(cvsq[:, :, :], csq[:, :, :], ACT.Square).then_inc(cv_sq.sem, 1)
                act.wait_ge(ml_var.sem, ml_var.at(l, 1))
                A(den[:, 2, :, 0:4], den[:, 1, :, 0:4], ACT.Sqrt).then_inc(ml_root.sem, 1)
                root(TILES, 3)
                for c in range(2):
                    act.wait_ge(ml_y.sem, ml_y.at(l, c + 1))
                    A(a_hi[:, c, :], yt[:, :], ACT.Copy).then_inc(ml_yhi.sem, 1)
                act.wait_ge(cv_n.sem, cv_n.at(l, 1))
                for c in range(2):
                    aa = A(csq[:, c, :], csq[:, c, :], ACT.Silu, bias=vecs[:, V_LNB + c:V_LNB + c + 1],
                           scale=vecs[:, V_LNG + c:V_LNG + c + 1])
                aa.then_inc(cv_act.sem, 1)

                def pointwise_high(o):
                    act.wait_ge(cv_pw.sem, cv_pw.at(l, o + 1))
                    A(blocks(a_hi[:, 2 + o, :]), banks(5), ACT.Copy).then_inc(cv_hi.sem, 1)

                act.wait_ge(at_krt.sem, at_krt.at(l, 1))

                def first_q(h):
                    act.wait_ge(at_pq.sem, at_pq.at(l, h + 1))
                    A(qk[:, 0:5, :], ps[:, 0, 0:5 * QK].rearrange("p (t n) -> p t n", n=QK), ACT.Copy)
                    A(qk[:, 5:9, :], ps[:, 1, 0:4 * QK].rearrange("p (t n) -> p t n", n=QK), ACT.Copy).then_inc(at_tq.sem, 1)

                def first_k(h):
                    act.wait_ge(at_pk.sem, at_pk.at(l, h + 1))
                    kv = flat[:, 0:KEYS].rearrange("p (t n) -> p t n", n=P)
                    A(qk[:, TILES:, NOPE:QK], krt[:, :, :], ACT.Copy)
                    own.inc(A(qk[:, TILES:, 0:NOPE], kv[:, :, 0:NOPE], ACT.Copy))
                    A(vt[:, :, :], kv[:, :, NOPE:P], ACT.Copy).then_inc(at_tk.sem, 1)
                    own.settle()
                    A(sq_[:, :, :], qk[:, :, :], ACT.Square).then_inc(at_sq.sem, 1)

                def values(h, e):
                    act.wait_ge(at_tk.sem, at_tk.at(l, h + 1))
                    if not isinstance(h, int) or h >= 2:
                        act.wait_ge(at_pv.sem, at_head(at_pv, STEPS, l, h, -STEPS))
                    A(va[e][:, :, 0:V_DIM], vt[:, :, :], ACT.Copy).then_inc(at_va.sem, 1)

                def first_root(h):
                    act.wait_ge(at_sum.sem, at_sum.at(l, h + 1))
                    own.link(A(small[:, 20:39], small[:, 0:19], ACT.Ln))
                    A(small[:, 40:59], small[:, 20:39], ACT.Exp, scale=-0.5).then_inc(at_root.sem, 1)

                def high_q(h, e):
                    act.wait_ge(at_trq.sem, at_trq.at(l, h + 1))
                    A(qh[e][0:QK, :], flat[0:QK, 0:TOK], ACT.Copy, scale=vecs[0:QK, V_QC:V_QC + 1]).then_inc(at_hq.sem, 1)

                def high_k(h, e):
                    act.wait_ge(at_trk.sem, at_trk.at(l, h + 1))
                    A(kh[e][0:QK, :], flat[0:QK, 0:KEYS], ACT.Copy, scale=vecs[0:QK, V_KC:V_KC + 1]).then_inc(at_hk.sem, 1)

                def high_rows(h, e):
                    act.wait_ge(at_mrow.sem, at_mrow.at(l, h + 1))
                    A(qh[e][QK:QK + 1, :], flat[QK:QK + 1, 0:TOK], ACT.Copy).then_inc(at_mhi.sem, 1)

                def yhigh(h, e, i0, o):
                    act.wait_ge(at_y.sem, at_head(at_y, 3, l, h, o + 1))
                    q0, n = PARTS[o]
                    half = slice(DH * e, DH * e + DH)
                    A(a_hi[half, bass.ds(i0 + 4, 1), q0:q0 + n], ya[half, (e + o) % 2, 0:n].unsqueeze(1), ACT.Copy).then_inc(at_yhi.sem, 1)

                def head(h, e, i0, part, i1, i2, before=None):
                    for s in part:
                        n = SEQ if s == 0 else 512
                        act.wait_ge(at_st.sem, at_head(at_st, STEPS, l, h, s + 1))
                        act.wait_ge(at_pv.sem, at_head(at_pv, STEPS, l, h, max(s - 2, 0)))
                        A(pt[:, s % 3, 0:n], ps[:, 3 + s % 3, 0:n], ACT.Exp, scale=SCALE_A).then_inc(at_exp.sem, 1)
                        if i1 and s == S_TRQ:
                            high_q(h + 1, 1 - e)
                            values(h + 1, 1 - e)
                        if before is not None and s == 2:
                            yhigh(h - 1, 1 - e, before, 2)
                        if i1 and s == S_TRK:
                            high_k(h + 1, 1 - e)
                        if i1 and s == S_ROW:
                            high_rows(h + 1, 1 - e)
                        if i2 and s == S_PQ:
                            first_q(h + 2)
                        if i2 and s == S_PK:
                            first_k(h + 2)
                        if i2 and s == S_ROOT:
                            first_root(h + 2)
                        if s == 6:
                            yhigh(h, e, i0, 0)
                        if s == 16:
                            yhigh(h, e, i0, 1)
                        if isinstance(h, int) and h == H - 1 and s in (8, 11):
                            w_high(16 + s // 11)

                first_q(0)
                pointwise_high(0)
                first_k(0)
                first_root(0)
                act.wait_ge(at_k1.sem, at_k1.at(l, 1))
                values(0, 0)
                high_q(0, 0)
                high_k(0, 0)
                pointwise_high(1)
                first_q(1)
                first_k(1)
                first_root(1)
                high_rows(0, 0)
                head(0, 0, 0, FIRST, True, True)
                with act.Fori(0, H // 2 - 1) as i:
                    own.enter(i, 16)
                    for e in range(2):
                        head(i * 2 + e, e, i, LATER, True, True)
                        head(i * 2 + (e + 1), 1 - e, i, FIRST, True, True, before=i)
                    own.leave(H // 2 - 1)
                head(H - 2, 0, H // 2 - 1, LATER, True, False)
                head(H - 1, 1, H // 2 - 1, FIRST, False, False, before=H // 2 - 1)
                head(H - 1, 1, H // 2 - 1, LATER, False, False)
                yhigh(H - 1, 1, H // 2 - 1, 2)

                for n in range(16, 24):
                    if n + 2 < 24:
                        w_high(n + 2)
                    square(1, n - 16)
                act.wait_ge(w_used.sem, w_used.at(l, 24))

                def f_high(slot, count, dst, used_sem, used):
                    act.wait_ge(f_in[slot].sem, f_in[0].at(l, count))
                    if used_sem is not None:
                        act.wait_ge(used_sem.sem, used)
                    A(dst, f_raw[:, slot], ACT.Copy).then_inc(f_hi_ok.sem, 1)

                def silu(v, g):
                    act.wait_ge(f_gu.sem, f_gu.at(l, g * 6 + (v + 1)))
                    if v or not isinstance(g, int) or g:
                        act.wait_ge(f_act.sem, f_act.at(l, g * 6 + (v - 1)))
                    A(sg[:, v % 2, :], ps[:, 2 * (v % 2), 0:BLK], ACT.Silu).then_inc(f_silu.sem, 1)

                for n in range(2):
                    f_high(n, 16, gu_hi[:, 0, n], None, None)
                norm(1)
                for n in range(2):
                    f_high(n, 32, gu_hi[:, 1, n], None, None)
                highs(1)
                silu(0, 0)

                def group(g):
                    for n in range(2):
                        f_high(n, 32 + g * 48 + 16, d_hi[:, n], f_dn, f_dn.at(l, g * 24))
                    silu(1, g)
                    silu(2, g)
                    for n in range(2):
                        f_high(n, 32 + g * 48 + 32, gu_hi[:, 0, n], f_gu, f_gu.at(l, g * 6 + 3))
                    for v in range(3, 6):
                        silu(v, g)
                    for n in range(2):
                        f_high(n, 32 + g * 48 + 48, gu_hi[:, 1, n], f_gu, f_gu.at(l, g * 6 + 6))
                    silu(0, g + 1)

                group(0)
                with act.Fori(0, NG - 2) as g:
                    group(g + 1)
                for n in range(2):
                    f_high(n, 32 + (NG - 1) * 48 + 16, d_hi[:, n], f_dn, f_dn.at(l, (NG - 1) * 24))
                for v in range(1, 6):
                    silu(v, NG - 1)
                own.end_layer()

        @block.vector
        def _(dve):
            for s in (f_res, at_y, f_act):
                dve.sem_inc(s.sem, s.first)
            dve.wait_ge(const_in.sem, 48)
            with dve.Fori(0, DEPTH) as l:
                own = Chain(dve, dve_own, l)
                link = own.link
                TT, TS, STT = V.tensor_tensor, V.tensor_scalar, V.scalar_tensor_tensor

                dve.wait_ge(vec_in.sem, vec_in.at(l, 16))

                def modulation(c, weights, scratch):
                    for s in range(2):
                        if own.n > 1:
                            own.settle(1)
                        own.inc(V.tensor_tensor_reduce(scratch[s], weights, crow[:, s, :], 1.0, vecs[:, V_BADA + c:V_BADA + c + 1],
                                                       ALU.mult, ALU.add, mod[:, c, s:s + 1]))

                def norm_gain(w, vn):
                    scale = mod[:, 8 + 24 * w:16 + 24 * w, :]
                    link(STT(gain[:, w], scale, 1.0, spread(vecs[:, vn:vn + KC], 2), ALU.add, ALU.mult))

                def root(k, *groups):
                    for i, (sums, width) in enumerate(groups):
                        ins = TS(small[:, TILES * i:TILES * (i + 1)], sums, 1.0 / width, EPS, ALU.mult, ALU.add)
                    ins.then_inc(rs_var.sem, 1)
                    n = TILES * len(groups)
                    dve.wait_ge(rs_root.sem, rs_root.at(l, k))
                    link(V.reciprocal(small[:, 40:40 + n], small[:, 20:20 + n]))

                def diagonals(dst=diag, at=0):
                    return TT(dst[:, :, :], ident.unsqueeze(1).to_broadcast([P, TILES, P]), spread(small[:, 40 + at:40 + at + TILES], P), ALU.mult)

                row = flat[:, 0:TOK]

                def first_modulation(part):
                    dve.wait_ge(ada1_vin[part].sem, ada1_vin[part].at(l, 16))
                    for j in range(ADA_CUTS[part], ADA_CUTS[part + 1]):
                        modulation(ADA_PE + j, wada_v[:, j, :], (nt[:, 0, 0:D_MODEL], nt[:, 1, 0:D_MODEL]))

                def norm(which):
                    if which == 0:
                        dve.wait_ge(crow_ok.sem, crow_ok.at(l, 1))
                        first_modulation(0)
                    dve.wait_ge(sq_used.sem, sq_used.at(l, (which + 1) * KC))
                    TS(normed[:, 0, :], ps[0:32 * NB, 6, 0:BLK], 1.0 / D_MODEL, EPS, ALU.mult, ALU.add).then_inc(rs_var.sem, 1)
                    dve.wait_ge(rs_root.sem, rs_root.at(l, (1, 4)[which]))
                    V.reciprocal(normed[:, 2, :], normed[:, 1, :]).then_inc(rs_inv.sem, 1)
                    if which == 0:
                        dve.wait_ge(ada1_used.sem, ada1_used.at(l, 1))
                        first_modulation(1)
                        own.inc(TT(mod[:, 0:ADA_PE, :], ps[:, 7, 0:2 * ADA_PE].rearrange("p (j s) -> p j s", s=2),
                                   spread(vecs[:, V_BADA:V_BADA + ADA_PE], 2), ALU.add))
                        own.settle()
                        norm_gain(0, V_N1)
                    dve.wait_ge(rs_rows.sem, rs_rows.at(l, which + 1))

                    def normalised(c):
                        if c >= 2:
                            s = alo_ok[c % 2]
                            dve.wait_ge(s.sem, s.at(l, which * KC // 2 + c // 2))
                        for s, part in REQUESTS:
                            ins = STT(nt[:, c % 2, part], x[:, c, part], gain[:, which, c, s:s + 1], inv_rows[:, part], ALU.mult, ALU.mult)
                        if c % 2:
                            link(ins)
                            for s, part in REQUESTS:
                                ins = TS(nt[:, 1, part], nt[:, 1, part], mod[:, 24 * which + c, s:s + 1], None, ALU.add)
                        ins.then_inc(nh_ok.sem, 1)

                    normalised(0)
                    for c in range(0, KC, 2):
                        normalised(c + 1)
                        dve.wait_ge(ahi_ok.sem, ahi_ok.at(l, which * KC + c + 1))
                        for s, part in REQUESTS:
                            ins = STT(a_lo[:, c, part], nt[:, 0, part], mod[:, 24 * which + c, s:s + 1],
                                      a_hi[:, c, part].bitcast(F32), ALU.add, ALU.subtract)
                        ins.then_inc(alo_ok[0].sem, 1)
                        if c + 2 < KC:
                            normalised(c + 2)

                dve.wait_ge(f_res.sem, f_res.at(l, 0))
                norm(0)
                for s in alo_ok:
                    dve.wait_ge(s.sem, s.at(l, KC // 2))
                link(V.memset(u[:, :, :], 0.0))

                def late_modulation(first, last):
                    for m in range(first, last):
                        dve.wait_ge(ada2_in[m % 4].sem, ada2_in[m % 4].at(l, 16 * (m // 4 + 1)))
                        modulation(16 + m, wada_z[:, m % 4, 0:D_MODEL], (yc[:, 0, 0:D_MODEL], yc[:, 1, 0:D_MODEL]))
                        own.settle()
                        dve.sem_inc(ada2_used.sem, 1)

                for c in range(2):
                    late_modulation((0, 5)[c], (5, 16)[c])
                    dve.wait_ge(w_used.sem, w_used.at(l, 2 * c + 2))
                    dve.wait_ge(z_free_a.sem, z_free_a.at(l, c + 1))
                    b0, at0 = 3, SEG + CONV_PAD
                    TT(u[:, c, CONV_PAD:CONV_PAD + SEQ], ps[:, b0, 0:SEQ], sigb[:, 0:SEQ], ALU.mult)
                    TT(u[:, c, at0:at0 + BLK - SEQ], ps[:, b0, SEQ:BLK], sigb[:, SEQ:BLK], ALU.mult)
                    TT(blocks(u[:, c, at0 + BLK - SEQ:at0 + DEC_SEQ]), banks(b0 + 1, 2), blocks(sigb[:, BLK:TOK]),
                       ALU.mult).then_inc(z_free_d.sem, 1)

                late_modulation(16, LATE)
                norm_gain(1, V_N2)
                dve.wait_ge(z_free_d.sem, z_free_d.at(l, 2))
                for k in range(CONV_WIDTH):
                    for c in range(2):
                        tap = vecs[:, V_DW + c * CONV_WIDTH + k:V_DW + c * CONV_WIDTH + k + 1]
                        if k == 0:
                            own.inc(TS(yc[:, c, 0:Y_LEN], u[:, c, 0:Y_LEN], tap, vecs[:, V_DWB + c:V_DWB + c + 1], ALU.mult, ALU.add))
                        elif k < CONV_WIDTH - 1:
                            own.settle(1)
                            own.inc(STT(yc[:, c, 0:Y_LEN], u[:, c, k:k + Y_LEN], tap, yc[:, c, 0:Y_LEN], ALU.mult, ALU.add))
                        else:
                            own.settle()
                            STT(csq[:, c, 0:SEQ], u[:, c, k:k + SEQ], tap, yc[:, c, 0:SEQ], ALU.mult, ALU.add)
                            ins = STT(csq[:, c, SEQ:TOK], u[:, c, SEG + k:SEG + k + DEC_SEQ], tap, yc[:, c, SEG:SEG + DEC_SEQ],
                                      ALU.mult, ALU.add)
                ins.then_inc(cv_y.sem, 1)
                dve.wait_ge(ml_reset.sem, ml_reset.at(l, 16))
                dve.wait_ge(ml_ln.sem, ml_ln.at(l, 1))
                V.memset(mrow[:, 0:2, :], 0.0)
                link(V.memset(rr[:, :], 0.0))
                link(TS(ra[0:DH, :], zc(Z_MISC)[DH:P, :], vecs[DH:P, V_BG:V_BG + 1], 0.0, ALU.add, ALU.min))
                link(TT(lf[:, :], ra[0:DH, :], lf[:, :], ALU.subtract))
                for r0, back in ((0, False), (32, True)):
                    rows = slice(r0, r0 + HEADS_M)

                    def way(ap):
                        return ap[:, ::-1] if back else ap

                    V.tensor_tensor_scan(way(ra[rows, :]), way(reset[rows, :]), way(lf[rows, :]), 0.0, ALU.mult, ALU.add)
                    V.tensor_tensor_scan(way(rr[rows, 0:SEQ]), way(lf[rows, 0:SEQ]), way(rb[rows, 0:SEQ]), 0.0, ALU.add, ALU.max)
                    ins = V.tensor_tensor_scan(way(rr[rows, SEQ:TOK]), way(lf[rows, SEQ:TOK]), way(rb[rows, SEQ:TOK]),
                                               vecs[rows, V_M0:V_M0 + 1], ALU.add, ALU.max)
                link(ins)

                def tiled(ap):
                    return ap.rearrange("p (t n) -> p t n", n=P)

                fw, bw = slice(0, HEADS_M), slice(32, 32 + HEADS_M)
                V.tensor_copy(rb[DH:P, :], rr[:, :])
                V.tensor_copy(mrow[fw, 0, 1:2], vecs[fw, V_M0:V_M0 + 1])
                V.tensor_copy(mrow[bw, 0, TILES - 1:TILES], vecs[bw, V_M0:V_M0 + 1])
                V.tensor_copy(mrow[fw, 0, 2:TILES], tiled(rr[fw, :])[:, 1:TILES - 1, P - 1])
                link(V.tensor_copy(mrow[bw, 0, 1:TILES - 1], tiled(rr[bw, :])[:, 2:TILES, 0]))
                link(TT(rr[:, :], ra[0:DH, :], rr[:, :], ALU.subtract))
                V.tensor_copy(mrow[fw, 1, :], tiled(rr[fw, :])[:, :, P - 1])
                V.tensor_copy(mrow[bw, 1, :], tiled(rr[bw, :])[:, :, 0])
                link(TT(ra[0:DH, :], rb[0:DH, :], ra[0:DH, :], ALU.subtract))
                TT(mrow[:, 2, :], mrow[:, 0, :], mrow[:, 1, :], ALU.add)
                TT(tiled(ra[DH:P, :]), tiled(ra[0:DH, :]), spread(mrow[:, 1, :], P), ALU.add)
                TT(tiled(rb[0:DH, :]), tiled(rr[:, :]), spread(mrow[:, 0, :], P), ALU.add).then_inc(ml_rows.sem, 1)

                dve.wait_ge(c_sum.sem, c_sum.at(l, 1))
                root(2, (ps[:, 6, 0:TILES], Q_RANK), (ps[:, 6, 16:16 + TILES], KV_RANK))
                diagonals().then_inc(c_diag.sem, 1)
                diagonals(diag2, TILES).then_inc(c_diag.sem, 1)
                V.memset(cst_st[:, 0], 0.0).then_inc(ml_zero.sem, 1)
                dve.wait_ge(ml_dmm.sem, ml_dmm.at(l, 1))
                V.tensor_copy(dcol[:, :, :], ps[:, 7, 0:4 * TILES].rearrange("p (j t) -> p j t", t=TILES)).then_inc(ml_dcol.sem, 1)
                def latent(c, k):
                    return STT(zc(c), zc(c), vecs[:, k:k + 1], flat[:, 2048:2048 + TOK], ALU.mult, ALU.mult)

                V.memset(vaug[:, :, :, DH:DH + 1], 1.0)
                for t in range(TILES):
                    dve.wait_ge(ml_kvt.sem, ml_kvt.at(l, t + 1))
                    V.tensor_copy(vaug[:, t, :, 0:DH], ps[:, 2 + t % 2, 0:2 * P].rearrange("p (h d) -> p h d", h=HEADS_M)) \
                        .then_inc(ml_kv_v.sem, 1)
                    if t == 1:
                        dve.wait_ge(c_row.sem, c_row.at(l, 1))
                        latent(Z_CQ, V_CQG)
                        latent(Z_CQ + 1, V_CQG + 1).then_inc(cq_ok.sem, 1)
                dve.wait_ge(c_row.sem, c_row.at(l, 2))
                latent(Z_CKV, V_CKVG).then_inc(cq_ok.sem, 1)
                dve.wait_ge(kr_t.sem, kr_t.at(l, 1))
                V.tensor_copy(krt[:, 0:TILES, :].rearrange("p t (g c) -> p t g c", g=2),
                              row.rearrange("p (t q c) -> p t q c", q=4, c=32)[:, :, 0:2, 4:20]).then_inc(at_krt.sem, 1)
                dve.wait_ge(ml_dcol.sem, ml_dcol.at(l, 1))
                dve.wait_ge(ml_cols.sem, ml_cols.at(l, 1))

                def masked(i):
                    for d in range(2):
                        if i:
                            dve.wait_ge(ml_s.sem, ml_s.at(l, 2 * (i - 1) + d + 1))
                        dve.wait_ge(ml_bc.sem, ml_bc.at(l, 2 * i + d + 1))
                        TT(em[:, d], ps[:, d, :].rearrange("p (h n) -> p h n", h=HEADS_M),
                           mc[:, M_MASK + d * P:M_MASK + (d + 1) * P].unsqueeze(1).to_broadcast([P, HEADS_M, P]),
                           ALU.add).then_inc(ml_em.sem, 1)

                masked(0)
                for i in range(TILES):
                    tiles = (i, (TILES - i) % TILES)
                    for d in range(2):
                        dve.wait_ge(ml_exp.sem, ml_exp.at(l, 2 * i + d + 1))
                        dve.wait_ge(ml_qk.sem, ml_qk.at(l, i + 1))
                        if i:
                            dve.wait_ge(ml_pv.sem, ml_pv.at(l, 2 * (i - 1) + d + 1))
                        TT(sp_[:, d].rearrange("p (j e) n -> p j e n", e=2),
                           ps[:, 2:4, 2 * P * d:2 * P * (d + 1)].rearrange("p e (j n) -> p j e n", j=2),
                           em[:, d].rearrange("p (j e) n -> p j e n", e=2), ALU.mult).then_inc(ml_s.sem, 1)
                    if i + 1 < TILES:
                        masked(i + 1)
                    for d, t in enumerate(tiles):
                        dve.wait_ge(ml_pv.sem, ml_pv.at(l, 2 * i + d + 1))
                        ds = slice(4 * d, 4 * d + 4)
                        link(TT(ni[:, d].rearrange("p (j e) n -> p j e n", e=2),
                                ps[:, 4:6, 130 * d:130 * (d + 1)].rearrange("p e (j n) -> p j e n", j=2),
                                spread(cols[:, 2, t, ds].rearrange("p (j e) -> p j e", e=2), DH + 1), ALU.mult))
                        out = ps[:, 6 + d, 0:260].rearrange("p (h n) -> p h n", n=DH + 1)
                        TT(hnum[:, t, ds, :], out[:, :, 0:DH], ni[:, d, :, 0:DH], ALU.add)
                        own.inc(TT(den[:, 0, t, ds], out[:, :, DH], ni[:, d, :, DH], ALU.add))
                        st = cst_st[:, min(i, 1), d]
                        for j in range(2):
                            ins = STT(st[:, j, :], st[:, j, :], dcol[:, 2 * d + j, t:t + 1], ps[:, 6 + d, 260 + 65 * j:325 + 65 * j],
                                      ALU.mult, ALU.add)
                        ins.then_inc(ml_out.sem, 1)
                        own.settle()
                        link(STT(den[:, 1, t, ds], den[:, 0, t, ds], -1.0, den[:, 0, t, ds], ALU.mult, ALU.max))
                        link(TT(den[:, 1, t, ds], den[:, 1, t, ds], cols[:, 3, t, ds], ALU.max))
                        link(V.reciprocal(den[:, 2, t, ds], den[:, 1, t, ds]))
                        own.inc(TT(hnum[:, t, ds, :], hnum[:, t, ds, :], spread(den[:, 2, t, ds], DH), ALU.mult))
                dve.wait_ge(ml_out.sem, ml_out.at(l, 2 * TILES))
                dve.wait_ge(st_out.sem, st_out.at(l, 48))
                own.settle()
                hs = hnum[:, :, 0:4, :].rearrange("p t h d -> p t (h d)")
                TT(hs, hs, hnum[:, :, 4:8, :].rearrange("p t h d -> p t (h d)"), ALU.add).then_inc(ml_hsum.sem, 1)
                dve.wait_ge(cv_sum.sem, cv_sum.at(l, 1))
                for c in range(2):
                    ins = STT(blocks(csq[:, c, :]), banks(5), -1.0 / CONV_CH, blocks(csq[:, c, :]), ALU.mult, ALU.add)
                ins.then_inc(cv_xc.sem, 1)
                dve.wait_ge(ml_hsq.sem, ml_hsq.at(l, 1))
                link(V.tensor_reduce(den[:, 0, :, 0:4], hsq[:, :, :].rearrange("p (t h) d -> p t h d", h=4), AX.X, ALU.add))
                TS(den[:, 1, :, 0:4], den[:, 0, :, 0:4], 1.0 / DH, EPS, ALU.mult, ALU.add).then_inc(ml_var.sem, 1)
                dve.wait_ge(ml_root.sem, ml_root.at(l, 1))
                link(V.reciprocal(den[:, 0, :, 0:4], den[:, 2, :, 0:4]))
                TT(hnum[:, :, 0:4, :], hnum[:, :, 0:4, :], spread(den[:, 0, :, 0:4], DH), ALU.mult).then_inc(ml_h.sem, 1)
                dve.wait_ge(cv_sum.sem, cv_sum.at(l, 2))
                root(3, (ps[:, 4, 0:TILES], CONV_CH))
                diagonals().then_inc(cv_diag.sem, 1)
                dve.wait_ge(ml_ht.sem, ml_ht.at(l, 1))
                dve.wait_ge(ml_og.sem, ml_og.at(l, 2))
                for c in range(2):
                    if c:
                        own.inc(ins)
                        own.settle()
                    STT(yt[:, :], flat[:, 2048 * c:2048 * c + TOK], vecs[:, V_MNG + c:V_MNG + c + 1], zc(Z_O + c),
                        ALU.mult, ALU.mult).then_inc(ml_y.sem, 1)
                    dve.wait_ge(ml_yhi.sem, ml_yhi.at(l, c + 1))
                    ins = TT(a_lo[:, c, :], yt[:, :], a_hi[:, c, :].bitcast(F32), ALU.subtract)
                ins.then_inc(ml_done.sem, 1)
                dve.wait_ge(cv_row.sem, cv_row.at(l, 1))
                for c in range(2):
                    ins = TT(csq[:, c, :], csq[:, c, :], flat[:, 2560:2560 + TOK], ALU.mult)
                ins.then_inc(cv_n.sem, 1)

                def pointwise_low(o):
                    dve.wait_ge(cv_hi.sem, cv_hi.at(l, o + 1))
                    TT(blocks(a_lo[:, 2 + o, :]), banks(5), blocks(a_hi[:, 2 + o, :].bitcast(F32)), ALU.subtract).then_inc(cv_done.sem, 1)

                dve.wait_ge(ml_done.sem, ml_done.at(l, 1))
                dve.wait_ge(at_in.sem, at_in.at(l, 48))
                for e in range(2):
                    V.memset(kh[e][QK:QK + 1, :].bitcast(F32), 1.0)
                    V.memset(kl[e][QK:QK + 1, :].bitcast(F32), 0.0)
                    ins = V.memset(va[e][:, :, V_DIM:P], 1.0)
                ins.then_inc(at_k1.sem, 1)

                def sums(h):
                    dve.wait_ge(at_sq.sem, at_sq.at(l, h + 1))
                    link(V.tensor_reduce(small[:, 0:19], sq_[:, :, :], AX.X, ALU.add))
                    TS(small[:, 0:19], small[:, 0:19], 1.0 / QK, EPS, ALU.mult, ALU.add).then_inc(at_sum.sem, 1)

                def inverse(h):
                    dve.wait_ge(at_root.sem, at_root.at(l, h + 1))
                    v_, y_, t_ = small[:, 0:19], small[:, 40:59], small[:, 20:39]
                    link(TT(t_, y_, y_, ALU.mult))
                    link(STT(t_, t_, -0.5, v_, ALU.mult, ALU.mult))
                    STT(y_, t_, 1.5, y_, ALU.add, ALU.mult).then_inc(at_inv.sem, 1)

                def low_q(h, e):
                    dve.wait_ge(at_hq.sem, at_hq.at(l, h + 1))
                    STT(ql[e][0:QK, :], flat[0:QK, 0:TOK], vecs[0:QK, V_QC:V_QC + 1], qh[e][0:QK, :].bitcast(F32),
                        ALU.mult, ALU.subtract).then_inc(at_lq.sem, 1)

                def low_k(h, e):
                    dve.wait_ge(at_hk.sem, at_hk.at(l, h + 1))
                    STT(kl[e][0:QK, :], flat[0:QK, 0:KEYS], vecs[0:QK, V_KC:V_KC + 1], kh[e][0:QK, :].bitcast(F32),
                        ALU.mult, ALU.subtract).then_inc(at_lk.sem, 1)

                def max_rows(h, e, more):
                    for u in range(UNITS):
                        if more and u == U_SUM:
                            sums(h + 1)
                        if more and u == U_INV:
                            inverse(h + 1)
                        t, b = (u + NB - 1) // NB, (u + NB - 1) % NB
                        dve.wait_ge(at_s.sem, at_head(at_s, UNITS, l, h, u + 1))
                        out, src = (pmx[:, 0, 0:1], ps[:, 0, 0:SEQ]) if t == 0 else (pmx[:, t, b:b + 1], ps[:, u % 3, 0:BLK])
                        V.tensor_reduce(out, src, AX.X, ALU.max).then_inc(at_mx.sem, 1)
                    dve.wait_ge(at_mx.sem, at_head(at_mx, UNITS, l, h, UNITS))
                    TS(nmx[:, 0:1], pmx[:, 0, 0:1], -1.0, None, ALU.mult)
                    V.tensor_reduce(nmx[:, 1:TILES], pmx[:, 1:TILES, :], AX.X, ALU.max, negate=True).then_inc(at_nm.sem, 1)

                def low_rows(h, e):
                    dve.wait_ge(at_mhi.sem, at_mhi.at(l, h + 1))
                    TT(ql[e][QK:QK + 1, :], flat[QK:QK + 1, 0:TOK], qh[e][QK:QK + 1, :].bitcast(F32), ALU.subtract).then_inc(at_mlo.sem, 1)

                def output(h, e, o):
                    half, n = slice(DH * e, DH * e + DH), PARTS[o][1]
                    dve.wait_ge(at_pv.sem, at_head(at_pv, STEPS, l, h, (1, 10, 19)[o]))
                    dve.wait_ge(at_y.sem, at_head(at_y, 3, l, h, o))
                    bank = 6 + (e + o) % 2
                    link(V.reciprocal(rec[0:DH, 0:n], ps[DH:P, bank, 0:n]))
                    dve.wait_ge(at_done.sem, at_head(at_done, 3, l, h, o - 1))
                    TT(ya[half, (e + o) % 2, 0:n], ps[0:DH, bank, 0:n], rec[0:DH, 0:n], ALU.mult).then_inc(at_y.sem, 1)

                def split(h, e):
                    low_q(h, e)
                    low_k(h, e)

                def head(h, e, i1, i2):
                    output(h, e, 0)
                    if i1:
                        max_rows(h + 1, 1 - e, i2)
                    output(h, e, 1)
                    if i1:
                        low_rows(h + 1, 1 - e)
                    output(h, e, 2)

                sums(0)
                inverse(0)
                pointwise_low(0)
                split(0, 0)
                pointwise_low(1)
                max_rows(0, 0, True)
                low_rows(0, 0)
                dve.wait_ge(ada3_used.sem, ada3_used.at(l, LAST))
                TT(mod[:, 48 - LAST:48, :], ps[:, 3, 0:2 * LAST].rearrange("p (j s) -> p j s", s=2),
                   spread(vecs[:, V_BADA + 48 - LAST:V_BADA + 48], 2), ALU.add).then_inc(mod_ok.sem, 1)
                split(1, 1)
                with dve.Fori(0, H // 2 - 1) as i:
                    own.enter(i, 32)
                    for e in range(2):
                        head(i * 2 + e, e, True, True)
                        split(i * 2 + (e + 2), e)
                    own.leave(H // 2 - 1)
                head(H - 2, 0, True, False)
                head(H - 1, 1, False, False)

                def f_low(slot, count, dst, hi):
                    dve.wait_ge(f_hi_ok.sem, f_hi_ok.at(l, count))
                    TT(dst, f_raw[:, slot], hi.bitcast(F32), ALU.subtract).then_inc(f_lo_ok.sem, 1)

                def gu_low(n):
                    f_low(n % 2, n + 1, gu_lo[:, n // 2, n % 2].rearrange("p k n -> p (k n)"),
                          gu_hi[:, n // 2, n % 2].rearrange("p k n -> p (k n)"))

                dve.wait_ge(x_back.sem, x_back.at(l, 16))
                def residual(dst, bank0, gate, sem):
                    STT(dst[:, 0:SEQ], ps[:, bank0, 0:SEQ], gate[:, 0:1], dst[:, 0:SEQ], ALU.mult, ALU.add)
                    STT(dst[:, SEQ:BLK], ps[:, bank0, SEQ:BLK], gate[:, 1:2], dst[:, SEQ:BLK], ALU.mult, ALU.add)
                    STT(blocks(dst[:, BLK:TOK]), banks(bank0 + 1, 2), gate[:, 1:2], blocks(dst[:, BLK:TOK]),
                        ALU.mult, ALU.add).then_inc(sem, 1)

                for n in range(16, 24):
                    dve.wait_ge(w_used.sem, w_used.at(l, n + 1))
                    residual(x[:, n - 16, :], 3 * (n % 2), mod[:, n, :], z_free_d.sem)
                dve.wait_ge(z_free_d.sem, z_free_d.at(l, 10))
                for n in range(2):
                    gu_low(n)
                norm(1)

                def product(v, g):
                    f, b = v // NB, slice((v % NB) * BLK, (v % NB + 1) * BLK)
                    dve.wait_ge(f_silu.sem, f_silu.at(l, g * 6 + (v + 1)))
                    link(TT(at[:, v % 2, :], ps[:, 2 * (v % 2) + 1, 0:BLK], sg[:, v % 2, :], ALU.mult))
                    link(V.tensor_copy(g_hi[:, f, b], at[:, v % 2, :]))
                    TT(g_lo[:, f, b], at[:, v % 2, :], g_hi[:, f, b].bitcast(F32), ALU.subtract).then_inc(f_act.sem, 1)

                def fold(g):
                    for o in range(KC):
                        gate = mod[:, 40 + o, :]
                        for b in range(NB):
                            n = o * NB + b
                            dve.wait_ge(f_dn.sem, f_dn.at(l, g * 24 + (n + 1)))
                            bank = 4 + n % 4
                            if b == 0:
                                STT(x[:, o, 0:SEQ], ps[:, bank, 0:SEQ], gate[:, 0:1], x[:, o, 0:SEQ], ALU.mult, ALU.add)
                                ins = STT(x[:, o, SEQ:BLK], ps[:, bank, SEQ:BLK], gate[:, 1:2], x[:, o, SEQ:BLK], ALU.mult, ALU.add)
                            else:
                                bs = slice(b * BLK, (b + 1) * BLK)
                                ins = STT(x[:, o, bs], ps[:, bank, 0:BLK], gate[:, 1:2], x[:, o, bs], ALU.mult, ALU.add)
                            ins.then_inc(f_res.sem, 1)

                for n in range(2, 4):
                    gu_low(n)
                for s in alo_ok:
                    dve.wait_ge(s.sem, s.at(l, KC))
                product(0, 0)

                def group(g):
                    for n in range(2):
                        f_low(n, 4 + g * 6 + n + 1, d_lo[:, n], d_hi[:, n])
                    product(1, g)
                    product(2, g)
                    for n in range(2):
                        f_low(n, 6 + g * 6 + n + 1, gu_lo[:, 0, n].rearrange("p k n -> p (k n)"), gu_hi[:, 0, n].rearrange("p k n -> p (k n)"))
                    for v in range(3, 6):
                        product(v, g)
                    for n in range(2):
                        f_low(n, 8 + g * 6 + n + 1, gu_lo[:, 1, n].rearrange("p k n -> p (k n)"), gu_hi[:, 1, n].rearrange("p k n -> p (k n)"))
                    fold(g)
                    product(0, g + 1)

                group(0)
                with dve.Fori(0, NG - 2) as g:
                    own.enter(g, 16)
                    group(g + 1)
                    own.leave(NG - 2)
                for n in range(2):
                    f_low(n, 4 + (NG - 1) * 6 + n + 1, d_lo[:, n], d_hi[:, n])
                for v in range(1, 6):
                    product(v, NG - 1)
                fold(NG - 1)
                dve.wait_ge(f_res.sem, f_res.at(l + 1, 0))
                own.end_layer()

        @block.gpsimd
        def _(pool):
            pool.sem_inc(at_done.sem, at_done.first)
            G = nc.gpsimd
            with pool.Fori(0, DEPTH) as l:
                own = Chain(pool, pool_own, l)
                link = own.link

                def w_low(n):
                    pool.wait_ge(w_hi_ok.sem, w_hi_ok.at(l, n + 1))
                    G.tensor_tensor(w_lo[:, n % 2, :], w_raw[:, n % 2, :], w_hi[:, n % 2, :].bitcast(F32), ALU.subtract).then_inc(w_lo_ok.sem, 1)

                def low_halves(which):
                    for c in range(1, KC, 2):
                        pool.wait_ge(ahi_ok.sem, ahi_ok.at(l, which * KC + c + 1))
                        G.tensor_tensor(a_lo[:, c, :], nt[:, 1, :], a_hi[:, c, :].bitcast(F32), ALU.subtract).then_inc(alo_ok[1].sem, 1)

                w_low(0)
                w_low(1)
                low_halves(0)
                for n in range(2, 16):
                    w_low(n)
                pool.wait_ge(ml_cols.sem, ml_cols.at(l, 1))
                pool.wait_ge(ml_kv_a.sem, ml_kv_a.at(l, TILES))
                for i in range(TILES):
                    for d, t in enumerate((i, (TILES - i) % TILES)):
                        if i:
                            pool.wait_ge(ml_pv.sem, ml_pv.at(l, 2 * (i - 1) + d + 1))
                        G.tensor_tensor(kw[:, d], kt[:, t, :].rearrange("p (h d) -> p h d", h=HEADS_M),
                                        spread(cols[:, 1, t, 4 * d:4 * d + 4], DH), ALU.mult).then_inc(ml_kw.sem, 1)

                pool.wait_ge(at_in.sem, at_in.at(l, 48))
                for t0, tl, vg in ((0, TILES, V_QN), (TILES, KTILES, V_KN)):
                    g = vecs[:, vg + NOPE:vg + QK]
                    G.tensor_tensor(rope[:, 0, t0:t0 + tl, :], rope_in[:, 0, 0:tl, :], g.unsqueeze(1).to_broadcast([P, tl, ROPE]), ALU.mult)
                    pairs = [ap.rearrange("p t (a b c) -> p t a b c", a=2, b=2) for ap in (rope[:, 1, t0:t0 + tl, :], rope_in[:, 1, 0:tl, :])]
                    gp = g.rearrange("p (a b c) -> p a b c", a=2, b=2)
                    for b in range(2):
                        ins = G.tensor_tensor(pairs[0][:, :, :, b, :], pairs[1][:, :, :, b, :],
                                              gp[:, :, 1 - b, :].unsqueeze(1).to_broadcast([P, tl, 2, 8]), ALU.mult)
                ins.then_inc(at_tab.sem, 1)

                def first(h):
                    pool.wait_ge(at_inv.sem, at_inv.at(l, h + 1))
                    link(G.tensor_tensor(qk[:, :, :], qk[:, :, :], spread(small[:, 40:59], QK), ALU.mult))
                    plain = qk[:, :, NOPE:QK]
                    by_cos, by_sin = sq_[:, :, 0:ROPE], sq_[:, :, ROPE:2 * ROPE]
                    x_, s_, sines = (ap.rearrange("p t (a b c) -> p t a b c", a=2, b=2) for ap in (plain, by_sin, rope[:, 1]))
                    G.tensor_tensor(by_cos, plain, rope[:, 0], ALU.mult)
                    for b in range(2):
                        ins = G.tensor_tensor(s_[:, :, :, b, :], x_[:, :, :, 1 - b, :], sines[:, :, :, b, :], ALU.mult)
                    link(ins)
                    G.tensor_tensor(plain, by_cos, by_sin, ALU.add).then_inc(at_rope.sem, 1)

                def low(h, e, i0, o):
                    q0, n = PARTS[o]
                    half, chunk = slice(DH * e, DH * e + DH), bass.ds(i0 + 4, 1)
                    pool.wait_ge(at_done.sem, at_head(at_done, 3, l, h, o))
                    pool.wait_ge(at_yhi.sem, at_head(at_yhi, 3, l, h, o + 1))
                    G.tensor_tensor(a_lo[half, chunk, q0:q0 + n], ya[half, (e + o) % 2, 0:n].unsqueeze(1),
                                    a_hi[half, chunk, q0:q0 + n].bitcast(F32), ALU.subtract).then_inc(at_done.sem, 1)

                def head(h, e, i0, i2):
                    low(h, e, i0, 0)
                    if i2:
                        pool.wait_ge(at_done.sem, at_head(at_done, 3, l, h, 1))
                        first(h + 2)
                        pool.wait_ge(at_rope.sem, at_rope.at(l, h + 3))
                    low(h, e, i0, 1)
                    if isinstance(h, int) and h == H - 1:
                        pool.wait_ge(at_done.sem, at_done.at(l, 3 * H - 1))
                        w_low(16)
                        w_low(17)
                        pool.wait_ge(w_lo_ok.sem, w_lo_ok.at(l, 18))
                    low(h, e, i0, 2)

                pool.wait_ge(at_tab.sem, at_tab.at(l, 1))
                first(0)
                first(1)
                with pool.Fori(0, H // 2 - 1) as i:
                    own.enter(i, 8)
                    for e in range(2):
                        pool.wait_ge(at_rope.sem, at_rope.at(l, i * 2 + (e + 2)))
                        head(i * 2 + e, e, i, True)
                    own.leave(H // 2 - 1)
                head(H - 2, 0, H // 2 - 1, False)
                head(H - 1, 1, H // 2 - 1, False)
                pool.wait_ge(at_done.sem, at_done.at(l, 3 * H))
                for n in range(18, 24):
                    w_low(n)
                low_halves(1)
                own.end_layer()


def constants():
    cst = np.zeros((P, NCONST), np.float32)
    cst[:, C_ID:C_ID + P] = np.eye(P)
    cst[:, C_ONE:C_ONE + P] = 1.0
    quarter = ROPE // 4
    freqs = np.float32(ROPE_BASE) ** (-np.arange(quarter, dtype=np.float32) / np.float32(quarter))
    t = np.arange(DEC_SEQ)
    ang = np.stack([(t // GRID_W).astype(np.float32)[:, None] * freqs, (t % GRID_W).astype(np.float32)[:, None] * freqs], 1)
    tab = np.zeros((2, KTILES, P, 2, 2, quarter), np.float32)
    tab[0] = 1.0
    tab[0, 1:TILES] = np.cos(ang).reshape(8, P, 2, 1, quarter)
    tab[1, 1:TILES] = np.sin(ang).reshape(8, P, 2, 1, quarter) * np.array([-1, 1], np.float32)[:, None]
    cst[:, C_ROPE:NCONST] = tab.transpose(2, 0, 1, 3, 4, 5).reshape(P, -1)
    cst[:, C_EPS] = EPS
    mc = np.zeros((P, NMC), np.float32)
    s, q = np.arange(P)[:, None], np.arange(P)[None, :]
    mc[:, M_MASK:M_MASK + P] = np.where(s <= q, 0.0, NEG)
    mc[:, M_MASK + P:M_MASK + 2 * P] = np.where(s >= q, 0.0, NEG)
    for d in range(2):
        for h in range(HEADS_M):
            at = M_SEL + (4 * d + h) * P
            mc[32 * d + h, at:at + P] = 1.0
            at = M_PAIR + (2 * d + h // 2) * P + DH * (h % 2)
            mc[32 * d + h, at:at + DH] = 1.0
    reset = np.ones((DH, TILES, P), np.float32)
    reset[0:32, :, 0] = 0.0
    reset[32:64, :, P - 1] = 0.0
    mc[0:DH, M_RESET:NMC] = reset.reshape(DH, TOK)
    return cst, mc


def kernel(**inputs):
    import concourse.bacc as bacc
    from concourse.bass_utils import run_bass_kernel_spmd as run

    g = {k: np.asarray(v) for k, v in inputs.items()}
    f32 = np.float32
    L = DEPTH

    def fm(a):
        return a.T.reshape(-1, P, a.shape[0]).transpose(1, 0, 2)

    arr = {}
    arr["xin"] = fm(np.concatenate([g["x_prompt"][0], g["x_sample"][0]], 0))
    arr["cvec"] = np.stack([g["c_ctx"], g["c"][0]], 1).reshape(KC, P, 2).transpose(1, 0, 2)
    arr["crow_d"] = np.broadcast_to(np.stack([g["c_ctx"], g["c"][0]], 0), (P, 2, D_MODEL))
    vec = np.zeros((L, P, NVEC), f32)

    def put(at, a):
        a = a.reshape(L, -1, P).transpose(0, 2, 1)
        vec[:, :, at:at + a.shape[2]] = a

    put(V_BADA, g["b_ada"]); put(V_N1, g["norm1_g"]); put(V_N2, g["norm2_g"]); put(V_MNG, g["mlstm_norm_g"])
    put(V_DWB, g["conv_dw_b"]); put(V_LNG, g["conv_ln_g"]); put(V_LNB, g["conv_ln_b"])
    put(V_CQG, g["mla_cq_g"]); put(V_CKVG, g["mla_ckv_g"])
    vec[:, :, V_DW:V_DW + 2 * CONV_WIDTH] = g["conv_dw_w"].reshape(L, CONV_WIDTH, 2, P).transpose(0, 3, 2, 1).reshape(L, P, -1)
    gates = {0: 0, 64: 4, 32: 8, 96: 12}
    for part, col in gates.items():
        vec[:, part:part + 4, V_BG] = g["b_gates"][:, col:col + 4]
    for d in range(2):
        vec[:, 32 * d:32 * d + 4, V_M0] = g["state_m"][0, :, d, :]
    vec[:, :, V_QN:V_QN + QK] = g["mla_qn_g"][:, None, :]
    vec[:, :, V_KN:V_KN + QK] = g["mla_kn_g"][:, None, :]
    for at, name in ((V_QC, "mla_qn_g"), (V_KC, "mla_kn_g")):
        vec[:, 0:NOPE, at], vec[:, NOPE:, at] = g[name][:, 0:NOPE], 1.0
    arr["vec"] = vec
    arr["const"], arr["mconst"] = constants()

    def tiles(w):
        n = w.shape[2] // P
        return w.reshape(L, -1, P, n, P).transpose(0, 3, 2, 1, 4)

    wa = tiles(g["w_ada"])
    arr["wada_a"] = np.concatenate([wa[:, 0:ADA_PE], wa[:, 48 - LAST:]], 1).transpose(0, 2, 1, 3, 4)
    arr["wada_b"] = g["w_ada"][:, :, ADA_PE * P:(48 - LAST) * P].reshape(L, D_MODEL, -1, P).transpose(0, 3, 2, 1)
    w = g["w_in"]
    misc = np.zeros((L, D_MODEL, P), f32)
    for part, col in gates.items():
        misc[:, :, part:part + 4] = w[:, :, 1024 + col:1028 + col]
    misc[:, :, 4:20], misc[:, :, 36:52] = w[:, :, 1936:1952], w[:, :, 1952:1968]
    conv = w[:, :, 1040:1552]
    cols = [conv[:, :, 256:384], conv[:, :, 0:128], conv[:, :, 384:512], conv[:, :, 128:256],
            misc, w[:, :, 0:1024], w[:, :, 1552:1936]]
    arr["win"] = tiles(np.concatenate(cols, 2)).reshape(L, 16, P, KC * P)
    arr["wout"] = tiles(g["w_out"]).reshape(L, KC, P, KC * P)
    gu = tiles(g["ffn_w_gu"])
    arr["wgu"] = np.stack([gu[:, 0:FC], gu[:, FC:]], 3).reshape(L, FC, P, 2, KC * P)
    arr["wdn"] = g["ffn_w_down"].reshape(L, FC, P, D_MODEL)
    arr["pww"] = g["conv_pw_w"].reshape(L, 2, P, 2, P).transpose(0, 2, 1, 3, 4)
    wq = g["mla_w_uq"].reshape(L, 2, P, HEADS_A, QK).transpose(0, 3, 2, 1, 4).reshape(L, HEADS_A, P, 2 * QK)
    wkv = g["mla_w_ukv"].reshape(L, P, HEADS_A, P).transpose(0, 2, 1, 3)
    arr["whd"] = np.concatenate([wq, wkv], 3)
    arr["ctx_ckv"] = g["cache_ckv"][0].transpose(0, 2, 1)
    arr["ctx_kr"] = g["cache_krope"][0]
    cn = np.concatenate([g["state_C"][0], g["state_n"][0][..., None]], -1)
    arr["c0"] = cn.reshape(L, 2, 2, 2, DH, DH + 1).transpose(0, 3, 4, 1, 2, 5).reshape(L, P, 2, 2, DH + 1)
    arr = {k: np.ascontiguousarray(v) for k, v in arr.items()}

    outs = {"yout": (P, KC, TOK), "o_ckv": (L, P, SEQ), "o_kr": (L, 2, 16, SEQ), "o_c": (L, P, 2, 2, DH + 1), "o_m": (L, 2, 4, 1)}
    nc = bacc.Bacc("TRN2", target_bir_lowering=False, num_devices=1)
    aps = [nc.dram_tensor(k, v.shape, F32, kind="ExternalInput").ap() for k, v in arr.items()]
    aps += [nc.dram_tensor(k, s, F32, kind="ExternalOutput").ap() for k, s in outs.items()]
    aps.append(nc.dram_tensor("spill", (P, KC, TOK), F32, kind="Internal").ap())
    build(nc, *aps)
    r = run(nc, [arr], core_ids=[0]).results[0]

    y = r["yout"].transpose(2, 1, 0).reshape(TOK, D_MODEL)
    ckv = r["o_ckv"].transpose(0, 2, 1)[None]
    kr = r["o_kr"].reshape(L, ROPE, SEQ).transpose(0, 2, 1)[None]
    cn = r["o_c"].reshape(L, 2, DH, 2, 2, DH + 1).transpose(0, 3, 4, 1, 2, 5).reshape(L, 2, HEADS_M, DH, DH + 1)
    return tuple(np.ascontiguousarray(v) for v in (
        y[None, :SEQ], y[None, SEQ:], ckv, kr, cn[None, ..., :DH], cn[None, ..., DH], r["o_m"].reshape(1, L, 2, HEADS_M)))
```
